# Optimizing a Trainium2 kernel written in Bass

```python
import jax, jax.numpy as jnp
from jax import lax
import numpy as np
import jax
import jax.numpy as jnp

D_MODEL = 1024
BATCH = 1
SEQ = 512
DEPTH = 1

CHUNK = 64
HEAD_DIM = 64
RWKV_HEADS = 8
D_RWKV = RWKV_HEADS * HEAD_DIM
DECAY_LORA = 64
ICLR_LORA = 64
DECAY_SCALE = 0.606531
GN_EPS = 64e-5
ATT_HEADS = 8
D_ATT = ATT_HEADS * HEAD_DIM
IDX_HEADS = 8
IDX_DIM = 64
TOPK_MAX = 256
Q_BLOCK = 128
NORM_EPS = 1e-6

N_RWKV_COLS = 3 * D_RWKV + DECAY_LORA + ICLR_LORA + D_RWKV
N_DSA_COLS = 3 * D_ATT + D_ATT + IDX_HEADS * IDX_DIM + IDX_DIM + IDX_HEADS
N_MERGE_COLS = 2 * D_MODEL
N_IN = N_RWKV_COLS + N_DSA_COLS + N_MERGE_COLS
RWKV_SPLITS = (D_RWKV, 2 * D_RWKV, 3 * D_RWKV, 3 * D_RWKV + DECAY_LORA,
               3 * D_RWKV + DECAY_LORA + ICLR_LORA)
DSA_SPLITS = (D_ATT, 2 * D_ATT, 3 * D_ATT, 4 * D_ATT,
              4 * D_ATT + IDX_HEADS * IDX_DIM,
              4 * D_ATT + IDX_HEADS * IDX_DIM + IDX_DIM)


def rms_norm(x, g, eps=NORM_EPS):
    xf = x.astype(jnp.float32)
    y = xf * lax.rsqrt(jnp.mean(xf * xf, axis=-1, keepdims=True) + eps)
    return (y * g.astype(jnp.float32)).astype(x.dtype)

def rwkv7_time_mix(pa, mu, w0, w_up, a0, a_up, k_k, k_a, r_k, gn_w, gn_b):
    B, S, _ = pa.shape
    prev = jnp.pad(pa, ((0, 0), (1, 0), (0, 0)))[:, :S]
    pa = pa + mu * (prev - pa)
    r, k, v, wd, ad, g = jnp.split(pa, RWKV_SPLITS, axis=-1)
    w = jnp.exp(-DECAY_SCALE * jax.nn.sigmoid((w0 + jnp.tanh(wd) @ w_up).astype(jnp.float32)))
    a = jax.nn.sigmoid((a0 + ad @ a_up).astype(jnp.float32))
    kk = (k * k_k).astype(jnp.float32).reshape(B, S, RWKV_HEADS, HEAD_DIM)
    kk = kk / jnp.maximum(jnp.linalg.norm(kk, axis=-1, keepdims=True), 1e-12)
    k = (k * (1.0 + (a - 1.0) * k_a)).astype(jnp.float32)
    hs = lambda t: t.astype(jnp.float32).reshape(B, S, RWKV_HEADS, HEAD_DIM)
    r_h, w_h, k_h, v_h, a_h = hs(r), hs(w), hs(k), hs(v), hs(a)
    b_h = kk * a_h
    tm = lambda t: jnp.moveaxis(t, 1, 0)

    def step(state, inp):
        r_t, w_t, k_t, v_t, nkk_t, b_t = inp
        sa = jnp.einsum('bhvk,bhk->bhv', state, nkk_t)
        state = (state * w_t[:, :, None, :]
                 + sa[..., None] * b_t[:, :, None, :]
                 + v_t[..., None] * k_t[:, :, None, :])
        y_t = jnp.einsum('bhvk,bhk->bhv', state, r_t)
        return state, y_t

    s0 = jnp.zeros((B, RWKV_HEADS, HEAD_DIM, HEAD_DIM), jnp.float32)
    _, y = lax.scan(step, s0, (tm(r_h), tm(w_h), tm(k_h), tm(v_h), tm(-kk), tm(b_h)))
    y = jnp.moveaxis(y, 0, 1)
    mean = jnp.mean(y, axis=-1, keepdims=True)
    var = jnp.mean(jnp.square(y - mean), axis=-1, keepdims=True)
    y = (y - mean) * lax.rsqrt(var + GN_EPS)
    y = y * gn_w.reshape(RWKV_HEADS, HEAD_DIM) + gn_b.reshape(RWKV_HEADS, HEAD_DIM)
    bonus = jnp.sum(r_h * k_h * r_k.astype(jnp.float32), axis=-1, keepdims=True) * v_h
    y = (y + bonus).reshape(B, S, D_RWKV).astype(pa.dtype)
    return y, g

def dsa_sparse_attention(q, k, v, iq, ik, iw):
    B, S, H, Dh = q.shape
    topk = min(TOPK_MAX, S // 4)
    nb = S // Q_BLOCK
    key_chunk = jnp.arange(S) // CHUNK
    ik32 = ik.astype(jnp.float32)
    iw32 = iw.astype(jnp.float32) * (IDX_HEADS ** -0.5)
    blocks = lambda t: jnp.moveaxis(t.reshape((B, nb, Q_BLOCK) + t.shape[2:]), 1, 0)
    q_pos = jnp.arange(S).reshape(nb, Q_BLOCK)
    scale = HEAD_DIM ** -0.5

    def block_fn(args):
        qb, iqb, iwb, pos = args
        q_chunk = pos // CHUNK
        sc = jnp.einsum('bqhd,bsd->bqhs', iqb.astype(jnp.float32), ik32) * (IDX_DIM ** -0.5)
        idx_score = jnp.einsum('bqhs,bqh->bqs', jax.nn.relu(sc), iwb)
        adm = key_chunk[None, :] <= q_chunk[:, None]
        idx_score = jnp.where(adm[None], idx_score, -jnp.inf)
        _, sel = lax.top_k(idx_score, topk)
        valid = (sel // CHUNK) <= q_chunk[None, :, None]
        k_sel = jax.vmap(lambda kb, ib: kb[ib])(k, sel)
        v_sel = jax.vmap(lambda vb, ib: vb[ib])(v, sel)
        logits = jnp.einsum('bqhd,bqkhd->bqhk', qb.astype(jnp.float32),
                            k_sel.astype(jnp.float32)) * scale
        logits = jnp.where(valid[:, :, None, :], logits, -jnp.inf)
        p = jax.nn.softmax(logits, axis=-1)
        return jnp.einsum('bqhk,bqkhd->bqhd', p, v_sel.astype(jnp.float32)).astype(q.dtype)

    out = lax.map(block_fn, (blocks(q), blocks(iq), blocks(iw32), q_pos))
    return jnp.moveaxis(out, 0, 1).reshape(B, S, H, Dh)

def hybrid_layer(x, c, norm_w, w_ada, b_ada, w_in, mu, w0, w_up, a0, a_up, k_k, k_a,
                 r_k, gn_w, gn_b, q_gain, k_gain, w_a_out, w_b_out, w_o):
    B, S, D = x.shape
    mod = jax.nn.silu(c) @ w_ada + b_ada
    shift, scale, gate = jnp.split(mod, 3, axis=-1)
    h = rms_norm(x, norm_w) * (1.0 + scale[:, None, :]) + shift[:, None, :]
    p = h @ w_in
    pa = p[..., :N_RWKV_COLS]
    pb = p[..., N_RWKV_COLS:N_RWKV_COLS + N_DSA_COLS]
    pg = p[..., N_RWKV_COLS + N_DSA_COLS:]
    ya, ga = rwkv7_time_mix(pa, mu, w0, w_up, a0, a_up, k_k, k_a, r_k, gn_w, gn_b)
    ya = (ya * jax.nn.silu(ga)) @ w_a_out
    q, k, v, gb, iq, ik, iw = jnp.split(pb, DSA_SPLITS, axis=-1)
    heads = lambda t: t.reshape(B, S, ATT_HEADS, HEAD_DIM)
    q = rms_norm(heads(q), q_gain)
    k = rms_norm(heads(k), k_gain)
    v = heads(v)
    iq = iq.reshape(B, S, IDX_HEADS, IDX_DIM)
    yb = dsa_sparse_attention(q, k, v, iq, ik, iw).reshape(B, S, D_ATT)
    yb = (yb * jax.nn.silu(gb)) @ w_b_out
    gm_a, gm_b = jnp.split(pg, 2, axis=-1)
    merged = jax.nn.sigmoid(gm_a) * ya + jax.nn.sigmoid(gm_b) * yb
    out = merged @ w_o
    return x + gate[:, None, :] * out

def first_inputs(seed: int = 0) -> dict:
    key = jax.random.key(seed)
    ks = jax.random.split(key, 24)
    nrm = lambda k, shape, s: jax.random.normal(k, shape, jnp.float32) * s
    L = DEPTH
    return {
        "x": nrm(ks[0], (BATCH, SEQ, D_MODEL), 1.0),
        "c": nrm(ks[1], (BATCH, D_MODEL), 1.0),
        "norm_w": 1.0 + nrm(ks[2], (L, D_MODEL), 0.02),
        "w_ada": nrm(ks[3], (L, D_MODEL, 3 * D_MODEL), 0.5 * D_MODEL ** -0.5),
        "b_ada": nrm(ks[4], (L, 3 * D_MODEL), 0.02),
        "w_in": nrm(ks[5], (L, D_MODEL, N_IN), D_MODEL ** -0.5),
        "mu": jax.random.uniform(ks[6], (L, N_RWKV_COLS), jnp.float32),
        "w0": nrm(ks[7], (L, D_RWKV), 0.5),
        "w_up": nrm(ks[8], (L, DECAY_LORA, D_RWKV), 0.5 * DECAY_LORA ** -0.5),
        "a0": nrm(ks[9], (L, D_RWKV), 0.1),
        "a_up": nrm(ks[10], (L, ICLR_LORA, D_RWKV), 0.5 * ICLR_LORA ** -0.5),
        "k_k": 0.85 + nrm(ks[11], (L, D_RWKV), 0.05),
        "k_a": 1.0 + nrm(ks[12], (L, D_RWKV), 0.05),
        "r_k": nrm(ks[13], (L, RWKV_HEADS, HEAD_DIM), 0.1),
        "gn_w": 1.0 + nrm(ks[14], (L, D_RWKV), 0.02),
        "gn_b": nrm(ks[15], (L, D_RWKV), 0.02),
        "q_gain": 1.0 + nrm(ks[16], (L, HEAD_DIM), 0.02),
        "k_gain": 1.0 + nrm(ks[17], (L, HEAD_DIM), 0.02),
        "w_a_out": nrm(ks[18], (L, D_RWKV, D_MODEL), D_RWKV ** -0.5),
        "w_b_out": nrm(ks[19], (L, D_ATT, D_MODEL), D_ATT ** -0.5),
        "w_o": nrm(ks[20], (L, D_MODEL, D_MODEL), D_MODEL ** -0.5),
    }

def first_block(x, c, norm_w, w_ada, b_ada, w_in, mu, w0, w_up, a0, a_up, k_k, k_a,
              r_k, gn_w, gn_b, q_gain, k_gain, w_a_out, w_b_out, w_o):
    for l in range(DEPTH):
        x = hybrid_layer(x, c, norm_w[l], w_ada[l], b_ada[l], w_in[l], mu[l], w0[l],
                         w_up[l], a0[l], a_up[l], k_k[l], k_k[l] * 0.0 + k_a[l] if False else k_a[l],
                         r_k[l], gn_w[l], gn_b[l], q_gain[l], k_gain[l],
                         w_a_out[l], w_b_out[l], w_o[l])
    return x


_first_inputs = first_inputs


def first_inputs(seed=0):
    import zlib

    import numpy as np

    out = dict(_first_inputs(seed))
    spreads = {}
    factors = {}
    for name, (base, spread) in spreads.items():
        noise = np.random.default_rng([zlib.crc32(name.encode()), seed]).standard_normal(out[name].shape)
        drawn = base * np.exp(spread * noise) if base else spread * noise
        out[name] = __import__('jax').numpy.asarray(drawn.astype(out[name].dtype))
    for name, factor in factors.items():
        out[name] = (out[name] * factor).astype(out[name].dtype)
    return out


_narrow_inputs = first_inputs


def first_inputs(seed=0):

    out = dict(_narrow_inputs(seed))
    wider = {'norm_w': 12.0,
     'b_ada': 6.29,
     'w0': 3.27,
     'w_up': 8.25,
     'a0': 12.0,
     'k_k': 12.0,
     'k_a': 10.31,
     'gn_w': 12.0,
     'gn_b': 12.0,
     'q_gain': 12.0,
     'k_gain': 12.0}
    for name, times in wider.items():
        mean = out[name].mean()
        out[name] = (mean + times * (out[name] - mean)).astype(out[name].dtype)
    return out


GRID_W = 64
CTX_LEN = 256
D_MIX = D_MODEL
CONV_CH = D_MIX // 2
CONV_WIDTH = 31
N_HEADS = 8
HEAD_DIM_2 = (D_MIX - CONV_CH) // N_HEADS
ATTN_W = N_HEADS * HEAD_DIM_2
NA_ROWS = 8
NA_COLS = 16
QB_W = 16
KB_W = 32
N_EXPERTS = 16
D_EXPERT = 2048
EC_FACTOR = 2
N_MOD = 6
EPS = 1e-6
NEG_INF = -1e30
W_IN_COLS = 2 * CONV_CH + 3 * ATTN_W


def rms_norm_2(x, g):
    xf = x.astype(jnp.float32)
    y = xf * lax.rsqrt(jnp.mean(xf * xf, axis=-1, keepdims=True) + EPS)
    return (y * g.astype(jnp.float32)).astype(x.dtype)

def layer_norm(x, g, b):
    xf = x.astype(jnp.float32)
    mu = jnp.mean(xf, axis=-1, keepdims=True)
    var = jnp.mean(jnp.square(xf - mu), axis=-1, keepdims=True)
    y = (xf - mu) * lax.rsqrt(var + EPS)
    return (y * g.astype(jnp.float32) + b.astype(jnp.float32)).astype(x.dtype)

def adaln(cvec, w_mod, b_mod):
    m = (jax.nn.silu(cvec) @ w_mod + b_mod).reshape(-1, 1, N_MOD * D_MODEL)
    return jnp.split(m, N_MOD, axis=-1)

def modulate(h, shift, scale):
    return h * (1.0 + scale) + shift

def conv_mixer(u, conv_w, conv_b, ln_g, ln_b):
    a, g = jnp.split(u, 2, axis=-1)
    v = a * jax.nn.sigmoid(g)
    y = lax.conv_general_dilated(
        v, conv_w[:, None, :].astype(v.dtype), window_strides=(1,),
        padding=[(CONV_WIDTH // 2, CONV_WIDTH // 2)],
        dimension_numbers=('NWC', 'WIO', 'NWC'), feature_group_count=CONV_CH) + conv_b
    return jax.nn.silu(layer_norm(y, ln_g, ln_b))

def na_indices(rows):
    kh = min(NA_ROWS, rows)
    n_blk = GRID_W // QB_W
    r = jnp.arange(rows)
    r0 = jnp.clip(r - kh // 2, 0, rows - kh)
    key_rows = r0[:, None] + jnp.arange(kh)[None, :]
    q_cols = jnp.arange(GRID_W).reshape(n_blk, QB_W)
    band0 = jnp.clip(jnp.arange(n_blk) * QB_W - (KB_W - QB_W) // 2, 0, GRID_W - KB_W)
    key_cols = band0[:, None] + jnp.arange(KB_W)[None, :]
    c0 = jnp.clip(q_cols - NA_COLS // 2, 0, GRID_W - NA_COLS)
    kc_b = key_cols[:, None, :]
    col_valid = (kc_b >= c0[:, :, None]) & (kc_b < c0[:, :, None] + NA_COLS)
    d_row = key_rows - r[:, None] + (NA_ROWS - 1)
    d_col = jnp.clip(kc_b - q_cols[:, :, None] + (NA_COLS - 1), 0, 2 * NA_COLS - 2)
    return key_rows, key_cols, col_valid, d_row, d_col

def na_attention(q, k, v, k_ctx, v_ctx, rpb, idx):
    key_rows, key_cols, col_valid, d_row, d_col = idx
    B, T, _ = q.shape
    rows, kh = key_rows.shape
    n_blk = GRID_W // QB_W
    L = k_ctx.shape[1]
    f32 = jnp.float32
    qb = q.reshape(B, rows, n_blk, QB_W, N_HEADS, HEAD_DIM_2).astype(f32) * (HEAD_DIM_2 ** -0.5)
    kg = k.reshape(B, rows, GRID_W, N_HEADS, HEAD_DIM_2)
    vg = v.reshape(B, rows, GRID_W, N_HEADS, HEAD_DIM_2)
    ri = key_rows[:, None, :, None]
    ci = key_cols[None, :, None, :]
    k_band = kg[:, ri, ci]
    v_band = vg[:, ri, ci]
    kcx = k_ctx.reshape(B, L, N_HEADS, HEAD_DIM_2)
    vcx = v_ctx.reshape(B, L, N_HEADS, HEAD_DIM_2)
    bias = rpb[:, d_row[:, None, None, :, None], d_col[None, :, :, None, :]]
    s_loc = jnp.einsum('brnqhd,brnjwhd->bhrnqjw', qb, k_band.astype(f32)) + bias.astype(f32)[None]
    s_loc = jnp.where(col_valid[:, :, None, :], s_loc, NEG_INF)
    s_ctx = jnp.einsum('brnqhd,blhd->bhrnql', qb, kcx.astype(f32))
    n_loc = kh * KB_W
    s = jnp.concatenate([s_loc.reshape(s_loc.shape[:5] + (n_loc,)), s_ctx], axis=-1)
    p = jax.nn.softmax(s, axis=-1).astype(v.dtype)
    p_loc = p[..., :n_loc].reshape(s_loc.shape)
    p_ctx = p[..., n_loc:]
    o = (jnp.einsum('bhrnqjw,brnjwhd->brnqhd', p_loc, v_band)
         + jnp.einsum('bhrnql,blhd->brnqhd', p_ctx, vcx))
    return o.reshape(B, T, ATTN_W)

def ctx_attention(q, k, v):
    B, L, _ = q.shape
    f32 = jnp.float32
    qh = q.reshape(B, L, N_HEADS, HEAD_DIM_2).astype(f32) * (HEAD_DIM_2 ** -0.5)
    kh = k.reshape(B, L, N_HEADS, HEAD_DIM_2).astype(f32)
    vh = v.reshape(B, L, N_HEADS, HEAD_DIM_2)
    p = jax.nn.softmax(jnp.einsum('blhd,bmhd->bhlm', qh, kh), axis=-1).astype(v.dtype)
    return jnp.einsum('bhlm,bmhd->blhd', p, vh).reshape(B, L, ATTN_W)

def ec_moe(h, w_router, w_gate, w_up, w_down):
    B, T, _ = h.shape
    cap = EC_FACTOR * T // N_EXPERTS
    aff = jax.nn.softmax((h @ w_router).astype(jnp.float32), axis=-1)
    wts, tok = lax.top_k(jnp.swapaxes(aff, 1, 2), cap)
    bidx = jnp.arange(B)[:, None, None]
    xs = h[bidx, tok]
    hid = jax.nn.silu(jnp.einsum('becd,edf->becf', xs, w_gate)) * jnp.einsum('becd,edf->becf', xs, w_up)
    y = jnp.einsum('becf,efd->becd', hid, w_down) * wts[..., None].astype(h.dtype)
    return jnp.zeros_like(h).at[bidx, tok].add(y)

def second_inputs(seed: int = 0) -> dict:
    key = jax.random.key(seed)
    ks = jax.random.split(key, 21)
    f32 = jnp.float32

    def nrm(k, shape, scale):
        return jax.random.normal(k, shape, f32) * scale

    return {
        'x': nrm(ks[0], (BATCH, SEQ, D_MODEL), 1.0),
        'c': nrm(ks[1], (BATCH, D_MODEL), 1.0),
        'ctx': nrm(ks[2], (BATCH, CTX_LEN, D_MODEL), 1.0),
        'c_ctx': nrm(ks[3], (D_MODEL,), 1.0),
        'w_mod': nrm(ks[4], (DEPTH, D_MODEL, N_MOD * D_MODEL), 0.5 * D_MODEL ** -0.5),
        'b_mod': nrm(ks[5], (DEPTH, N_MOD * D_MODEL), 0.02),
        'norm_mix_g': 1.0 + nrm(ks[6], (DEPTH, D_MODEL), 0.02),
        'w_in': nrm(ks[7], (DEPTH, D_MODEL, W_IN_COLS), D_MODEL ** -0.5),
        'conv_w': nrm(ks[8], (DEPTH, CONV_WIDTH, CONV_CH), CONV_WIDTH ** -0.5),
        'conv_b': nrm(ks[9], (DEPTH, CONV_CH), 0.02),
        'conv_ln_g': 1.0 + nrm(ks[10], (DEPTH, CONV_CH), 0.02),
        'conv_ln_b': nrm(ks[11], (DEPTH, CONV_CH), 0.02),
        'rpb': nrm(ks[12], (DEPTH, N_HEADS, 2 * NA_ROWS - 1, 2 * NA_COLS - 1), 0.1),
        'w_out': nrm(ks[13], (DEPTH, D_MIX, D_MODEL), D_MIX ** -0.5),
        'norm_ffn_g': 1.0 + nrm(ks[14], (DEPTH, D_MODEL), 0.02),
        'w_router': nrm(ks[15], (DEPTH, D_MODEL, N_EXPERTS), D_MODEL ** -0.5),
        'w_gate': nrm(ks[16], (DEPTH, N_EXPERTS, D_MODEL, D_EXPERT), D_MODEL ** -0.5),
        'w_up': nrm(ks[17], (DEPTH, N_EXPERTS, D_MODEL, D_EXPERT), D_MODEL ** -0.5),
        'w_down': nrm(ks[18], (DEPTH, N_EXPERTS, D_EXPERT, D_MODEL), D_EXPERT ** -0.5),
        'norm_final_g': 1.0 + nrm(ks[19], (D_MODEL,), 0.02),
    }

def second_block(x, c, ctx, c_ctx, w_mod, b_mod, norm_mix_g, w_in, conv_w, conv_b, conv_ln_g, conv_ln_b,
              rpb, w_out, norm_ffn_g, w_router, w_gate, w_up, w_down, norm_final_g):
    B, T, _ = x.shape
    rows = T // GRID_W
    idx = na_indices(rows)
    splits = [2 * CONV_CH, 2 * CONV_CH + ATTN_W, 2 * CONV_CH + 2 * ATTN_W]
    for l in range(DEPTH):
        last = l == DEPTH - 1
        sh1, sc1, g1, sh2, sc2, g2 = adaln(c, w_mod[l], b_mod[l])
        csh1, csc1, cg1, csh2, csc2, cg2 = adaln(c_ctx, w_mod[l], b_mod[l])

        h = modulate(rms_norm_2(x, norm_mix_g[l]), sh1, sc1)
        hc = modulate(rms_norm_2(ctx, norm_mix_g[l]), csh1, csc1)
        u, q, k, v = jnp.split(h @ w_in[l], splits, axis=-1)
        if last:
            k_c, v_c = jnp.split(hc @ w_in[l][:, splits[1]:], 2, axis=-1)
        else:
            u_c, q_c, k_c, v_c = jnp.split(hc @ w_in[l], splits, axis=-1)
        y_conv = conv_mixer(u, conv_w[l], conv_b[l], conv_ln_g[l], conv_ln_b[l])
        y_attn = na_attention(q, k, v, k_c, v_c, rpb[l], idx)
        x = x + g1 * (jnp.concatenate([y_conv, y_attn], axis=-1) @ w_out[l])
        if not last:
            yc_conv = conv_mixer(u_c, conv_w[l], conv_b[l], conv_ln_g[l], conv_ln_b[l])
            yc_attn = ctx_attention(q_c, k_c, v_c)
            ctx = ctx + cg1 * (jnp.concatenate([yc_conv, yc_attn], axis=-1) @ w_out[l])

        h2 = modulate(rms_norm_2(x, norm_ffn_g[l]), sh2, sc2)
        x = x + g2 * ec_moe(h2, w_router[l], w_gate[l], w_up[l], w_down[l])
        if not last:
            hc2 = modulate(rms_norm_2(ctx, norm_ffn_g[l]), csh2, csc2)
            ctx = ctx + cg2 * ec_moe(hc2, w_router[l], w_gate[l], w_up[l], w_down[l])
    return rms_norm_2(x, norm_final_g)


DEPTH_3 = 2

EXPAND = 2
MIX_WIDTH = EXPAND * D_MODEL
GMLP_WIDTH = MIX_WIDTH // 2
GMLP_GROUPS = 4
GMLP_GROUP_DIM = GMLP_WIDTH // GMLP_GROUPS
GMLP_CHUNK = 128
ATTN_WIDTH = MIX_WIDTH // 2
HEAD_DIM_3 = 128
N_Q_HEADS = ATTN_WIDTH // HEAD_DIM_3
N_KV_HEADS = 2
GQA_GROUP = N_Q_HEADS // N_KV_HEADS
KV_WIDTH = N_KV_HEADS * HEAD_DIM_3
WINDOW = 128
ATTN_BLOCK = 128
HGRN_WIDTH = MIX_WIDTH
HGRN_HEAD_DIM = 128
HGRN_HEADS = HGRN_WIDTH // HGRN_HEAD_DIM
HGRN_CHUNK = 64

N_EVEN = (DEPTH_3 + 1) // 2
N_ODD = DEPTH_3 // 2
EVEN_SPLITS = [GMLP_WIDTH, GMLP_WIDTH, GMLP_WIDTH, ATTN_WIDTH, KV_WIDTH, KV_WIDTH, ATTN_WIDTH]
ODD_SPLITS = [HGRN_WIDTH] * 5
IN_EVEN = sum(EVEN_SPLITS)
IN_ODD = sum(ODD_SPLITS)


F32 = jnp.float32

def rms_norm_3(x, g):
    xf = x.astype(F32)
    y = xf * lax.rsqrt(jnp.mean(xf * xf, axis=-1, keepdims=True) + EPS)
    return (y * g.astype(F32)).astype(x.dtype)

def split_cols(t, sizes):
    idx = [int(i) for i in np.cumsum(sizes)[:-1]]
    return jnp.split(t, idx, axis=-1)

def alibi_slopes(n):
    return jnp.exp2(-8.0 * jnp.arange(1, n + 1, dtype=F32) / n)

def chunked_sgu(u, v, ln_g, ln_b, w_s, b_s):
    B, S, _ = v.shape
    vf = v.astype(F32)
    mu = jnp.mean(vf, axis=-1, keepdims=True)
    var = jnp.mean(jnp.square(vf - mu), axis=-1, keepdims=True)
    vn = ((vf - mu) * lax.rsqrt(var + EPS) * ln_g.astype(F32) + ln_b.astype(F32)).astype(v.dtype)
    vc = vn.reshape(B, S // GMLP_CHUNK, GMLP_CHUNK, GMLP_GROUPS, GMLP_GROUP_DIM)
    mixed = jnp.einsum('gts,bnsgc->bntgc', w_s, vc) + b_s.T[None, None, :, :, None]
    return u * mixed.reshape(B, S, GMLP_WIDTH)

def window_attention(q, k, v, sink):
    B, S = q.shape[0], q.shape[1]
    nb = S // ATTN_BLOCK
    qb = q.reshape(B, nb, ATTN_BLOCK, N_KV_HEADS, GQA_GROUP, HEAD_DIM_3)

    def band(t):
        tp = jnp.pad(t, ((0, 0), (ATTN_BLOCK, ATTN_BLOCK), (0, 0), (0, 0)))
        tb = tp.reshape(B, nb + 2, ATTN_BLOCK, N_KV_HEADS, HEAD_DIM_3)
        return jnp.concatenate([tb[:, :-2], tb[:, 1:-1], tb[:, 2:]], axis=2)

    kb, vb = band(k), band(v)
    scores = jnp.einsum('bnqhgd,bnshd->bnhgqs', qb, kb).astype(F32) * (HEAD_DIM_3 ** -0.5)
    qi = jnp.arange(ATTN_BLOCK)
    kj = jnp.arange(3 * ATTN_BLOCK) - ATTN_BLOCK
    dist = jnp.abs(kj[None, :] - qi[:, None])
    kpos = (jnp.arange(nb) * ATTN_BLOCK)[:, None] + kj[None, :]
    valid = (dist[None] <= WINDOW) & (kpos[:, None, :] >= 0) & (kpos[:, None, :] < S)
    slopes = alibi_slopes(N_Q_HEADS).reshape(N_KV_HEADS, GQA_GROUP)
    scores = scores - slopes[:, :, None, None] * dist.astype(F32)
    scores = jnp.where(valid[None, :, None, None], scores, -jnp.inf)
    sink_l = sink.astype(F32).reshape(N_KV_HEADS, GQA_GROUP)[None, None, :, :, None, None]
    m = jnp.maximum(jnp.max(scores, axis=-1, keepdims=True), sink_l)
    p = jnp.exp(scores - m)
    p = p / (jnp.sum(p, axis=-1, keepdims=True) + jnp.exp(sink_l - m))
    out = jnp.einsum('bnhgqs,bnshd->bnqhgd', p.astype(v.dtype), vb)
    return out.reshape(B, S, N_Q_HEADS * HEAD_DIM_3)

def hgrn2_direction(q, f_logit, i, lb):
    B, S, H, D = q.shape
    nc = S // HGRN_CHUNK
    C = HGRN_CHUNK
    f = lb + (1.0 - lb) * jax.nn.sigmoid(f_logit.astype(F32))
    k = 1.0 - f
    g = jnp.log(f)

    def chunk(t):
        return t.reshape(B, nc, C, H, D)

    qc, kc, vc, gc = chunk(q.astype(F32)), chunk(k), chunk(i.astype(F32)), chunk(g)
    bcum = jnp.cumsum(gc, axis=2)
    blast = bcum[:, :, -1:]
    q_t = qc * jnp.exp(bcum)
    k_t = kc * jnp.exp(-bcum)
    k_end = kc * jnp.exp(blast - bcum)
    a = jnp.einsum('bnthd,bnshd->bnhts', q_t, k_t)
    a = jnp.where(jnp.tril(jnp.ones((C, C), dtype=bool)), a, 0.0)
    o_intra = jnp.einsum('bnhts,bnshv->bnthv', a, vc)

    def step(state, xs):
        qn, kn, vn, dn = xs
        o = jnp.einsum('bthd,bhdv->bthv', qn, state)
        state = state * dn[..., None] + jnp.einsum('bshd,bshv->bhdv', kn, vn)
        return state, o

    xs = (jnp.moveaxis(q_t, 1, 0), jnp.moveaxis(k_end, 1, 0), jnp.moveaxis(vc, 1, 0),
          jnp.moveaxis(jnp.exp(blast[:, :, 0]), 1, 0))
    s0 = jnp.zeros((B, H, D, D), dtype=F32)
    _, o_inter = lax.scan(step, s0, xs)
    o = o_intra + jnp.moveaxis(o_inter, 0, 1)
    return o.reshape(B, S, H, D)

def hgrn_lower_bound(gamma, layer):
    c = jnp.cumsum(jax.nn.softmax(gamma.astype(F32), axis=0), axis=0)
    return (c[layer] - c[0]).reshape(HGRN_HEADS, HGRN_HEAD_DIM)

def even_layer(x, norm_g, w_in, ln_g, ln_b, w_s, b_s, sink, w_out):
    B, S, _ = x.shape
    h = rms_norm_3(x, norm_g)
    proj = h @ w_in
    u_a, v_a, z_a, q_b, k_b, v_b, z_b = split_cols(proj, EVEN_SPLITS)
    a_out = chunked_sgu(u_a, v_a, ln_g, ln_b, w_s, b_s) * jax.nn.silu(z_a)
    b_out = window_attention(q_b.reshape(B, S, N_Q_HEADS, HEAD_DIM_3),
                             k_b.reshape(B, S, N_KV_HEADS, HEAD_DIM_3),
                             v_b.reshape(B, S, N_KV_HEADS, HEAD_DIM_3), sink) * jax.nn.silu(z_b)
    return jnp.concatenate([a_out, b_out], axis=-1) @ w_out

def odd_layer(x, norm_g, w_in, gamma_f, gamma_b, head_norm_g, w_out, layer):
    B, S, _ = x.shape
    h = rms_norm_3(x, norm_g)
    proj = h @ w_in
    q, f_f, f_b, i, z = split_cols(proj, ODD_SPLITS)
    shp = (B, S, HGRN_HEADS, HGRN_HEAD_DIM)
    q = jax.nn.silu(q).reshape(shp)
    i = i.reshape(shp)
    o_f = hgrn2_direction(q, f_f.reshape(shp), i, hgrn_lower_bound(gamma_f, layer))
    o_b = jnp.flip(hgrn2_direction(jnp.flip(q, 1), jnp.flip(f_b.reshape(shp), 1), jnp.flip(i, 1),
                                   hgrn_lower_bound(gamma_b, layer)), 1)
    o = o_f + o_b
    o = o * lax.rsqrt(jnp.mean(o * o, axis=-1, keepdims=True) + EPS)
    o = (o.reshape(B, S, HGRN_WIDTH) * head_norm_g.astype(F32)).astype(x.dtype)
    return (o * jax.nn.silu(z)) @ w_out

def third_inputs(seed: int = 0) -> dict:
    key = jax.random.key(seed)
    ks = jax.random.split(key, 16)
    nrm = jax.random.normal
    return {
        "x": nrm(ks[0], (BATCH, SEQ, D_MODEL), F32),
        "norm_g_even": 1.0 + 0.02 * nrm(ks[1], (N_EVEN, D_MODEL), F32),
        "w_in_even": nrm(ks[2], (N_EVEN, D_MODEL, IN_EVEN), F32) * D_MODEL ** -0.5,
        "gmlp_ln_g": 1.0 + 0.02 * nrm(ks[3], (N_EVEN, GMLP_WIDTH), F32),
        "gmlp_ln_b": 0.02 * nrm(ks[4], (N_EVEN, GMLP_WIDTH), F32),
        "gmlp_w_s": nrm(ks[5], (N_EVEN, GMLP_GROUPS, GMLP_CHUNK, GMLP_CHUNK), F32) * GMLP_CHUNK ** -0.5,
        "gmlp_b_s": 1.0 + 0.02 * nrm(ks[6], (N_EVEN, GMLP_GROUPS, GMLP_CHUNK), F32),
        "attn_sink": 0.5 * nrm(ks[7], (N_EVEN, N_Q_HEADS), F32),
        "w_out_even": nrm(ks[8], (N_EVEN, GMLP_WIDTH + ATTN_WIDTH, D_MODEL), F32) * (GMLP_WIDTH + ATTN_WIDTH) ** -0.5,
        "norm_g_odd": 1.0 + 0.02 * nrm(ks[9], (N_ODD, D_MODEL), F32),
        "w_in_odd": nrm(ks[10], (N_ODD, D_MODEL, IN_ODD), F32) * D_MODEL ** -0.5,
        "hgrn_gamma_fwd": 1.0 + 0.1 * nrm(ks[11], (DEPTH_3, HGRN_WIDTH), F32),
        "hgrn_gamma_bwd": 1.0 + 0.1 * nrm(ks[12], (DEPTH_3, HGRN_WIDTH), F32),
        "hgrn_head_norm_g": 1.0 + 0.02 * nrm(ks[13], (N_ODD, HGRN_WIDTH), F32),
        "w_out_odd": nrm(ks[14], (N_ODD, HGRN_WIDTH, D_MODEL), F32) * HGRN_WIDTH ** -0.5,
        "final_norm_g": 1.0 + 0.02 * nrm(ks[15], (D_MODEL,), F32),
    }

def third_block(x, norm_g_even, w_in_even, gmlp_ln_g, gmlp_ln_b, gmlp_w_s, gmlp_b_s, attn_sink,
              w_out_even, norm_g_odd, w_in_odd, hgrn_gamma_fwd, hgrn_gamma_bwd, hgrn_head_norm_g,
              w_out_odd, final_norm_g):
    for layer in range(DEPTH_3):
        j = layer // 2
        if layer % 2 == 0:
            x = x + even_layer(x, norm_g_even[j], w_in_even[j], gmlp_ln_g[j], gmlp_ln_b[j],
                               gmlp_w_s[j], gmlp_b_s[j], attn_sink[j], w_out_even[j])
        else:
            x = x + odd_layer(x, norm_g_odd[j], w_in_odd[j], hgrn_gamma_fwd, hgrn_gamma_bwd,
                              hgrn_head_norm_g[j], w_out_odd[j], layer)
    return rms_norm_3(x, final_norm_g)


_first_inputs_3 = third_inputs


def third_inputs(seed=0):
    import zlib

    import numpy as np

    out = dict(_first_inputs_3(seed))
    spreads = {}
    factors = {}
    for name, (base, spread) in spreads.items():
        noise = np.random.default_rng([zlib.crc32(name.encode()), seed]).standard_normal(out[name].shape)
        drawn = base * np.exp(spread * noise) if base else spread * noise
        out[name] = __import__('jax').numpy.asarray(drawn.astype(out[name].dtype))
    for name, factor in factors.items():
        out[name] = (out[name] * factor).astype(out[name].dtype)
    return out


_narrow_inputs_3 = third_inputs


def third_inputs(seed=0):

    out = dict(_narrow_inputs_3(seed))
    wider = {'norm_g_even': 3.22,
     'gmlp_ln_g': 8.44,
     'gmlp_ln_b': 8.4,
     'gmlp_b_s': 7.91,
     'attn_sink': 12.0,
     'norm_g_odd': 4.85,
     'hgrn_gamma_fwd': 12.0,
     'hgrn_gamma_bwd': 12.0,
     'hgrn_head_norm_g': 6.89,
     'final_norm_g': 3.21}
    for name, times in wider.items():
        mean = out[name].mean()
        out[name] = (mean + times * (out[name] - mean)).astype(out[name].dtype)
    return out


def setup_inputs(seed=0):
    out = dict(first_inputs(seed))
    for name, value in second_inputs(seed + 1).items():
        if name != "x":
            out[name + "_2"] = value
    for name, value in third_inputs(seed + 2).items():
        if name != "x":
            out[name + "_3"] = value
    return out


def reference(
    x, c, norm_w, w_ada, b_ada, w_in, mu, w0, w_up, a0, a_up, k_k, k_a, r_k, gn_w, gn_b, q_gain,
    k_gain, w_a_out, w_b_out, w_o, c_2, ctx_2, c_ctx_2, w_mod_2, b_mod_2, norm_mix_g_2, w_in_2,
    conv_w_2, conv_b_2, conv_ln_g_2, conv_ln_b_2, rpb_2, w_out_2, norm_ffn_g_2, w_router_2,
    w_gate_2, w_up_2, w_down_2, norm_final_g_2, norm_g_even_3, w_in_even_3, gmlp_ln_g_3,
    gmlp_ln_b_3, gmlp_w_s_3, gmlp_b_s_3, attn_sink_3, w_out_even_3, norm_g_odd_3, w_in_odd_3,
    hgrn_gamma_fwd_3, hgrn_gamma_bwd_3, hgrn_head_norm_g_3, w_out_odd_3, final_norm_g_3,
):
    x = first_block(
        x, c, norm_w, w_ada, b_ada, w_in, mu, w0, w_up, a0, a_up, k_k, k_a, r_k, gn_w, gn_b,
        q_gain, k_gain, w_a_out, w_b_out, w_o,
    )
    x = second_block(
        x, c_2, ctx_2, c_ctx_2, w_mod_2, b_mod_2, norm_mix_g_2, w_in_2, conv_w_2, conv_b_2,
        conv_ln_g_2, conv_ln_b_2, rpb_2, w_out_2, norm_ffn_g_2, w_router_2, w_gate_2, w_up_2,
        w_down_2, norm_final_g_2,
    )
    return third_block(
        x, norm_g_even_3, w_in_even_3, gmlp_ln_g_3, gmlp_ln_b_3, gmlp_w_s_3, gmlp_b_s_3,
        attn_sink_3, w_out_even_3, norm_g_odd_3, w_in_odd_3, hgrn_gamma_fwd_3, hgrn_gamma_bwd_3,
        hgrn_head_norm_g_3, w_out_odd_3, final_norm_g_3,
    )


_drawn_inputs = setup_inputs


def setup_inputs(seed=0):
    import zlib

    import numpy as np

    out = dict(_drawn_inputs(seed))
    spreads = {}
    factors = {'q_gain': 5.89,
     'k_gain': 7.6,
     'b_mod_2': 2.92,
     'norm_mix_g_2': 8.0,
     'conv_b_2': 7.84,
     'conv_ln_g_2': 8.0,
     'conv_ln_b_2': 8.0,
     'rpb_2': 8.0,
     'norm_ffn_g_2': 6.184}
    for name, (base, spread) in spreads.items():
        noise = np.random.default_rng([zlib.crc32(name.encode()), seed]).standard_normal(out[name].shape)
        drawn = base * np.exp(spread * noise) if base else spread * noise
        out[name] = jnp.asarray(drawn.astype(out[name].dtype))
    for name, factor in factors.items():
        out[name] = (out[name] * factor).astype(out[name].dtype)
    return out
```

```python
from contextlib import ExitStack

import numpy as np
import concourse.bass as bass
from concourse import mybir

F32 = mybir.dt.float32
ALU = mybir.AluOpType
ACT = mybir.ActivationFunctionType
AXX = mybir.AxisListType.X
MUL, ADD, SUB, MAX, MIN = ALU.mult, ALU.add, ALU.subtract, ALU.max, ALU.min

P = 128
T = 512
D = 1024
KD = D // P
TB = T // P
L = 256
HD = 64
BIG = 1e30
BANKS = 8
RING = 4
SLOT = 4096
DECAY = 0.606531
E_ = 16
CAP = 64
FE = 2048


class Counter:

    def __init__(self, sem):
        self.sem, self.total, self.base = sem, 0, 0

    def rebase(self):
        self.base = self.total
        return self

    def at(self, n):
        return self.base + n


class Line:

    def __init__(self, eng, own):
        self.eng, self.own = eng, own

    def __call__(self, ins, sig=None, step=1):
        sig = sig or self.own
        ins.then_inc(sig.sem, step)
        sig.total += step
        self.eng.wait_ge(sig.sem, sig.total)

    def after(self, sig, n):
        self.eng.wait_ge(sig.sem, sig.at(n))


VECTORS = [
    ("c", 8), ("norm_w", 8), ("b_ada", 24), ("mu", 17), ("w0", 4), ("a0", 4), ("k_k", 4), ("k_a", 4),
    ("r_k", 4), ("gn_w", 4), ("gn_b", 4), ("q_gain", 1), ("k_gain", 1),
    ("c_2", 8), ("c_ctx_2", 8), ("b_mod_2", 48), ("norm_mix_g_2", 8), ("conv_w_2", 31 * 4),
    ("conv_b_2", 4), ("conv_ln_g_2", 4), ("conv_ln_b_2", 4), ("norm_ffn_g_2", 8), ("norm_final_g_2", 8),
    ("norm_g_even_3", 8), ("norm_g_odd_3", 8), ("hgrn_gamma_fwd_3", 32), ("hgrn_gamma_bwd_3", 32),
    ("hgrn_head_norm_g_3", 16), ("final_norm_g_3", 8), ("attn_sink_3", 8),
]
AT = {}
_n = 0
for _name, _w in VECTORS:
    AT[_name] = (_n, _w)
    _n += _w
NVEC = _n

MASKS = ["ident", "ones", "blk64", "mU16", "mL16", "mUoff", "mU", "mUI", "mLI", "bd", "adm", "iota", "win"]


def mask_arrays():
    i = np.arange(P)
    row, col = i[:, None], i[None, :]
    c64, c16 = row // 64 == col // 64, row // 16 == col // 16
    m = {
        "ident": row == col, "ones": np.ones((P, P), bool), "blk64": c64,
        "mU16": (row < col) & c16, "mL16": (row > col) & c16, "mUoff": (row < col) & c64 & ~c16,
        "mU": (row < col) & c64, "mUI": (row <= col) & c64, "mLI": (row >= col) & c64, "bd": c64,
        "iota": (col % 64 + 1) * np.ones((P, 1)),
        "win": -BIG * ((col < np.clip(row % 64 - 8, 0, 48)) | (col >= np.clip(row % 64 - 8, 0, 48) + 16)),
        "adm": -BIG * ((row < 64) & (col >= 64)),
    }
    return np.concatenate([m[k].astype(np.float32) for k in MASKS], 1)


class Chip:

    def __init__(self, nc, ctx, arrays, plan):
        self.nc, self.ctx, self.A, self.plan = nc, ctx, arrays, plan

        def sb(name, shape, dt=F32):
            return ctx.enter_context(nc.sbuf_tensor(name, shape, dt))

        self.xT = sb("xT", [P, KD, T])
        self.hT = sb("hT", [P, KD, T])
        self.ring = sb("weight_ring", [P, RING, SLOT])
        self.W = sb("work", [P, 12, 2048])
        self.vec = sb("vectors", [P, NVEC])
        self.msk = sb("masks", [P, len(MASKS) * P])
        self.csil = sb("silu_of_conditions", [P, KD, 32])
        self.mstage = sb("modulation_rows", [P, 4, P])
        self.mod1 = sb("mod1", [P, 24])
        self.mod2 = sb("mod2", [P, 48, 2])
        self.sm = sb("small", [P, 192])
        self.eps = sb("eps", [P, 4])
        self.ps = ctx.enter_context(nc.psum_tensor("ps", [P, BANKS, 512], F32))
        self.S = {}
        self.free_at = {}
        for n in ("tensor_step", "vector_step", "scalar_step", "pool_step", "aux_loaded"):
            self.counter(n)
        self.loaded = [self.counter(f"weights_loaded{i}") for i in range(RING)]
        self.arrived = {}
        self.issued = 0
        self.used = 0

    def counter(self, name):
        if name not in self.S:
            self.S[name] = Counter(self.ctx.enter_context(self.nc.semaphore(name)))
        return self.S[name].rebase()

    def counters(self, *names):
        return [self.counter(n) for n in names]

    def v(self, name, i=0, n=None):
        a, w = AT[name]
        return self.vec[:, a + i:a + i + (n or 1)]

    def m(self, name):
        i = MASKS.index(name)
        return self.msk[:, i * P:(i + 1) * P]

    def m4(self, name):
        return self.m(name).unsqueeze(1).to_broadcast([P, 4, P])

    def slot(self, i, n=1, kt=None):
        a = self.W[:, i:i + n, :].rearrange("p s n -> p (s n)")
        return a.rearrange("p (k t) -> p k t", t=T)

    def rslot(self, i):
        a = self.ring[:, i // 2, (i % 2) * 2048:(i % 2 + 1) * 2048]
        return a.rearrange("p (k t) -> p k t", t=T)

    def stream(self, sp, upto):
        upto = min(upto, len(self.plan))
        while self.issued < upto:
            i = self.issued
            sources, kt, c = self.plan[i]
            if i >= RING:
                sp.wait_ge(*self.free_at[i - RING])
            sig = self.loaded[i % RING]
            dst = self.block_view(i)
            for src, c0, n in sources:
                sp.dma_start(dst[:, :, c0:c0 + n], src).then_inc(sig.sem, 16)
                sig.total += 16
            self.arrived[i] = (sig.sem, sig.total)
            self.issued += 1

    def block_view(self, i):
        _, kt, c = self.plan[i]
        return self.ring[:, i % RING, 0:kt * c].rearrange("p (k c) -> p k c", k=kt)

    def block_wait(self, eng, i):
        eng.wait_ge(*self.arrived[i])


def blocks(w, c0, c1):
    kt = w.shape[0] // P
    width = min(SLOT // kt, 512)
    out = []
    for c in range(c0, c1, width):
        n = min(width, c1 - c)
        out.append(([(w[:, c:c + n].rearrange("(k p) c -> p k c", p=P), 0, n)], kt, n))
    return out


def joined(w, parts):
    c, sources = 0, []
    for c0, c1 in parts:
        sources.append((w[:, c0:c1].rearrange("(k p) c -> p k c", p=P), c, c1 - c0))
        c += c1 - c0
    return [(sources, w.shape[0] // P, c)]


def project(ch, nblocks, tiles, ahead=RING, extra_sync=None, vector_after=None, scalar_after=None):
    nc = ch.nc
    first = ch.used
    R = BANKS
    ready, by_act, by_dve = ch.counters("tile_ready", "tile_scalar_done", "tile_vector_done")
    na = np.cumsum([t[5][0] is not None for t in tiles])
    nv = np.cumsum([t[5][1] is not None for t in tiles])

    def shape(t):
        b, kind, where, src, ntok, _ = t
        c = ch.plan[first + b][2] if b is not None else P
        if kind == "T":
            return min(P, c - where), ntok
        if kind == "N":
            return P, c
        if isinstance(kind, tuple):
            return P, kind[2] - kind[1]
        return P, P

    for n, t in enumerate(tiles):
        if t[0] is not None:
            ch.free_at[first + t[0]] = (ready.sem, ready.at(n + 1))

    with nc.Block() as block:
        @block.sync
        def _(sp):
            if extra_sync:
                extra_sync(sp)
            ch.stream(sp, first + nblocks + ahead)

        @block.tensor
        def _(pe):
            last = -1
            for n, t in enumerate(tiles):
                b, kind, where, src, ntok, ev = t
                i = first + b if b is not None else None
                if b is not None and b != last:
                    ch.block_wait(pe, i)
                    last = b
                if n >= R:
                    if tiles[n - R][5][1] is not None:
                        pe.wait_ge(by_dve.sem, by_dve.at(int(nv[n - R])))
                    else:
                        pe.wait_ge(by_act.sem, by_act.at(int(na[n - R])))
                m, f = shape(t)
                bank = ch.ps[:, n % R, :]
                if kind == "X":
                    pe.wait_ge(by_act.sem, by_act.at(int(na[where])))
                    ins = pe.transpose(bank[:, 0:P], src, ch.m("ident"))
                    ins.then_inc(ready.sem, 1)
                    ready.total += 1
                    continue
                w = ch.block_view(i)
                _, kt, c = ch.plan[i]
                if kind == "M":
                    for k in range(kt):
                        for g in range(4):
                            ins = pe.matmul(bank[32 * g:32 * g + 32, 0:P], ch.csil[:, k, :],
                                            w[:, k, g * P:(g + 1) * P], start=k == 0, stop=k == kt - 1)
                else:
                    for k in range(kt):
                        if kind == "T":
                            ins = pe.matmul(bank[0:m, 0:f], w[:, k, where:where + m], src[:, k, 0:ntok],
                                            start=k == 0, stop=k == kt - 1)
                        else:
                            c0 = kind[1] if isinstance(kind, tuple) else 0
                            ins = pe.matmul(bank[0:m, 0:f], src[:, k, where:where + P], w[:, k, c0:c0 + f],
                                            start=k == 0, stop=k == kt - 1)
                ins.then_inc(ready.sem, 1)
                ready.total += 1

        @block.scalar
        def _(act):
            a = Line(act, ch.S["scalar_step"])
            for n, t in enumerate(tiles):
                if t[5][0] is not None:
                    m, f = shape(t)
                    a.after(ready, n + 1)
                    t[5][0](a, act, ch.ps[0:m, n % R, 0:f], by_act)
            if scalar_after:
                scalar_after(a, act)

        @block.vector
        def _(dve):
            v = Line(dve, ch.S["vector_step"])
            for n, t in enumerate(tiles):
                if t[5][1] is not None:
                    m, f = shape(t)
                    v.after(ready, n + 1)
                    if t[5][0] is not None:
                        v.after(by_act, int(na[n]))
                    t[5][1](v, dve, ch.ps[0:m, n % R, 0:f], by_dve)
            if vector_after:
                vector_after(v, dve)
    ch.used = first + nblocks


def weave(main, side):
    out = []
    for i in range(max(len(main), len(side))):
        out += [x[i] for x in (main, side) if i < len(x)]
    return out


def modulated(ch, tiles, nblocks, bands):
    place = {}
    for x in weave([("main", b) for b in range(nblocks)], [("side", i) for i in range(len(bands))]):
        place[x] = len(place)
    out, pending = [], []

    def turn_rows(i, m):
        dst, bias, first = bands[i]
        n = dst.shape[2]

        def part(v, dve, ps, sig):
            v(dve.tensor_tensor(dst, ps.rearrange("p (g r) -> p g r", r=32)[:, :, first:first + n],
                                bias.unsqueeze(2).to_broadcast([P, 4, n]), ADD), sig)
        return (None, "X", m, ch.mstage[:, i % 4, :], T, (None, part))

    for kind, i in sorted(place, key=place.get):
        b = place[kind, i]
        if kind == "main":
            mine = [t for t in tiles if t[0] == i]
            out += [(b,) + mine[0][1:]]
            out += [turn_rows(*x) for x in pending]
            pending = []
            out += [(b,) + t[1:] for t in mine[1:]]
        else:
            if pending and nblocks <= i:
                out += [turn_rows(*x) for x in pending]
                pending = []
            pending.append((i, len(out)))
            out.append((b, "M", 0, None, T, copy_to(ch.mstage[:, i % 4, :])))
    return out + [turn_rows(*x) for x in pending], len(place)


def copy_to(out):
    return (lambda a, act, ps, sig: a(act.copy(out, ps), sig), None)


def act_to(out, func, **kw):
    return (lambda a, act, ps, sig: a(act.activation(out, ps, func, **kw), sig), None)


def normalise(ch, src, dst, ntok, gain, shift, width=D):
    nc, kt = ch.nc, width // P
    sq_ready, sq_used, root_ready, scaled, shifted = ch.counters(
        "square_ready", "square_used", "root_ready", "scaled", "shifted")
    sq = ch.slot(0)
    rstd = ch.slot(1)[:, 0, 0:ntok]
    tmp = ch.slot(1)[:, 1:3, 0:ntok]
    with nc.Block() as block:
        @block.scalar
        def _(act):
            a = Line(act, ch.S["scalar_step"])
            for k in range(kt):
                if k >= 4:
                    a.after(sq_used, k - 3)
                a(act.square(sq[:, k % 4, 0:ntok], src[:, k, 0:ntok]), sq_ready)
            a.after(sq_used, kt)
            a(act.activation(rstd, ch.ps[:, 0, 0:ntok], ACT.Sqrt, bias=ch.eps[:, 0:1], scale=1.0 / width),
              root_ready)
            if shift is not None:
                for k in range(kt):
                    a.after(scaled, k + 1)
                    a(act.activation(dst[:, k, 0:ntok], tmp[:, k % 2, :], ACT.Identity, bias=shift[k]),
                      shifted)

        @block.tensor
        def _(pe):
            for k in range(kt):
                pe.wait_ge(sq_ready.sem, sq_ready.at(k + 1))
                pe.matmul(ch.ps[:, 0, 0:ntok], ch.m("ones"), sq[:, k % 4, 0:ntok],
                          start=k == 0, stop=k == kt - 1).then_inc(sq_used.sem, 1)
                sq_used.total += 1

        @block.vector
        def _(dve):
            v = Line(dve, ch.S["vector_step"])
            v.after(root_ready, 1)
            v(dve.reciprocal(rstd, rstd))
            for k in range(kt):
                if shift is not None and k >= 2:
                    v.after(shifted, k - 1)
                out = dst[:, k, 0:ntok] if shift is None else tmp[:, k % 2, :]
                v(dve.scalar_tensor_tensor(out, src[:, k, 0:ntok], gain[k], rstd, MUL, MUL), scaled)



def load_constants(ch):
    nc, A = ch.nc, ch.A
    got = ch.counter("aux_loaded")
    with nc.Block() as block:
        @block.sync
        def _(sp):
            for dst, src in ((ch.vec[:, :], A["vectors"]), (ch.msk[:, :], A["masks"]),
                             (ch.xT[:, :, :], A["xT"].rearrange("(k p) t -> p k t", p=P))):
                sp.dma_start(dst, src).then_inc(got.sem, 16)
                got.total += 16
            ch.stream(sp, RING)
            sp.wait_ge(got.sem, got.total)

        @block.vector
        def _(dve):
            v = Line(dve, ch.S["vector_step"])
            for i, e in enumerate((1e-6, 64e-5, 0.0, 1.0)):
                v(dve.memset(ch.eps[:, i:i + 1], e))
            v(dve.memset(ch.csil[:, :, :], 0.0))
    with nc.Block() as block:
        @block.scalar
        def _(act):
            a = Line(act, ch.S["scalar_step"])
            for i, name in enumerate(("c", "c_2", "c_ctx_2")):
                a(act.activation(ch.csil[:, :, i], ch.v(name, 0, 8), ACT.Silu))


def block1_modulation(ch):
    bands = [(ch.mod1[:, 4 * b:4 * b + 4].unsqueeze(2), ch.v("b_ada", 4 * b, 4), 0) for b in range(6)]
    tiles, n = modulated(ch, [], 0, bands)
    project(ch, n, tiles)
    with ch.nc.Block() as block:
        @block.vector
        def _(dve):
            v = Line(dve, ch.S["vector_step"])
            v(dve.scalar_tensor_tensor(ch.sm[:, 24:32], ch.mod1[:, 8:16], 1.0, ch.v("norm_w", 0, 8), ADD, MUL))
            v(dve.tensor_scalar(ch.sm[:, 32:49], ch.v("mu", 0, 17), -1.0, 1.0, MUL, ADD))


def bands2(ch, b0, b1):
    return [(ch.mod2[:, 4 * b:4 * b + 4, :], ch.v("b_mod_2", 4 * b, 4), 1) for b in range(b0, b1)]


def block1_rwkv_projection(ch):
    tmp = ch.slot(9, 2)
    outs = [(ch.slot(0), 0), (ch.slot(1), 4), (ch.slot(2), 8), (ch.slot(11), 12), (ch.slot(3), 13)]
    tiles = []
    for b, (dst, first) in enumerate(outs):
        for j in range(1 if first == 12 else 4):
            t8 = tmp[:, len(tiles) % 8, :]
            one_mu, mu = ch.sm[:, 32 + first + j:33 + first + j], ch.v("mu", first + j)

            def part_a(a, act, ps, sig, t8=t8, one_mu=one_mu):
                a(act.activation(t8, ps, ACT.Identity, scale=one_mu, bias=ch.eps[:, 2:3]), sig)

            def part_v(v, dve, ps, sig, t8=t8, mu=mu, o=dst[:, j, :]):
                v(dve.tensor_copy(o[:, 0:1], t8[:, 0:1]))
                v(dve.scalar_tensor_tensor(o[:, 1:T], ps[:, 0:T - 1], mu, t8[:, 1:T], MUL, ADD), sig)
            tiles.append((b, "T", j * P, ch.hT, T, (part_a, part_v)))
    tiles, n = modulated(ch, tiles, 5, bands2(ch, 0, 5))
    project(ch, n, tiles, ahead=0)


def rwkv_prepare(ch):
    nc = ch.nc
    rT, kT, vT, lora = ch.slot(0), ch.slot(1), ch.slot(2), ch.slot(11)[:, 0, :]
    nT, rdT, bT, kdT, bonus = ch.slot(4), ch.slot(5), ch.slot(6), ch.slot(7), ch.slot(8)
    t0, t1, t2, t3, t4, t5, t6, t7 = [ch.rslot(i) for i in range(8)]
    th = ch.slot(11)[:, 1, :]
    keep = ch.slot(11)[:, 2, :]
    wup = ch.slot(9)[:, 0, :]
    aux = ch.counter("aux_loaded")
    (sq_ready, th_ready, products, lora_out, roots, cum_ready, exps, cml_ready, bonus_in) = ch.counters(
        "key_square_ready", "tanh_ready", "prep_products", "lora_read", "roots_ready", "cum_ready",
        "exps_ready", "cml_ready", "bonus_in_ready")
    ps = ch.ps
    with nc.Block() as block:
        @block.sync
        def _(sp):
            for dst, src in ((wup[0:64, :], ch.A["w_up"]), (wup[64:128, :], ch.A["a_up"])):
                sp.dma_start(dst, src).then_inc(aux.sem, 16)
                aux.total += 16

        @block.vector
        def _(dve):
            v = Line(dve, ch.S["vector_step"])
            for j in range(4):
                v(dve.tensor_scalar(t0[:, j, :], kT[:, j, :], ch.v("k_k", j), None, MUL))
                v(dve.tensor_tensor(t1[:, j, :], t0[:, j, :], t0[:, j, :], MUL), sq_ready)
            v(dve.memset(keep, 1.0))
            v(dve.memset(keep.rearrange("p (c t) -> p c t", t=64)[:, :, 0:1], 0.0))
            v.after(lora_out, 8)
            v(dve.tensor_scalar(t2, t2, -DECAY, None, MUL))
            for j in range(4):
                v(dve.tensor_tensor_scan(t4[:, j, :], keep, t2[:, j, :], 0.0, MUL, ADD), cum_ready)
            v(dve.tensor_tensor(t5, t4, t2, SUB), cml_ready)
            v.after(roots, 4)
            v(dve.tensor_scalar(t1, t1, 1e-12, None, MAX))
            v(dve.reciprocal(t1, t1))
            v(dve.tensor_tensor(t0, t0, t1, MUL))
            v(dve.tensor_tensor(t1, t0, t3, MUL))
            for j in range(4):
                v(dve.tensor_scalar(t3[:, j, :], t3[:, j, :], 1.0, ch.v("k_a", j), SUB, MUL))
                v(dve.scalar_tensor_tensor(t3[:, j, :], t3[:, j, :], 1.0, kT[:, j, :], ADD, MUL))
                v(dve.scalar_tensor_tensor(t2[:, j, :], rT[:, j, :], ch.v("r_k", j), t3[:, j, :], MUL, MUL),
                  bonus_in)
            v.after(exps, 3)
            v(dve.scalar_tensor_tensor(nT, t0, -1.0, t5, MUL, MUL))
            v(dve.tensor_tensor(rdT, rT, t6, MUL))
            v(dve.tensor_tensor(bT, t1, t7, MUL))
            v(dve.tensor_tensor(kdT, t3, t7, MUL))
            v(dve.tensor_copy(ch.sm[:, 64:96].rearrange("p (j c) -> p j c", c=8),
                              t6.rearrange("p j (c t) -> p j c t", t=64)[:, :, :, 63]))
            for j in range(4):
                v.after(products, 13 + j)
                v(dve.tensor_tensor(bonus[:, j, :], vT[:, j, :], ps[:, 4 + j, :], MUL))

        @block.scalar
        def _(act):
            a = Line(act, ch.S["scalar_step"])
            a(act.activation(th[0:64, :], lora[0:64, :], ACT.Tanh), th_ready)
            for j in range(4):
                a.after(products, j + 1)
                a(act.activation(t2[:, j, :], ps[:, j, :], ACT.Sigmoid, bias=ch.v("w0", j)), lora_out)
            for j in range(4):
                a.after(products, 5 + j)
                a(act.activation(t3[:, j, :], ps[:, 4 + j, :], ACT.Sigmoid, bias=ch.v("a0", j)), lora_out)
            for j in range(4):
                a.after(products, 9 + j)
                a(act.activation(t1[:, j, :], ps[:, j, :], ACT.Sqrt, bias=ch.eps[:, 2:3]), roots)
            a.after(cum_ready, 4)
            a(act.activation(t6, t4, ACT.Exp), exps)
            a(act.activation(t7, t4, ACT.Exp, scale=-1.0), exps)
            a.after(cml_ready, 1)
            a(act.activation(t5, t5, ACT.Exp), exps)

        @block.tensor
        def _(pe):
            def product(*args):
                pe.matmul(*args, start=True, stop=True).then_inc(products.sem, 1)
                products.total += 1
            pe.wait_ge(aux.sem, aux.total)
            pe.wait_ge(th_ready.sem, th_ready.at(1))
            for j in range(4):
                product(ps[:, j, :], wup[0:64, j * P:(j + 1) * P], th[0:64, :])
            for j in range(4):
                product(ps[:, 4 + j, :], wup[64:128, j * P:(j + 1) * P], lora[64:128, :])
            for j in range(4):
                pe.wait_ge(sq_ready.sem, sq_ready.at(j + 1))
                pe.wait_ge(lora_out.sem, lora_out.at(j + 1))
                product(ps[:, j, :], ch.m("blk64"), t1[:, j, :])
            for j in range(4):
                pe.wait_ge(bonus_in.sem, bonus_in.at(j + 1))
                pe.wait_ge(lora_out.sem, lora_out.at(8))
                product(ps[:, 4 + j, :], ch.m("blk64"), t2[:, j, :])


def rwkv_transpose(ch):
    nc, ps = ch.nc, ch.ps
    pairs = [(ch.slot(6), ch.slot(9)), (ch.slot(7), ch.slot(10)), (ch.slot(2), ch.slot(11)),
             (ch.slot(4), ch.rslot(7))]
    turned, copied = ch.counters("turned", "turned_copied")
    with nc.Block() as block:
        @block.tensor
        def _(pe):
            for n in range(16):
                src = pairs[n // 4][0]
                if n >= 4:
                    pe.wait_ge(copied.sem, copied.at(n - 3))
                for j in range(4):
                    ins = pe.transpose(ps[:, n % 4, j * P:(j + 1) * P], src[:, j, (n % 4) * P:(n % 4 + 1) * P],
                                       ch.m("ident"))
                ins.then_inc(turned.sem, 1)
                turned.total += 1

        @block.scalar
        def _(act):
            a = Line(act, ch.S["scalar_step"])
            for n in range(16):
                a.after(turned, n + 1)
                a(act.copy(pairs[n // 4][1][:, n % 4, :], ps[:, n % 4, :]), copied)


def rwkv_within_chunks(ch):
    nc, ps = ch.nc, ch.ps
    nT, bT, kdT = ch.slot(4), ch.slot(6), ch.slot(7)
    vN, nN = ch.slot(11), ch.rslot(7)
    w1T, w2 = ch.slot(0), ch.slot(1)

    def mats(i):
        return ch.rslot(i).rearrange("p b (s t) -> p b s t", t=P)
    d, xd, xo, lk, d2, xd2, inv = [mats(i) for i in range(7)]
    I4 = ch.m4("ident")
    products, evacuated = ch.counters("chunk_products", "chunk_evacuated")

    def head(half, b):
        h = 4 * half + b
        return h, slice(64 * (h % 2), 64 * (h % 2) + 64), h // 2

    def tok(s):
        return slice(s * P, (s + 1) * P)

    def steps(half):
        def gram(left, right):
            def f(b, s):
                h, rows, j = head(half, b)
                return left[rows, j, tok(s)], right[rows, j, tok(s)]
            return f

        def mm(left, right):
            return lambda b, s: (left[:, b, s, :], right[:, b, s, :])

        def value(left):
            def f(b, s):
                h, _, _ = head(half, b)
                return left[:, b, s, :], vN[:, s, h * HD:(h + 1) * HD]
            return f
        return [
            (gram(nT, bT), "mask", [(d, "mL16")]), (gram(bT, nT), "mask", [(xd, "mU16"), (xo, "mUoff")]),
            (gram(kdT, nT), "mask", [(lk, "mU")]),
            (mm(xd, d), "copy", d2), (mm(d, xd), "copy", xd2),
            (mm(d2, inv), "add", (inv, inv)),
            (mm(xd2, d2), "copy", d), (mm(d2, xd2), "copy", xd),
            (mm(d, inv), "add", (inv, inv)),
            (mm(xd, d), "copy", d2), (mm(d2, inv), "add", (inv, inv)),
            ("turn", "copy", xd2), (mm(xo, xd2), "copy", d2),
            (mm(d2, inv), "add", (d, inv)), (mm(d2, d), "add", (d, inv)), (mm(d2, d), "add", (d, inv)),
            (value(lk), "value", xd), ("w2", "w2", None), ("w1", "w1", None),
        ]

    with nc.Block() as block:
        @block.tensor
        def _(pe):
            n = 0
            for half in range(2):
                for left_right, how, _ in steps(half):
                    for b in range(4):
                        if n >= 4:
                            pe.wait_ge(evacuated.sem, evacuated.at(n - 3))
                        h, rows, j = head(half, b)
                        bank = ps[:, n % BANKS, :]
                        for s in range(4):
                            if left_right == "turn":
                                ins = pe.transpose(bank[:, tok(s)], inv[:, b, s, :], ch.m("ident"))
                            elif left_right == "w2":
                                ins = pe.matmul(bank[:, s * HD:(s + 1) * HD], d[:, b, s, :], xd[:, b, s, 0:HD],
                                                start=True, stop=True)
                            elif left_right == "w1":
                                ins = pe.matmul(bank[rows, tok(s)], nN[:, s, h * HD:(h + 1) * HD],
                                                d[:, b, s, :], start=True, stop=True)
                            else:
                                left, right = left_right(b, s)
                                ins = pe.matmul(bank[:, s * right.shape[-1]:(s + 1) * right.shape[-1]],
                                                left, right, start=True, stop=True)
                        ins.then_inc(products.sem, 1)
                        products.total += 1
                        n += 1

        @block.vector
        def _(dve):
            v = Line(dve, ch.S["vector_step"])
            n = 0
            for half in range(2):
                for left_right, how, out in steps(half):
                    for b in range(4):
                        h, rows, j = head(half, b)
                        v.after(products, n + 1)
                        flat = ps[:, n % BANKS, :]
                        bank = flat.rearrange("p (s t) -> p s t", t=P)
                        if how == "mask":
                            if len(out) == 2:
                                v(dve.tensor_tensor(out[0][0][:, b], bank, ch.m4(out[0][1]), MUL))
                                v(dve.tensor_tensor(inv[:, b], out[0][0][:, b], I4, ADD))
                            v(dve.tensor_tensor(out[-1][0][:, b], bank, ch.m4(out[-1][1]), MUL), evacuated)
                        elif how == "copy":
                            v(dve.tensor_copy(out[:, b], bank), evacuated)
                        elif how == "add":
                            v(dve.tensor_tensor(out[0][:, b], bank, out[1][:, b], ADD), evacuated)
                        elif how == "value":
                            v(dve.tensor_copy(xd[:, b, :, 0:HD], flat[:, 0:4 * HD].rearrange("p (s t) -> p s t", t=HD)),
                              evacuated)
                        elif how == "w2":
                            v(dve.tensor_copy(w2[:, :, h * HD:(h + 1) * HD],
                                              flat[:, 0:4 * HD].rearrange("p (s t) -> p s t", t=HD)), evacuated)
                        elif how == "w1":
                            v(dve.tensor_copy(w1T[rows, j, :], flat[rows, :]), evacuated)
                        n += 1


def rwkv_chain(ch):
    nc, ps = ch.nc, ch.ps
    w1T, u = ch.slot(0), ch.slot(1)
    bN, kN, vN = ch.slot(9), ch.slot(10), ch.slot(11)
    states = [ch.rslot(c).rearrange("p j (h t) -> p (j h t)", t=P)[:, 0:512].rearrange("p (j t) -> p j t", t=P)
              for c in range(8)]
    tmp = ch.rslot(0)[:, 1, :].rearrange("p (j t) -> p j t", t=P)
    bd = ch.m4("bd")
    end = ch.sm[:, 64:96].rearrange("p (j c) -> p j c", c=8)
    u_sum, u_ready, s_sum, s_ready = ch.counters("u_sum", "u_ready", "state_sum", "state_ready")
    with nc.Block() as block:
        @block.tensor
        def _(pe):
            for c in range(7):
                s, rows = c // 2, slice(64 * (c % 2), 64 * (c % 2) + 64)
                if c > 0:
                    pe.wait_ge(s_ready.sem, s_ready.at(c + 1))
                    for j in range(4):
                        ins = pe.matmul(ps[rows, 0, j * P:(j + 1) * P], w1T[:, j, c * 64:(c + 1) * 64],
                                        states[c][:, j, :], start=True, stop=True)
                    ins.then_inc(u_sum.sem, 1)
                    u_sum.total += 1
                    pe.wait_ge(u_ready.sem, u_ready.at(c))
                for j in range(4):
                    cols = slice(j * P, (j + 1) * P)
                    pe.matmul(ps[:, 1, cols], kN[rows, s, cols], vN[rows, s, cols], start=True, stop=False)
                    ins = pe.matmul(ps[:, 1, cols], bN[rows, s, cols], u[rows, s, cols], start=False, stop=True)
                ins.then_inc(s_sum.sem, 1)
                s_sum.total += 1
            pe.wait_ge(s_ready.sem, s_ready.at(8))
            for j in range(4):
                ins = pe.matmul(ps[64:128, 0, j * P:(j + 1) * P], w1T[:, j, 7 * 64:8 * 64],
                                states[7][:, j, :], start=True, stop=True)
            ins.then_inc(u_sum.sem, 1)
            u_sum.total += 1

        @block.vector
        def _(dve):
            v = Line(dve, ch.S["vector_step"])
            v(dve.memset(states[0], 0.0), s_ready)
            for c in range(8):
                s, rows = c // 2, slice(64 * (c % 2), 64 * (c % 2) + 64)
                if c > 0:
                    v.after(u_sum, c)
                    v(dve.tensor_tensor(u[rows, s, :], ps[rows, 0, :], u[rows, s, :], ADD), u_ready)
                if c < 7:
                    v.after(s_sum, c + 1)
                    v(dve.tensor_tensor(tmp, ps[:, 1, :].rearrange("p (j t) -> p j t", t=P), bd, MUL))
                    v(dve.tensor_tensor(tmp, tmp, states[c], ADD))
                    v(dve.tensor_tensor(states[c + 1], tmp, end[:, :, c:c + 1].to_broadcast([P, 4, P]), MUL),
                      s_ready)


def rwkv_output(ch):
    nc, ps = ch.nc, ch.ps
    rdT, bT, kdT, bonus, gate = ch.slot(5), ch.slot(6), ch.slot(7), ch.slot(8), ch.slot(3)
    u, vN, yT = ch.slot(1), ch.slot(11), ch.slot(2)
    states = [ch.rslot(c).rearrange("p j (h t) -> p (j h t)", t=P)[:, 0:512].rearrange("p (j t) -> p j t", t=P)
              for c in range(8)]
    mb = [ch.rslot(i)[:, 2, :].rearrange("p (s t) -> p s t", t=P) for i in range(4)]
    mI = ch.m4("mUI")
    cen, sq = ch.slot(0), ch.slot(4)
    grams, masked, y_sum, y_out, sums, cen_out, sq_out, roots = ch.counters(
        "grams", "grams_masked", "y_sum", "y_out", "y_means", "y_centred", "y_squares", "y_roots")
    with nc.Block() as block:
        @block.tensor
        def _(pe):
            for j in range(4):
                for e in range(2):
                    rows = slice(64 * e, 64 * e + 64)
                    for i, key in enumerate((bT, kdT)):
                        n = 4 * j + 2 * e + i
                        if n >= 4:
                            pe.wait_ge(masked.sem, masked.at(n - 3))
                            if j >= 1:
                                pe.wait_ge(y_sum.sem, y_sum.at(j))
                        for s in range(4):
                            cols = slice(s * P, (s + 1) * P)
                            ins = pe.matmul(ps[:, 2 * e + i, cols], key[rows, j, cols], rdT[rows, j, cols],
                                            start=True, stop=True)
                        ins.then_inc(grams.sem, 1)
                        grams.total += 1
                pe.wait_ge(masked.sem, masked.at(4 * j + 4))
                if j >= 2:
                    pe.wait_ge(y_out.sem, y_out.at(j - 1))
                bank = 4 + j % 2
                for c in range(8):
                    pe.matmul(ps[:, bank, c * 64:(c + 1) * 64], states[c][:, j, :], rdT[:, j, c * 64:(c + 1) * 64],
                              start=c == 0, stop=False, skip_group_check=True)
                for e in range(2):
                    rows, hc = slice(64 * e, 64 * e + 64), slice((2 * j + e) * HD, (2 * j + e + 1) * HD)
                    for s in range(4):
                        cols = slice(s * P, (s + 1) * P)
                        pe.matmul(ps[rows, bank, cols], u[:, s, hc], mb[2 * e][:, s, :], start=False, stop=False,
                                  skip_group_check=True)
                        ins = pe.matmul(ps[rows, bank, cols], vN[:, s, hc], mb[2 * e + 1][:, s, :],
                                        start=False, stop=e == 1 and s == 3, skip_group_check=True)
                ins.then_inc(y_sum.sem, 1)
                y_sum.total += 1
            for j in range(4):
                pe.wait_ge(y_out.sem, y_out.at(j + 1))
                pe.matmul(ps[:, j, :], ch.m("blk64"), yT[:, j, :], start=True, stop=True).then_inc(sums.sem, 1)
                sums.total += 1
            for j in range(4):
                pe.wait_ge(sq_out.sem, sq_out.at(j + 1))
                if j < 2:
                    pe.wait_ge(y_out.sem, y_out.at(4))
                pe.matmul(ps[:, 4 + j, :], ch.m("blk64"), sq[:, j, :], start=True, stop=True).then_inc(sums.sem, 1)
                sums.total += 1

        @block.vector
        def _(dve):
            v = Line(dve, ch.S["vector_step"])
            for j in range(4):
                for n in range(4):
                    v.after(grams, 4 * j + n + 1)
                    if j >= 1 and n == 0:
                        v.after(y_sum, j)
                    v(dve.tensor_tensor(mb[n], ps[:, n, :].rearrange("p (s t) -> p s t", t=P), mI, MUL), masked)
            for j in range(4):
                v.after(sums, j + 1)
                v(dve.scalar_tensor_tensor(cen[:, j, :], ps[:, j, :], -1.0 / HD, yT[:, j, :], MUL, ADD), cen_out)
            v.after(roots, 4)
            v(dve.reciprocal(sq, sq))
            v(dve.tensor_tensor(cen, cen, sq, MUL))
            for j in range(4):
                v(dve.tensor_scalar(cen[:, j, :], cen[:, j, :], ch.v("gn_w", j), ch.v("gn_b", j), MUL, ADD))
            v(dve.tensor_tensor(cen, cen, bonus, ADD))
            v.after(roots, 5)
            v(dve.tensor_tensor(yT, cen, gate, MUL))

        @block.scalar
        def _(act):
            a = Line(act, ch.S["scalar_step"])
            for j in range(4):
                a.after(y_sum, j + 1)
                a(act.copy(yT[:, j, :], ps[:, 4 + j % 2, :]), y_out)
            for j in range(4):
                a.after(cen_out, j + 1)
                a(act.square(sq[:, j, :], cen[:, j, :]), sq_out)
            for j in range(4):
                a.after(sums, 5 + j)
                a(act.activation(sq[:, j, :], ps[:, 4 + j, :], ACT.Sqrt, bias=ch.eps[:, 1:2], scale=1.0 / HD), roots)
            a(act.activation(gate, gate, ACT.Silu), roots)


def head_norm(ch, tiles, mask, width, eps_col=0):
    nc, ps = ch.nc, ch.ps
    squares, sums, roots, normed = ch.counters("hn_squares", "hn_sums", "hn_roots", "hn_normed")
    n = tiles[0][0].shape[-1]
    sq = ch.slot(9)[:, :, 0:n]
    rt = ch.slot(10)[:, :, 0:n]
    with nc.Block() as block:
        @block.scalar
        def _(act):
            a = Line(act, ch.S["scalar_step"])
            for i in range(len(tiles) + 2):
                if i < len(tiles):
                    if i >= 4:
                        a.after(sums, i - 3)
                    a(act.square(sq[:, i % 4, :], tiles[i][0]), squares)
                if i >= 2:
                    k = i - 2
                    a.after(sums, k + 1)
                    if k >= 4:
                        a.after(normed, k - 3)
                    a(act.activation(rt[:, k % 4, :], ps[:, k % 4, 0:n], ACT.Sqrt, bias=ch.eps[:, eps_col:eps_col + 1],
                                     scale=1.0 / width), roots)

        @block.tensor
        def _(pe):
            for i in range(len(tiles)):
                pe.wait_ge(squares.sem, squares.at(i + 1))
                if i >= 4:
                    pe.wait_ge(roots.sem, roots.at(i - 3))
                pe.matmul(ps[:, i % 4, 0:n], ch.m(mask), sq[:, i % 4, :], start=True, stop=True).then_inc(sums.sem, 1)
                sums.total += 1

        @block.vector
        def _(dve):
            v = Line(dve, ch.S["vector_step"])
            for i, (x, gain) in enumerate(tiles):
                v.after(roots, i + 1)
                v(dve.reciprocal(rt[:, i % 4, :], rt[:, i % 4, :]))
                v(dve.scalar_tensor_tensor(x, x, gain, rt[:, i % 4, :], MUL, MUL), normed)


def attention(ch, units, scale, sinks=False, sync_body=None):
    nc, ps = ch.nc, ch.ps
    wide = ch.slot(9, 2).rearrange("p k t -> p (k t)")
    S = [wide[:, i * 768:(i + 1) * 768] for i in range(3)]
    pT = [wide[:, (3 + i) * 768:(4 + i) * 768] for i in range(2)]
    st = ch.sm[:, 96:120].rearrange("p (i c) -> p i c", c=6)
    scores, softened, taken_max, expd, normed, turned, copied, summed, taken = ch.counters(
        "scores", "scores_scaled", "maxima_ready", "exps_done", "probs_normed", "probs_turned", "probs_copied",
        "values_summed", "group_taken")
    N = len(units)
    group, g = [], 0
    for u in units:
        group.append(g)
        g += u["close"] is not None
    with nc.Block() as block:
        if sync_body:
            @block.sync
            def _(sp):
                sync_body(sp, softened)

        @block.tensor
        def _(pe):
            for i in range(N + 3):
                if i < N:
                    u = units[i]
                    if i >= 2:
                        pe.wait_ge(softened.sem, softened.at(i - 1))
                    for k, c0 in u["keys"]:
                        n = k.shape[-1] if len(k.shape) == 2 else k.shape[-1] * k.shape[-2]
                        bank, off = 2 * (i % 2) + c0 // 512, c0 % 512
                        ins = pe.matmul(ps[:, bank, off:off + n], u["q"], k, start=True, stop=True)
                    ins.then_inc(scores.sem, 1)
                    scores.total += 1
                if 2 <= i < N + 2:
                    u = units[i - 2]
                    pe.wait_ge(normed.sem, normed.at(i - 1))
                    if i >= 3:
                        pe.wait_ge(copied.sem, copied.at(i - 2))
                    for t in range(u["cols"] // P):
                        ins = pe.transpose(ps[:, 4 + t // 4, (t % 4) * P:(t % 4 + 1) * P],
                                           S[(i - 2) % 3][:, t * P:(t + 1) * P], ch.m("ident"))
                    ins.then_inc(turned.sem, 1)
                    turned.total += 1
                if i >= 3:
                    u, gi = units[i - 3], group[i - 3]
                    pe.wait_ge(copied.sem, copied.at(i - 2))
                    if gi >= 2:
                        pe.wait_ge(taken.sem, taken.at(gi - 1))
                    vs = u["values"]
                    for t, val in enumerate(vs):
                        ins = pe.matmul(ps[u["rows"], 6 + gi % 2, u["col"]:u["col"] + P], val,
                                        pT[(i - 3) % 2][:, t * P:(t + 1) * P], start=t == 0, stop=t == len(vs) - 1)
                    ins.then_inc(summed.sem, 1)
                    summed.total += 1

        @block.vector
        def _(dve):
            v = Line(dve, ch.S["vector_step"])
            for i in range(N + 5):
                if i < N:
                    u, s = units[i], S[i % 3]
                    stat = st[:, i % 4, :]
                    v.after(scores, i + 1)
                    if i >= 3:
                        v.after(turned, i - 2)
                    if u.get("prepare"):
                        u["prepare"](v, dve)
                    both = ps[:, 2 * (i % 2):2 * (i % 2) + 2, :].rearrange("p b n -> p (b n)")
                    for n, (b, c0, w) in enumerate(u["biases"]):
                        v(dve.scalar_tensor_tensor(s[:, c0:c0 + w], both[:, c0:c0 + w], scale, b, MUL, ADD),
                          softened if n + 1 == len(u["biases"]) and not u["plain"] else None)
                    for n, (c0, w) in enumerate(u["plain"]):
                        v(dve.tensor_scalar(s[:, c0:c0 + w], both[:, c0:c0 + w], scale, None, MUL),
                          softened if n + 1 == len(u["plain"]) else None)
                    v(dve.tensor_reduce(stat[:, 0:1], s[:, 0:u["cols"]], AXX, MAX))
                    if sinks:
                        v(dve.tensor_scalar(stat[:, 1:2], stat[:, 0:1], u["sink"], -1.0, MAX, MUL), taken_max)
                    else:
                        v(dve.tensor_scalar(stat[:, 1:2], stat[:, 0:1], -1.0, None, MUL), taken_max)
                if 1 <= i < N + 1:
                    u, stat = units[i - 1], st[:, (i - 1) % 4, :]
                    v.after(expd, i)
                    if sinks:
                        v(dve.tensor_tensor(stat[:, 2:3], stat[:, 2:3], stat[:, 4:5], ADD))
                    v(dve.reciprocal(stat[:, 3:4], stat[:, 2:3]))
                    s = S[(i - 1) % 3][:, 0:u["cols"]]
                    v(dve.tensor_scalar(s, s, stat[:, 3:4], None, MUL), normed)
                if i >= 5 and units[i - 5]["close"] is not None:
                    v.after(summed, i - 4)
                    units[i - 5]["close"](v, dve, ps[:, 6 + group[i - 5] % 2, :], taken)

        @block.scalar
        def _(act):
            a = Line(act, ch.S["scalar_step"])
            for i in range(N + 2):
                if i < N:
                    u, s, stat = units[i], S[i % 3][:, 0:units[i]["cols"]], st[:, i % 4, :]
                    a.after(taken_max, i + 1)
                    if sinks:
                        a(act.activation(stat[:, 4:5], u["sink"], ACT.Exp, bias=stat[:, 1:2]))
                    a(act.activation(s, s, ACT.Exp, bias=stat[:, 1:2], accum_out=stat[:, 2:3]), expd)
                if i >= 2:
                    u = units[i - 2]
                    a.after(turned, i - 1)
                    if i >= 4:
                        a.after(summed, i - 3)
                    both = ps[:, 4:6, :].rearrange("p b n -> p (b n)")
                    a(act.copy(pT[(i - 2) % 2][:, 0:u["cols"]], both[:, 0:u["cols"]]), copied)


def dsa_projection(ch):
    q, k, gate, iq, ik = ch.slot(0), ch.slot(1), ch.slot(4), ch.slot(5), ch.slot(6)
    v = ch.slot(3)
    iw = ch.sm[:, 120:152]
    tiles = []
    for b, dst in ((0, q), (1, k)):
        tiles += [(b, "T", j * P, ch.hT, T, copy_to(dst[:, j, :])) for j in range(4)]
    tiles += [(2, "N", s * P, ch.hT, T, copy_to(v[:, s, :])) for s in range(4)]
    tiles += [(3, "T", j * P, ch.hT, T, act_to(gate[:, j, :], ACT.Silu)) for j in range(4)]
    tiles += [(4, "T", j * P, ch.hT, T, copy_to(iq[:, j, :])) for j in range(4)]
    tiles += [(5, "T", 0, ch.hT, T, copy_to(ik[:, 0, :]))]
    tiles += [(5, ("N", P, P + 8), s * P, ch.hT, T,
               (lambda a, act, ps, sig, s=s: a(act.mul(iw[:, 8 * s:8 * s + 8], ps, 8 ** -0.5), sig), None))
              for s in range(4)]
    tiles, n = modulated(ch, tiles, 6, bands2(ch, 5, 10))
    project(ch, n, tiles)


def dsa_scores(ch):
    nc, ps = ch.nc, ch.ps
    iq, ik, score = ch.slot(5), ch.slot(6), ch.slot(8)
    iw = ch.sm[:, 120:152]
    rel = ch.slot(9)
    dots, relus, added = ch.counters("index_dots", "index_relus", "index_added")
    units = [(s, h) for s in range(1, 4) for h in range(8)]
    with nc.Block() as block:
        @block.tensor
        def _(pe):
            for i, (s, h) in enumerate(units):
                if i >= 4:
                    pe.wait_ge(relus.sem, relus.at(i - 3))
                rows, n = slice(64 * (h % 2), 64 * (h % 2) + 64), P * (s + 1)
                pe.matmul(ps[:, i % 4, 0:n], iq[rows, h // 2, s * P:(s + 1) * P], ik[rows, 0, 0:n],
                          start=True, stop=True).then_inc(dots.sem, 1)
                dots.total += 1

        @block.scalar
        def _(act):
            a = Line(act, ch.S["scalar_step"])
            for i, (s, h) in enumerate(units):
                a.after(dots, i + 1)
                if i >= 4:
                    a.after(added, i - 3)
                n = P * (s + 1)
                a(act.activation(rel[:, i % 4, 0:n], ps[:, i % 4, 0:n], ACT.Relu, scale=HD ** -0.5), relus)

        @block.vector
        def _(dve):
            v = Line(dve, ch.S["vector_step"])
            for i, (s, h) in enumerate(units):
                v.after(relus, i + 1)
                n = P * (s + 1)
                w = iw[:, 8 * s + h:8 * s + h + 1]
                if h == 0:
                    v(dve.tensor_scalar(score[:, s, 0:n], rel[:, i % 4, 0:n], w, None, MUL), added)
                else:
                    v(dve.scalar_tensor_tensor(score[:, s, 0:n], rel[:, i % 4, 0:n], w, score[:, s, 0:n], MUL, ADD),
                      added)


def dsa_select(ch):
    score, bias = ch.slot(8), ch.slot(7)
    best = ch.sm[:, 152:160]

    def run(v, dve):
        v(dve.tensor_copy(bias[:, 0, 0:P], ch.m("adm")))
        for s in range(1, 4):
            n = P * (s + 1)
            row = score[:, s, 0:n]
            v(dve.tensor_tensor(row[:, n - P:n], row[:, n - P:n], ch.m("adm"), ADD))
            for _ in range(P // 8):
                v(dve.max(best, row))
                v(dve.match_replace(row, best, row, -3e38))
            v(dve.tensor_scalar(bias[:, s, 0:n], row, -2e38, -BIG, ALU.is_gt, MUL))
    return run


def dsa_attention(ch):
    q, k, v, gate, bias, out = (ch.slot(0), ch.slot(1), ch.slot(3), ch.slot(4), ch.slot(7), ch.slot(11))
    units = []
    for h in range(8):
        rows, j = slice(64 * (h % 2), 64 * (h % 2) + 64), h // 2
        for s in range(4):
            n = P * (s + 1)

            def close(line, dve, ps, sig, j=j):
                line(dve.tensor_tensor(out[:, j, :], ps, gate[:, j, :], MUL), sig)
            units.append(dict(
                q=q[rows, j, s * P:(s + 1) * P], keys=[(k[rows, j, 0:n], 0)],
                biases=[(bias[:, s, 0:n], 0, n)], plain=[], cols=n,
                values=[v[:, t, h * HD:(h + 1) * HD] for t in range(s + 1)],
                rows=rows, col=s * P, close=close if h % 2 == 1 and s == 3 else None))
    attention(ch, units, HD ** -0.5)


def block1(ch):
    A = ch.A
    load_constants(ch)
    block1_modulation(ch)
    gain = [ch.sm[:, 24 + k:25 + k] for k in range(8)]
    shift = [ch.mod1[:, k:k + 1] for k in range(8)]
    normalise(ch, ch.xT, ch.hT, T, gain, shift)
    block1_rwkv_projection(ch)
    rwkv_prepare(ch)
    rwkv_transpose(ch)
    rwkv_within_chunks(ch)
    rwkv_chain(ch)
    rwkv_output(ch)
    dsa_projection(ch)
    head_norm(ch, [(ch.slot(i)[:, j, :], ch.v(g)) for i, g in ((0, "q_gain"), (1, "k_gain")) for j in range(4)],
              "blk64", HD)
    dsa_scores(ch)
    ga = ch.slot(5, 2)
    project(ch, 2, [(b, "T", j * P, ch.hT, T, act_to(ga[:, 4 * b + j, :], ACT.Sigmoid)) for b in range(2)
                    for j in range(4)], vector_after=dsa_select(ch))
    dsa_attention(ch)
    gb, merged, y, yb = ch.slot(0, 2), ch.slot(7, 2), ch.slot(2), ch.slot(11)
    tmp = ch.slot(9)
    tiles = [(b, "T", j * P, ch.hT, T, act_to(gb[:, 4 * b + j, :], ACT.Sigmoid)) for b in range(2) for j in range(4)]
    for b in range(2):
        for j in range(4):
            def part(v, dve, ps, sig, n=4 * b + j):
                v(dve.tensor_tensor(merged[:, n, :], ps, ga[:, n, :], MUL), sig)
            tiles.append((2 + b, "T", j * P, y, T, (None, part)))
    for b in range(2):
        for j in range(4):
            def part(v, dve, ps, sig, n=4 * b + j):
                v(dve.tensor_tensor(tmp[:, n % 4, :], ps, gb[:, n, :], MUL), sig)
                v(dve.tensor_tensor(merged[:, n, :], merged[:, n, :], tmp[:, n % 4, :], ADD))
            tiles.append((4 + b, "T", j * P, yb, T, (None, part)))
    tiles, n = modulated(ch, tiles, 6, bands2(ch, 10, 12))
    project(ch, n, tiles)
    tiles = []
    for b in range(2):
        for j in range(4):
            def part(v, dve, ps, sig, n=4 * b + j):
                v(dve.scalar_tensor_tensor(ch.xT[:, n, :], ps, ch.mod1[:, 16 + n:17 + n], ch.xT[:, n, :], MUL, ADD), sig)
            tiles.append((b, "T", j * P, merged, T, (None, part)))
    project(ch, 2, tiles)


def block1_plan(A):
    w, m = A["w_in"], blocks(A["w_mod_2"], 0, 6144)
    return (blocks(A["w_ada"], 0, 3072)
            + weave(blocks(w, 0, 1536) + blocks(w, 1536, 1664) + blocks(w, 1664, 2176), m[0:5])
            + weave(blocks(w, 2176, 4736) + joined(w, [(4736, 4800), (4736, 4800), (4800, 4808)]), m[5:10])
            + blocks(w, 4808, 5832)
            + weave(blocks(w, 5832, 6856) + blocks(A["w_a_out"], 0, 1024) + blocks(A["w_b_out"], 0, 1024), m[10:12])
            + blocks(A["w_o"], 0, 1024))



def block2_gains(ch):
    with ch.nc.Block() as block:
        @block.vector
        def _(dve):
            v = Line(dve, ch.S["vector_step"])
            for o, j, c, g in ((24, 8, 0, "norm_mix_g_2"), (32, 8, 1, "norm_mix_g_2"), (40, 32, 0, "norm_ffn_g_2")):
                v(dve.scalar_tensor_tensor(ch.sm[:, o:o + 8], ch.mod2[:, j:j + 8, c], 1.0, ch.v(g, 0, 8), ADD, MUL))


def conv_taps(ch, vpad, y):
    def run(v, dve):
        for j in range(4):
            for w in range(31):
                src, tap = vpad[:, j, w:w + T], ch.v("conv_w_2", 4 * w + j)
                if w == 0:
                    v(dve.tensor_scalar(y[:, j, :], src, tap, ch.v("conv_b_2", j), MUL, ADD))
                else:
                    v(dve.scalar_tensor_tensor(y[:, j, :], src, tap, y[:, j, :], MUL, ADD))
    return run


def conv_norm(ch, y):
    nc, ps = ch.nc, ch.ps
    sq, mean, rstd = ch.slot(5), ch.slot(9)[:, 0, :], ch.slot(9)[:, 1, :]
    sums, centred, squares, root = ch.counters("cn_sums", "cn_centred", "cn_squares", "cn_root")
    with nc.Block() as block:
        @block.tensor
        def _(pe):
            for j in range(4):
                ins = pe.matmul(ps[:, 0, :], ch.m("ones"), y[:, j, :], start=j == 0, stop=j == 3)
            ins.then_inc(sums.sem, 1)
            for j in range(4):
                pe.wait_ge(squares.sem, squares.at(j + 1))
                ins = pe.matmul(ps[:, 1, :], ch.m("ones"), sq[:, j, :], start=j == 0, stop=j == 3)
            ins.then_inc(sums.sem, 1)
            sums.total += 2

        @block.vector
        def _(dve):
            v = Line(dve, ch.S["vector_step"])
            v.after(sums, 1)
            v(dve.tensor_scalar(mean, ps[:, 0, :], 1.0 / 512, None, MUL))
            for j in range(4):
                v(dve.tensor_tensor(y[:, j, :], y[:, j, :], mean, SUB), centred)
            v.after(root, 1)
            v(dve.reciprocal(rstd, rstd))
            for j in range(4):
                v(dve.tensor_tensor(sq[:, j, :], y[:, j, :], rstd, MUL), centred)

        @block.scalar
        def _(act):
            a = Line(act, ch.S["scalar_step"])
            for j in range(4):
                a.after(centred, j + 1)
                a(act.square(sq[:, j, :], y[:, j, :]), squares)
            a.after(sums, 2)
            a(act.activation(rstd, ps[:, 1, :], ACT.Sqrt, bias=ch.eps[:, 0:1], scale=1.0 / 512), root)
            for j in range(4):
                a.after(centred, 5 + j)
                a(act.activation(y[:, j, :], sq[:, j, :], ACT.Silu, bias=ch.v("conv_ln_b_2", j),
                                 scale=ch.v("conv_ln_g_2", j)))


def neighbourhood_attention(ch):
    q, k, v, out = ch.slot(0), ch.slot(1, 2), ch.slot(3, 2), ch.slot(8)
    k = k.rearrange("p a t -> p (a t)")[:, 0:3072].rearrange("p (j t) -> p j t", t=768)
    v = v[:, 0:6, :]
    flat = ch.slot(11).rearrange("p a t -> p (a t)")
    tab = [flat[:, i * 896:(i + 1) * 896] for i in range(2)]
    loaded = ch.counter("bias_loaded")

    def load(sp, softened):
        for h in range(8):
            if h >= 2:
                sp.wait_ge(softened.sem, softened.at(4 * (h - 1)))
            sp.dma_start(tab[h % 2], ch.A["rpb"][:, h * 896:(h + 1) * 896]).then_inc(loaded.sem, 16)
            loaded.total += 16
            sp.wait_ge(loaded.sem, loaded.total)

    units = []
    for h in range(8):
        rows, j = slice(64 * (h % 2), 64 * (h % 2) + 64), h // 2

        def prepare(line, dve, h=h):
            line.after(loaded, 16 * (h + 1))
            t = tab[h % 2].rearrange("p (r c) -> p r c", c=64)
            line(dve.tensor_tensor(t, t, ch.m("win")[:, 0:64].unsqueeze(1).to_broadcast([P, 14, 64]), ADD))
        for s in range(4):
            def close(line, dve, ps, sig, j=j):
                line(dve.tensor_copy(out[:, j, :], ps), sig)
            units.append(dict(
                q=q[rows, j, s * P:(s + 1) * P], keys=[(k[rows, j, 0:512], 0), (k[rows, j, 512:768], 512)],
                biases=[(tab[h % 2][:, (6 - 2 * s) * 64:(6 - 2 * s) * 64 + 512], 0, 512)], plain=[(512, 256)],
                cols=768, values=[v[:, t, h * HD:(h + 1) * HD] for t in range(6)],
                rows=rows, col=s * P, close=close if h % 2 == 1 and s == 3 else None,
                prepare=prepare if s == 0 else None))
    attention(ch, units, HD ** -0.5, sync_body=load)


def block2_mixer(ch):
    nc = ch.nc
    ctxT, hcT = (ch.W[:, i, :].rearrange("p (k t) -> p k t", t=L) for i in (2, 11))
    aux = ch.counter("aux_loaded")
    with nc.Block() as block:
        @block.sync
        def _(sp):
            sp.dma_start(ctxT, ch.A["ctxT"].rearrange("(k p) t -> p k t", p=P)).then_inc(aux.sem, 16)
            aux.total += 16
            sp.wait_ge(aux.sem, aux.total)
    normalise(ch, ctxT, hcT, L, [ch.sm[:, 32 + i:33 + i] for i in range(8)], [ch.mod2[:, i, 1:2] for i in range(8)])
    normalise(ch, ch.xT, ch.hT, T, [ch.sm[:, 24 + i:25 + i] for i in range(8)], [ch.mod2[:, i, 0:1] for i in range(8)])
    q, a_, y = ch.slot(0), ch.slot(8), ch.slot(7)
    k = ch.slot(1, 2).rearrange("p a t -> p (a t)")[:, 0:3072].rearrange("p (j t) -> p j t", t=768)
    v = ch.slot(3, 2)
    vpad = ch.slot(5, 2).rearrange("p a t -> p (a t)")[:, 0:4 * 542].rearrange("p (j t) -> p j t", t=542)
    sig_g = ch.slot(9)
    tiles = [(0, "T", j * P, ch.hT, T, copy_to(a_[:, j, :])) for j in range(4)]
    with nc.Block() as block:
        @block.vector
        def _(dve):
            Line(dve, ch.S["vector_step"])(dve.memset(vpad, 0.0))
    for j in range(4):
        def part_a(a, act, ps, sig, j=j):
            a(act.activation(sig_g[:, j, :], ps, ACT.Sigmoid), sig)

        def part_v(v_, dve, ps, sig, j=j):
            v_(dve.tensor_tensor(vpad[:, j, 15:15 + T], a_[:, j, :], sig_g[:, j, :], MUL), sig)
        tiles.append((1, "T", j * P, ch.hT, T, (part_a, part_v)))
    tiles += [(2, "T", j * P, ch.hT, T, copy_to(q[:, j, :])) for j in range(4)]
    tiles += [(3, "T", j * P, ch.hT, T, copy_to(k[:, j, 0:T])) for j in range(4)]
    tiles += [(3, "T", j * P, hcT, L, copy_to(k[:, j, T:T + L])) for j in range(4)]
    tiles += [(4, "N", s * P, ch.hT, T, copy_to(v[:, s, :])) for s in range(4)]
    tiles += [(4, "N", s * P, hcT, L, copy_to(v[:, 4 + s, :])) for s in range(2)]
    project(ch, 5, tiles, vector_after=conv_taps(ch, vpad, y))
    conv_norm(ch, y)
    neighbourhood_attention(ch)
    tiles = []
    for b in range(2):
        for j in range(4):
            def part(v_, dve, ps, sig, n=4 * b + j):
                v_(dve.scalar_tensor_tensor(ch.xT[:, n, :], ps, ch.mod2[:, 16 + n, 0:1], ch.xT[:, n, :], MUL, ADD), sig)
            tiles.append((b, "T", j * P, ch.slot(7, 2), T, (None, part)))
    project(ch, 2, tiles)


def route(ch):
    nc, ps = ch.nc, ch.ps
    wr = ch.slot(2).rearrange("p a t -> p (a t)")[:, 0:128].rearrange("p (k e) -> p k e", e=E_)
    hN = ch.slot(0, 2).rearrange("p a t -> p (a t)").rearrange("p (s d) -> p s d", d=D)
    aff, place = (ch.slot(3)[:, i, 0:64].rearrange("p (s e) -> p s e", e=E_) for i in (0, 1))
    row, sel, pos = (ch.slot(4)[0:E_, i, :] for i in (0, 1, 2))
    best = ch.sm[0:E_, 152:160]
    st = ch.sm[:, 96:104].rearrange("p (i s) -> p i s", s=4)
    aux, turned, copied, steps, expd = ch.counters("aux_loaded", "route_turned", "route_copied", "route_steps",
                                                  "route_exp")
    with nc.Block() as block:
        @block.sync
        def _(sp):
            sp.dma_start(wr, ch.A["w_router_2"].rearrange("(k p) e -> p k e", p=P)).then_inc(aux.sem, 16)
            aux.total += 16

        @block.tensor
        def _(pe):
            pe.wait_ge(aux.sem, aux.at(16))
            for s in range(4):
                for k in range(KD):
                    ins = pe.matmul(ps[:, 0, s * E_:(s + 1) * E_], ch.hT[:, k, s * P:(s + 1) * P], wr[:, k, :],
                                    start=k == 0, stop=k == KD - 1)
            ins.then_inc(turned.sem, 1)
            for n in range(8):
                if n >= 4:
                    pe.wait_ge(copied.sem, copied.at(n - 3))
                for j in range(4):
                    k, s = 4 * (n % 2) + j, n // 2
                    ins = pe.transpose(ps[:, 1 + n % 4, j * P:(j + 1) * P], ch.hT[:, k, s * P:(s + 1) * P], ch.m("ident"))
                ins.then_inc(turned.sem, 1)
            pe.wait_ge(steps.sem, steps.at(1))
            for s in range(4):
                ins = pe.transpose(ps[0:E_, 5, s * P:(s + 1) * P], aff[:, s, :], ch.m("ident"))
            ins.then_inc(turned.sem, 1)
            pe.wait_ge(steps.sem, steps.at(2))
            for s in range(4):
                ins = pe.transpose(ps[:, 6, s * E_:(s + 1) * E_], pos[:, s * P:(s + 1) * P], ch.m("ident")[0:E_, 0:E_])
            ins.then_inc(turned.sem, 1)
            turned.total += 11

        @block.scalar
        def _(act):
            a = Line(act, ch.S["scalar_step"])
            a.after(expd, 1)
            a(act.activation(aff, aff, ACT.Exp), expd)
            for n in range(8):
                a.after(turned, n + 2)
                a(act.copy(hN[:, n // 2, (n % 2) * 512:(n % 2 + 1) * 512], ps[:, 1 + n % 4, :]), copied)

        @block.vector
        def _(dve):
            v = Line(dve, ch.S["vector_step"])
            v.after(turned, 1)
            logits = ps[:, 0, 0:64].rearrange("p (s e) -> p s e", e=E_)
            wide = st[:, 0, :].unsqueeze(2).to_broadcast([P, 4, E_])
            v(dve.tensor_reduce(st[:, 0, :], logits, AXX, MAX))
            v(dve.tensor_tensor(aff, logits, wide, SUB), expd)
            v.after(expd, 2)
            v(dve.tensor_reduce(st[:, 0, :], aff, AXX, ADD))
            v(dve.reciprocal(st[:, 0, :], st[:, 0, :]))
            v(dve.tensor_tensor(aff, aff, wide, MUL), steps)
            v.after(turned, 10)
            v(dve.tensor_copy(row, ps[0:E_, 5, :]))
            for _ in range(CAP // 8):
                v(dve.max(best, row))
                v(dve.match_replace(row, best, row, -1.0))
            v(dve.tensor_scalar(sel, row, 0.0, None, ALU.is_lt))
            v(dve.tensor_tensor_scan(pos, ch.eps[0:E_, 3:4].to_broadcast([E_, T]), sel, 0.0, MUL, ADD))
            v(dve.tensor_tensor(pos, pos, sel, MUL), steps)
            v.after(turned, 11)
            v(dve.tensor_copy(place, ps[:, 6, 0:64].rearrange("p (s e) -> p s e", e=E_)))


def experts(ch):
    nc, ps = ch.nc, ch.ps
    hN = ch.slot(0, 2).rearrange("p a t -> p (a t)").rearrange("p (s d) -> p s d", d=D)
    aff, place = (ch.slot(3)[:, i, 0:64].rearrange("p (s e) -> p s e", e=E_) for i in (0, 1))
    oh = ch.slot(4)[:, 0, 0:256].rearrange("p (s c) -> p s c", c=CAP)
    pw = ch.slot(4)[:, 1, :].rearrange("p (s c) -> p s c", c=P)
    pwT = ch.slot(4)[:, 2, :], ch.slot(4)[:, 3, :]
    xs = ch.slot(5)[:, 0, :].rearrange("p (k c) -> p k c", c=CAP)
    sil = ch.slot(6)[:, 0:2, :]
    hid = ch.slot(6)[:, 2:4, :]
    hidT = ch.slot(7)[:, 0:2, :].rearrange("p a (i q c) -> p a i q c", q=2, c=CAP)
    y = ch.slot(7)[:, 2, :]
    iota = ch.m("iota")
    first = ch.used
    (oh_ready, gathered, xs_ready, gate_up, silus, hid_ready, turned, hidT_ready, down, y_ready,
     pw_ready, pw_turned, pwT_ready, scattered, added) = ch.counters(
        "onehot_ready", "gathered", "xs_ready", "gate_up_done", "silus", "hidden_ready", "hidden_turned",
        "hiddenT_ready", "down_done", "y_ready", "scatter_ready", "scatter_turned", "scatterT_ready", "scattered",
        "residual_added")
    for e in range(E_):
        for i in range(8):
            ch.free_at[first + 12 * e + i] = (gate_up.sem, gate_up.at(4 * e + i // 2 + 1))
        for i in range(4):
            ch.free_at[first + 12 * e + 8 + i] = (down.sem, down.at(4 * e + i + 1))

    with nc.Block() as block:
        @block.sync
        def _(sp):
            ch.stream(sp, first + 12 * E_ + RING)

        @block.tensor
        def _(pe):
            def gather(e):
                pe.wait_ge(oh_ready.sem, oh_ready.at(e + 1))
                if e > 0:
                    pe.wait_ge(xs_ready.sem, xs_ready.at(e))
                for k in range(KD):
                    for s in range(4):
                        ins = pe.matmul(ps[:, 0, k * CAP:(k + 1) * CAP], hN[:, s, k * P:(k + 1) * P], oh[:, s, :],
                                        start=s == 0, stop=s == 3)
                ins.then_inc(gathered.sem, 1)
                gathered.total += 1
                pe.wait_ge(pw_ready.sem, pw_ready.at(e + 1))
                if e > 1:
                    pe.wait_ge(added.sem, added.at(8 * (e - 1)))
                elif e == 1:
                    pe.wait_ge(pwT_ready.sem, pwT_ready.at(1))
                for s in range(4):
                    ins = pe.transpose(ps[:, 5, s * P:(s + 1) * P], pw[:, s, :], ch.m("ident"))
                ins.then_inc(pw_turned.sem, 1)
                pw_turned.total += 1

            def gate_and_up(e, n):
                b0 = first + 12 * e + 2 * n
                w = [ch.block_view(b0 + q) for q in range(2)]
                ch.block_wait(pe, b0)
                ch.block_wait(pe, b0 + 1)
                if e > 0:
                    pe.wait_ge(hid_ready.sem, hid_ready.at(2 * e - 1 + n // 2))
                for k in range(KD):
                    for q in range(2):
                        ins = pe.matmul(ps[64 * q:64 * q + 64, 1 + n, :], xs[:, k, :], w[q][:, k, :],
                                        start=k == 0, stop=k == KD - 1)
                ins.then_inc(gate_up.sem, 1)
                gate_up.total += 1

            def scatter(e):
                pe.wait_ge(y_ready.sem, y_ready.at(e + 1))
                for n in range(8):
                    q, bank = n // 4, 5 + n % 2
                    if n < 2:
                        pe.wait_ge(hidT_ready.sem, hidT_ready.at(2 * e + 2))
                    else:
                        pe.wait_ge(added.sem, added.at(8 * e + n - 1))
                    rows = slice(64 * q, 64 * q + 64)
                    pe.matmul(ps[:, bank, :], y[rows, (n % 4) * P:(n % 4 + 1) * P], pwT[e % 2][rows, :], start=True,
                              stop=True).then_inc(scattered.sem, 1)
                    scattered.total += 1

            gather(0)
            for e in range(E_):
                pe.wait_ge(xs_ready.sem, xs_ready.at(e + 1))
                gate_and_up(e, 0)
                gate_and_up(e, 1)
                if e > 0:
                    scatter(e - 1)
                gate_and_up(e, 2)
                gate_and_up(e, 3)
                if e > 0:
                    pe.wait_ge(added.sem, added.at(8 * e))
                pe.wait_ge(hid_ready.sem, hid_ready.at(2 * e + 1))
                for i in range(4):
                    ins = pe.transpose(ps[:, 6, i * P:(i + 1) * P], hid[:, 0, i * P:(i + 1) * P], ch.m("ident"))
                ins.then_inc(turned.sem, 1)
                if e + 1 < E_:
                    gather(e + 1)
                pe.wait_ge(hid_ready.sem, hid_ready.at(2 * e + 2))
                pe.wait_ge(pwT_ready.sem, pwT_ready.at(min(e + 2, E_)))
                for i in range(4):
                    ins = pe.transpose(ps[:, 5, i * P:(i + 1) * P], hid[:, 1, i * P:(i + 1) * P], ch.m("ident"))
                ins.then_inc(turned.sem, 1)
                turned.total += 2
                if e > 0:
                    pe.wait_ge(y_ready.sem, y_ready.at(e))
                for i in range(4):
                    w = ch.block_view(first + 12 * e + 8 + i)
                    ch.block_wait(pe, first + 12 * e + 8 + i)
                    if i % 2 == 0:
                        pe.wait_ge(hidT_ready.sem, hidT_ready.at(2 * e + 1 + i // 2))
                    for t in range(4):
                        f = 4 * i + t
                        for q in range(2):
                            ins = pe.matmul(ps[64 * q:64 * q + 64, 7, :], hidT[:, f // 8, f % 4, (f // 4) % 2, :],
                                            w[:, t, q * 512:(q + 1) * 512], start=f == 0, stop=f == 15)
                    ins.then_inc(down.sem, 1)
                    down.total += 1
            scatter(E_ - 1)

        @block.scalar
        def _(act):
            a = Line(act, ch.S["scalar_step"])

            def gathered_parts(e):
                a.after(gathered, e + 1)
                a(act.copy(xs, ps[:, 0, :].rearrange("p (k c) -> p k c", c=CAP)), xs_ready)
                a.after(pw_turned, e + 1)
                a(act.copy(pwT[e % 2], ps[:, 5, :]), pwT_ready)

            gathered_parts(0)
            for e in range(E_):
                for p in range(2):
                    a.after(gate_up, 4 * e + 2 * p + 1)
                    if e > 0:
                        a.after(hid_ready, 2 * e - 1 + p)
                    a(act.activation(sil[:, p, :], ps[:, 1 + 2 * p, :], ACT.Silu), silus)
                a.after(turned, 2 * e + 1)
                a(act.copy(hidT[:, 0], ps[:, 6, :].rearrange("p (i q c) -> p i q c", q=2, c=CAP)), hidT_ready)
                if e + 1 < E_:
                    gathered_parts(e + 1)
                a.after(turned, 2 * e + 2)
                a(act.copy(hidT[:, 1], ps[:, 5, :].rearrange("p (i q c) -> p i q c", q=2, c=CAP)), hidT_ready)

        @block.vector
        def _(dve):
            v = Line(dve, ch.S["vector_step"])

            def selectors(e):
                if e > 0:
                    v.after(pw_turned, e)
                for s in range(4):
                    v(dve.tensor_scalar(oh[:, s, :], iota[:, 0:CAP], place[:, s, e:e + 1], None, ALU.is_equal),
                      oh_ready if s == 3 else None)
                for s in range(4):
                    v(dve.tensor_scalar(pw[:, s, :], iota, place[:, s, e:e + 1], aff[:, s, e:e + 1], ALU.is_equal, MUL),
                      pw_ready if s == 3 else None)

            def hidden(e, p):
                v.after(gate_up, 4 * e + 2 * p + 2)
                v.after(silus, 2 * e + p + 1)
                if e > 0:
                    v.after(turned, 2 * e - 1 + p)
                v(dve.tensor_tensor(hid[:, p, :], sil[:, p, :], ps[:, 2 + 2 * p, :], MUL), hid_ready)

            def add(e):
                for n in range(8):
                    v.after(scattered, 8 * e + n + 1)
                    v(dve.scalar_tensor_tensor(ch.xT[:, n, :], ps[:, 5 + n % 2, :], ch.mod2[:, 40 + n, 0:1],
                                               ch.xT[:, n, :], MUL, ADD), added)

            selectors(0)
            for e in range(E_):
                hidden(e, 0)
                if e > 0:
                    add(e - 1)
                if e + 1 < E_:
                    selectors(e + 1)
                hidden(e, 1)
                v.after(down, 4 * e + 4)
                v(dve.tensor_copy(y, ps[:, 7, :]), y_ready)
            add(E_ - 1)
    ch.used = first + 12 * E_


def block2(ch):
    block2_gains(ch)
    block2_mixer(ch)
    normalise(ch, ch.xT, ch.hT, T, [ch.sm[:, 40 + i:41 + i] for i in range(8)], [ch.mod2[:, 24 + i, 0:1] for i in range(8)])
    route(ch)
    experts(ch)
    normalise(ch, ch.xT, ch.xT, T, [ch.v("norm_final_g_2", i) for i in range(8)], None)


def block2_plan(A):
    out = blocks(A["w_in_2"], 0, 2560) + blocks(A["w_out_2"], 0, 1024)
    for e in range(E_):
        g, u = blocks(A["w_gate_2"][e], 0, FE), blocks(A["w_up_2"][e], 0, FE)
        out += g[0:2] + u[0:2] + g[2:4] + u[2:4]
        for i in range(4):
            w = A["w_down_2"][e, i * 512:(i + 1) * 512, :].rearrange("(k p) c -> p k c", p=P)
            out.append(([(w, 0, D)], 4, D))
    return out



def even_gating(ch):
    nc, ps = ch.nc, ch.ps
    u, z = ch.slot(0, 2), ch.slot(4, 2)
    v = ch.slot(2, 2).rearrange("p a t -> p (a t)").rearrange("p (s d) -> p s d", d=D)
    c = ch.slot(6, 2).rearrange("p a t -> p (a t)")
    gain, shift, bs, ws = c[:, 0:D], c[:, D:2 * D], c[:, 2 * D:2 * D + 512], c[:, 2 * D + 512:3 * D]
    tmp = ch.slot(8)
    stats = ch.sm[:, 0:48].rearrange("p (s i c) -> p s i c", s=4, c=6)
    mv = ch.sm[:, 48:56].rearrange("p (s c) -> p s c", c=2)
    loaded, var_ready, root, normed, mixed = ch.counters("aux_loaded", "var_ready", "ln_root", "ln_normed", "mixed")
    with nc.Block() as block:
        @block.sync
        def _(sp):
            sp.dma_start(c[:, 0:3 * D], ch.A["gmlp"]).then_inc(loaded.sem, 16)
            loaded.total += 16

        @block.vector
        def _(dve):
            line = Line(dve, ch.S["vector_step"])
            for s in range(4):
                for i in range(2):
                    line(dve.bn_stats(stats[:, s, i, :], v[:, s, i * 512:(i + 1) * 512]))
                line(dve.bn_aggr(mv[:, s, :], stats[:, s].rearrange("p i c -> p (i c)")),
                     var_ready if s == 3 else None)
            line.after(root, 1)
            line(dve.reciprocal(mv[:, :, 1], mv[:, :, 1]))
            line.after(loaded, 16)
            for s in range(4):
                line(dve.tensor_scalar(v[:, s, :], v[:, s, :], mv[:, s, 0:1], mv[:, s, 1:2], SUB, MUL))
                line(dve.tensor_tensor(v[:, s, :], v[:, s, :], gain, MUL))
                line(dve.tensor_tensor(v[:, s, :], v[:, s, :], shift, ADD), normed)
            for k in range(8):
                g = k // 2
                b = bs[:, g * P:(g + 1) * P].unsqueeze(1).to_broadcast([P, 4, P])
                line.after(mixed, k + 1)
                t = tmp[:, k % 4, :]
                line(dve.tensor_tensor(t.rearrange("p (s t) -> p s t", t=P),
                                       ps[:, k, :].rearrange("p (s t) -> p s t", t=P), b, ADD))
                line(dve.tensor_tensor(t, t, u[:, k, :], MUL))
                line(dve.tensor_tensor(u[:, k, :], t, z[:, k, :], MUL))

        @block.scalar
        def _(act):
            a = Line(act, ch.S["scalar_step"])
            a.after(var_ready, 1)
            a(act.activation(mv[:, :, 1], mv[:, :, 1], ACT.Sqrt, bias=ch.eps[:, 0:1]), root)

        @block.tensor
        def _(pe):
            pe.wait_ge(loaded.sem, loaded.at(16))
            pe.wait_ge(normed.sem, normed.at(4))
            for k in range(8):
                g = k // 2
                for s in range(4):
                    ins = pe.matmul(ps[:, k, s * P:(s + 1) * P], v[:, s, k * P:(k + 1) * P], ws[:, g * P:(g + 1) * P],
                                    start=True, stop=True)
                ins.then_inc(mixed.sem, 1)
                mixed.total += 1


def window_attention(ch):
    q, kv, gate = ch.slot(4, 2), ch.slot(6), ch.slot(2, 2)
    k, v = kv[:, 0:2, :], kv[:, 2:4, :].rearrange("p a t -> p (a t)").rearrange("p (s c) -> p s c", c=256)
    band = ch.slot(7).rearrange("p a t -> p (a t)")
    dist, mask = band[:, 0:384], band[:, 384:768]
    bias = [band[:, 768 + i * 384:768 + (i + 1) * 384] for i in range(2)]
    loaded = ch.counter("bias_loaded")

    def load(sp, softened):
        sp.dma_start(band[:, 0:768], ch.A["band"]).then_inc(loaded.sem, 16)
        loaded.total += 16

    units = []
    for h in range(8):
        g = h // 4

        def prepare(line, dve, h=h):
            if h == 0:
                line.after(loaded, 16)
            line(dve.scalar_tensor_tensor(bias[h % 2], dist, -2.0 ** -(h + 1), mask, MUL, ADD))
        for s in range(4):
            t0, t1 = max(s - 1, 0), min(s + 2, 4)
            n, c0 = (t1 - t0) * P, 128 if s == 0 else 0

            def close(line, dve, psum, sig, h=h):
                line(dve.tensor_tensor(gate[:, h, :], psum, gate[:, h, :], MUL), sig)
            units.append(dict(
                q=q[:, h, s * P:(s + 1) * P], keys=[(k[:, g, t0 * P:t1 * P], 0)],
                biases=[(bias[h % 2][:, c0:c0 + n], 0, n)], plain=[], cols=n,
                values=[v[:, t, g * P:(g + 1) * P] for t in range(t0, t1)], rows=slice(0, P), col=s * P,
                close=close if s == 3 else None, prepare=prepare if s == 0 else None, sink=ch.v("attn_sink_3", h)))
    attention(ch, units, P ** -0.5, sinks=True, sync_body=load)


def add_to_stream(ch, source, per, nblocks):
    tiles = []
    for b in range(nblocks):
        for j in range(per):
            def part(v, dve, ps, sig, n=per * b + j):
                v(dve.tensor_tensor(ch.xT[:, n, :], ps, ch.xT[:, n, :], ADD), sig)
            tiles.append((b, "T", j * P, source, T, (None, part)))
    project(ch, nblocks, tiles)


def even_layer(ch):
    normalise(ch, ch.xT, ch.hT, T, [ch.v("norm_g_even_3", i) for i in range(8)], None)
    u, z = ch.slot(0, 2), ch.slot(4, 2)
    v = ch.slot(2, 2).rearrange("p a t -> p (a t)").rearrange("p (s d) -> p s d", d=D)
    tiles = []
    for b in range(2):
        tiles += [(b, "T", j * P, ch.hT, T, copy_to(u[:, 4 * b + j, :])) for j in range(4)]
    for b in range(2):
        tiles += [(2 + b, "N", s * P, ch.hT, T, copy_to(v[:, s, b * 512:(b + 1) * 512])) for s in range(4)]
    for b in range(2):
        tiles += [(4 + b, "T", j * P, ch.hT, T, act_to(z[:, 4 * b + j, :], ACT.Silu)) for j in range(4)]
    project(ch, 6, tiles)
    even_gating(ch)
    q, kv, gate = ch.slot(4, 2), ch.slot(6), ch.slot(2, 2)
    vb = kv[:, 2:4, :].rearrange("p a t -> p (a t)").rearrange("p (s c) -> p s c", c=256)
    tiles = []
    for b in range(2):
        tiles += [(b, "T", j * P, ch.hT, T, copy_to(q[:, 4 * b + j, :])) for j in range(4)]
    tiles += [(2, "T", j * P, ch.hT, T, copy_to(kv[:, j, :])) for j in range(2)]
    tiles += [(2, ("N", 256, 512), s * P, ch.hT, T, copy_to(vb[:, s, :])) for s in range(4)]
    for b in range(2):
        tiles += [(3 + b, "T", j * P, ch.hT, T, act_to(gate[:, 4 * b + j, :], ACT.Silu)) for j in range(4)]
    project(ch, 5, tiles)
    window_attention(ch)
    add_to_stream(ch, ch.slot(0, 4), 2, 4)



def odd_bounds(ch):
    with ch.nc.Block() as block:
        @block.vector
        def _(dve):
            v = Line(dve, ch.S["vector_step"])
            for i, n in enumerate(("hgrn_gamma_fwd_3", "hgrn_gamma_bwd_3")):
                v(dve.tensor_tensor(ch.sm[:, 16 * i:16 * i + 16], ch.v(n, 16, 16), ch.v(n, 0, 16), SUB))
    with ch.nc.Block() as block:
        @block.scalar
        def _(act):
            a = Line(act, ch.S["scalar_step"])
            a(act.activation(ch.sm[:, 32:64], ch.sm[:, 0:32], ACT.Sigmoid, scale=-1.0))
            a(act.activation(ch.sm[:, 0:32], ch.sm[:, 0:32], ACT.Sigmoid))


def odd_project(ch, G):
    Q, F, B, I, Z = [ch.slot(i) for i in range(5)]
    qd, kd, ed = (ch.slot(5), ch.slot(8)), (ch.slot(6), ch.slot(9)), (ch.slot(7), ch.slot(10))
    keep = ch.slot(11)[:, 0, :]
    by_dve = ch.S["tile_vector_done"]
    tiles = []
    for d, dst in ((0, F), (1, B)):
        for j in range(4):
            lb = ch.sm[:, 16 * d + 4 * G + j:16 * d + 4 * G + j + 1]
            om = ch.sm[:, 32 + 16 * d + 4 * G + j:33 + 16 * d + 4 * G + j]

            def part_a(a, act, ps, sig, o=dst[:, j, :]):
                a(act.activation(o, ps, ACT.Sigmoid), sig)

            def part_v(v, dve, ps, sig, o=dst[:, j, :], k=kd[d][:, j, :], lb=lb, om=om):
                v(dve.tensor_scalar(o, o, om, lb, MUL, ADD))
                v(dve.tensor_scalar(k, o, -1.0, 1.0, MUL, ADD), sig)
            tiles.append((d, "T", j * P, ch.hT, T, (part_a, part_v)))

    def logs(a, act, ps, sig):
        a.after(by_dve, 8)
        a(act.activation(F, F, ACT.Ln))
        a(act.activation(B, B, ACT.Ln))
        a(act.activation(Q[:, 0, :], ps, ACT.Silu), sig)

    def scans(v, dve, ps, sig):
        v(dve.memset(keep, 1.0))
        v(dve.memset(keep.rearrange("p (c t) -> p c t", t=64)[:, :, 0:1], 0.0))
        for j in range(4):
            v(dve.tensor_tensor_scan(F[:, j, :], keep, F[:, j, :], 0.0, MUL, ADD))
        for j in range(4):
            v(dve.tensor_tensor_scan(B[:, j, ::-1], keep, B[:, j, ::-1], 0.0, MUL, ADD), sig if j == 3 else None)

    def exps(a, act, ps, sig):
        a.after(by_dve, 9)
        for d, x in ((0, F), (1, B)):
            a(act.activation(qd[d], x, ACT.Exp))
            a(act.activation(ed[d], x, ACT.Exp, scale=-1.0))
        a(act.copy(I[:, 0, :], ps), sig)

    def operands(v, dve, ps, sig):
        for d, last in ((0, 63), (1, 0)):
            end = ch.sm[:, 64 + 32 * d:96 + 32 * d]
            v(dve.tensor_copy(end.rearrange("p (j c) -> p j c", c=8),
                              qd[d].rearrange("p j (c t) -> p j c t", t=64)[:, :, :, last]))
            v(dve.tensor_tensor(qd[d], qd[d], Q, MUL))
            v(dve.tensor_tensor(kd[d], kd[d], ed[d], MUL))
            v(dve.tensor_tensor(ed[d].rearrange("p j (c t) -> p (j c) t", t=64),
                                kd[d].rearrange("p j (c t) -> p (j c) t", t=64),
                                end.unsqueeze(2).to_broadcast([P, 32, 64]), MUL), sig if d == 1 else None)

    tiles.append((2, "T", 0, ch.hT, T, (logs, scans)))
    tiles += [(2, "T", j * P, ch.hT, T, act_to(Q[:, j, :], ACT.Silu)) for j in range(1, 4)]
    tiles.append((3, "N", 0, ch.hT, T, (exps, operands)))
    tiles += [(3, "N", s * P, ch.hT, T, copy_to(I[:, s, :])) for s in range(1, 4)]
    tiles += [(4, "T", j * P, ch.hT, T, act_to(Z[:, j, :], ACT.Silu)) for j in range(4)]
    project(ch, 5, tiles)


def odd_recurrence(ch, G):
    nc, ps = ch.nc, ch.ps
    I, Z = ch.slot(3), ch.slot(4)
    qd, kd, ed = (ch.slot(5), ch.slot(8)), (ch.slot(6), ch.slot(9)), (ch.slot(7), ch.slot(10))
    homes = (ch.slot(0), ch.slot(1)), (ch.slot(2), ch.slot(11))

    def piece(d, i):
        return homes[d][i // 4][:, i % 4, :].rearrange("p (h v) -> p h v", v=P)

    def state(d, c):
        return piece(d, c - 1 if d == 0 else c)
    aT = [piece(0, 7), piece(1, 7)]
    end = [ch.sm[:, 64 + 32 * d:96 + 32 * d].rearrange("p (j c) -> p j c", c=8) for d in range(2)]
    turned, natural, kv, stepped, grams, masked, summed, squared, sums, rooted, done = ch.counters(
        "end_keys_turned", "end_keys_natural", "kv_products", "states_stepped", "odd_grams", "odd_masked",
        "odd_summed", "odd_squared", "odd_sums", "odd_rooted", "odd_heads_done")
    with nc.Block() as block:
        @block.tensor
        def _(pe):
            for d in range(2):
                for s in range(4):
                    for h in range(4):
                        ins = pe.transpose(ps[:, 4 * d + s, h * P:(h + 1) * P], ed[d][:, h, s * P:(s + 1) * P],
                                           ch.m("ident"))
                ins.then_inc(turned.sem, 1)
                turned.total += 1

            def gram(h):
                pe.wait_ge(natural.sem, natural.at(8))
                if h >= 1:
                    pe.wait_ge(masked.sem, masked.at(h))
                for d in range(2):
                    for s in range(4):
                        cols = slice(s * P, (s + 1) * P)
                        ins = pe.matmul(ps[:, 2 + d, cols], kd[d][:, h, cols], qd[d][:, h, cols], start=True, stop=True)
                ins.then_inc(grams.sem, 1)
                grams.total += 1

            def output(h):
                pe.wait_ge(masked.sem, masked.at(h + 1))
                if h >= 2:
                    pe.wait_ge(done.sem, done.at(h - 1))
                bank = 4 + h % 2
                for s in range(4):
                    pe.matmul(ps[:, bank, s * P:(s + 1) * P], I[:, s, h * P:(h + 1) * P], aT[h % 2][:, s, :],
                              start=s == 0, stop=False, skip_group_check=True)
                for c in range(8):
                    cols = slice(c * 64, (c + 1) * 64)
                    for d in range(2):
                        if (c > 0) if d == 0 else (c < 7):
                            ins = pe.matmul(ps[:, bank, cols], state(d, c)[:, h, :], qd[d][:, h, cols], start=False,
                                            stop=c == 7, skip_group_check=True)
                ins.then_inc(summed.sem, 1)
                summed.total += 1

            def norm_sum(h):
                pe.wait_ge(squared.sem, squared.at(h + 1))
                pe.matmul(ps[:, 6 + h % 2, :], ch.m("ones"), qd[0][:, h, :], start=True, stop=True).then_inc(sums.sem, 1)
                sums.total += 1

            for i in range(7):
                for d in range(2):
                    c = i if d == 0 else 7 - i
                    s, rows = c // 2, slice(64 * (c % 2), 64 * (c % 2) + 64)
                    if i == 0:
                        pe.wait_ge(natural.sem, natural.at(4 * d + 4))
                    else:
                        pe.wait_ge(stepped.sem, stepped.at(2 * i - 1 + d))
                    for h in range(4):
                        cols = slice(h * P, (h + 1) * P)
                        ins = pe.matmul(ps[:, d, cols], ed[d][rows, s, cols], I[rows, s, cols], start=True, stop=True)
                    ins.then_inc(kv.sem, 1)
                    kv.total += 1
                if i in (1, 4):
                    gram(i // 3)
            pe.wait_ge(stepped.sem, stepped.at(14))
            output(0)
            gram(2)
            output(1)
            gram(3)
            norm_sum(0)
            output(2)
            norm_sum(1)
            output(3)
            norm_sum(2)
            norm_sum(3)

        @block.vector
        def _(dve):
            v = Line(dve, ch.S["vector_step"])

            def mask(h):
                v.after(grams, h + 1)
                if h >= 2:
                    v.after(summed, h - 1)
                b = [ps[:, 2 + d, :].rearrange("p (s t) -> p s t", t=P) for d in range(2)]
                v(dve.tensor_tensor(b[1], b[1], ch.m4("mLI"), MUL))
                v(dve.tensor_tensor(aT[h % 2], b[0], ch.m4("mUI"), MUL))
                v(dve.tensor_tensor(aT[h % 2], aT[h % 2], b[1], ADD), masked)

            def finish(h):
                t = qd[1][:, h, :]
                v.after(rooted, h + 1)
                v(dve.reciprocal(t, t))
                v(dve.scalar_tensor_tensor(t, t, ch.v("hgrn_head_norm_g_3", 4 * G + h), Z[:, h, :], MUL, MUL))
                v(dve.tensor_tensor(Z[:, h, :], ps[:, 4 + h % 2, :], t, MUL), done)

            for i in range(7):
                for d in range(2):
                    c = i if d == 0 else 7 - i
                    new = state(d, c + 1 if d == 0 else c - 1)
                    got = ps[:, d, :].rearrange("p (h v) -> p h v", v=P)
                    v.after(kv, 2 * i + d + 1)
                    if i == 0:
                        v(dve.tensor_copy(new, got), stepped)
                    else:
                        v(dve.tensor_tensor(new, state(d, c), end[d][:, :, c:c + 1].to_broadcast([P, 4, P]), MUL))
                        v(dve.tensor_tensor(new, new, got, ADD), stepped)
                if i in (2, 5):
                    mask(i // 3)
            mask(2)
            finish(0)
            mask(3)
            for h in range(1, 4):
                finish(h)

        @block.scalar
        def _(act):
            a = Line(act, ch.S["scalar_step"])
            for d in range(2):
                a.after(turned, d + 1)
                for s in range(4):
                    a(act.copy(ed[d][:, s, :], ps[:, 4 * d + s, :]), natural)
            for h in range(4):
                a.after(summed, h + 1)
                a(act.square(qd[0][:, h, :], ps[:, 4 + h % 2, :]), squared)
                a.after(sums, h + 1)
                a(act.activation(qd[1][:, h, :], ps[:, 6 + h % 2, :], ACT.Sqrt, bias=ch.eps[:, 0:1], scale=1.0 / P), rooted)


def odd_layer(ch):
    normalise(ch, ch.xT, ch.hT, T, [ch.v("norm_g_odd_3", i) for i in range(8)], None)
    odd_bounds(ch)
    for G in range(4):
        odd_project(ch, G)
        odd_recurrence(ch, G)
        add_to_stream(ch, ch.slot(4), 8, 1)


def block3(ch):
    even_layer(ch)
    odd_layer(ch)
    normalise(ch, ch.xT, ch.xT, T, [ch.v("final_norm_g_3", i) for i in range(8)], None)


def block3_plan(A):
    out = blocks(A["w_in_even_3"], 0, 5632) + blocks(A["w_out_even_3"], 0, D)
    w, o = A["w_in_odd_3"], A["w_out_odd_3"]
    for G in range(4):
        for i in (1, 2, 0, 3, 4):
            out += blocks(w, i * 2048 + G * 512, i * 2048 + (G + 1) * 512)
        out.append(([(o[G * 512:(G + 1) * 512, :].rearrange("(k p) c -> p k c", p=P), 0, D)], 4, D))
    return out


def program(nc, A, out):
    ctx = ExitStack()
    with ctx:
        ch = Chip(nc, ctx, A, plan(A))
        block1(ch)
        block2(ch)
        block3(ch)
        write_out(ch, out)


def plan(A):
    return block1_plan(A) + block2_plan(A) + block3_plan(A)


def write_out(ch, out):
    done = ch.counter("output_written")
    with ch.nc.Block() as block:
        @block.sync
        def _(sp):
            sp.dma_start(out.rearrange("(k p) t -> p k t", p=P), ch.xT[:, :, :]).then_inc(done.sem, 16)
            sp.wait_ge(done.sem, 16)


WEIGHTS = ["w_ada", "w_in", "w_up", "a_up", "w_a_out", "w_b_out", "w_o"]
WEIGHTS_2 = ["w_mod", "w_in", "w_out", "w_router", "w_gate", "w_up", "w_down"]
WEIGHTS_3 = ["w_in_even", "w_out_even", "w_in_odd", "w_out_odd"]


def laid_out(inputs):
    cols = []
    for name, w in VECTORS:
        a = np.asarray(inputs[name])
        if name in ("q_gain", "k_gain"):
            a = np.concatenate([a[0], a[0]])
        if name == "attn_sink_3":
            cols.append(np.ascontiguousarray(np.broadcast_to(a.reshape(1, 8), (P, 8))))
            continue
        cols.append(a.reshape(-1, P).T)
    arrays = {"vectors": np.ascontiguousarray(np.concatenate(cols, 1)), "masks": mask_arrays()}
    arrays["xT"] = np.ascontiguousarray(np.asarray(inputs["x"])[0].T)
    arrays["ctxT"] = np.ascontiguousarray(np.asarray(inputs["ctx_2"])[0].T)
    for name in WEIGHTS:
        arrays[name] = np.asarray(inputs[name])[0]
    for name in WEIGHTS_2:
        arrays[name + "_2"] = np.asarray(inputs[name + "_2"])[0]
    rpb = np.asarray(inputs["rpb_2"])[0]
    c, kc = np.arange(64)[:, None], np.arange(64)[None, :]
    dc = np.clip(kc - c + 15, 0, 30)
    lower, upper = rpb[:, 1:15][:, :, dc], rpb[:, 0:14][:, :, dc]
    arrays["rpb"] = np.ascontiguousarray(
        np.concatenate([lower, upper], 2).transpose(2, 0, 1, 3).reshape(P, 8 * 14 * 64))
    for name in WEIGHTS_3:
        arrays[name + "_3"] = np.asarray(inputs[name + "_3"])[0]
    rows = [np.broadcast_to(np.asarray(inputs[n]).reshape(1, -1), (P, np.asarray(inputs[n]).size))
            for n in ("gmlp_ln_g_3", "gmlp_ln_b_3", "gmlp_b_s_3")]
    mixers = np.asarray(inputs["gmlp_w_s_3"])[0].transpose(2, 0, 1).reshape(P, 512)
    arrays["gmlp"] = np.ascontiguousarray(np.concatenate(rows + [mixers], 1))
    dist = np.abs(np.arange(384)[None, :] - 128 - np.arange(P)[:, None]).astype(np.float32)
    arrays["band"] = np.concatenate([dist, np.where(dist > 128, np.float32(-BIG), np.float32(0))], 1)
    return arrays


def kernel(**inputs):
    import concourse.bacc as bacc
    from concourse.bass_utils import run_bass_kernel_spmd

    nc = bacc.Bacc("TRN2", target_bir_lowering=False, num_devices=1)
    arrays = laid_out(inputs)
    A = {n: nc.dram_tensor("in_" + n, a.shape, F32, kind="ExternalInput").ap() for n, a in arrays.items()}
    out = nc.dram_tensor("out", (D, T), F32, kind="ExternalOutput").ap()
    program(nc, A, out)
    r = run_bass_kernel_spmd(nc, [{"in_" + n: a for n, a in arrays.items()}], core_ids=[0])
    return np.ascontiguousarray(r.results[0]["out"].T).reshape(1, T, D)
```

```python
from contextlib import ExitStack

import numpy as np
import concourse.bass as bass
from concourse import mybir

F32 = mybir.dt.float32
ALU = mybir.AluOpType
ACT = mybir.ActivationFunctionType
AXX = mybir.AxisListType.X
MUL, ADD, SUB, MAX, MIN = ALU.mult, ALU.add, ALU.subtract, ALU.max, ALU.min

P = 128
T = 512
D = 1024
KD = D // P
TB = T // P
L = 256
HD = 64
BIG = 1e30
BANKS = 8
RING = 4
SLOT = 4096
DECAY = 0.606531
E_ = 16
CAP = 64
FE = 2048


class Counter:

    def __init__(self, sem):
        self.sem, self.total, self.base = sem, 0, 0

    def rebase(self):
        self.base = self.total
        return self

    def at(self, n):
        return self.base + n


class Line:

    def __init__(self, eng, own):
        self.eng, self.own = eng, own

    def __call__(self, ins, sig=None, step=1):
        sig = sig or self.own
        ins.then_inc(sig.sem, step)
        sig.total += step
        self.eng.wait_ge(sig.sem, sig.total)

    def after(self, sig, n):
        self.eng.wait_ge(sig.sem, sig.at(n))


VECTORS = [
    ("c", 8), ("norm_w", 8), ("b_ada", 24), ("mu", 17), ("w0", 4), ("a0", 4), ("k_k", 4), ("k_a", 4),
    ("r_k", 4), ("gn_w", 4), ("gn_b", 4), ("q_gain", 1), ("k_gain", 1),
    ("c_2", 8), ("c_ctx_2", 8), ("b_mod_2", 48), ("norm_mix_g_2", 8), ("conv_w_2", 31 * 4),
    ("conv_b_2", 4), ("conv_ln_g_2", 4), ("conv_ln_b_2", 4), ("norm_ffn_g_2", 8), ("norm_final_g_2", 8),
    ("norm_g_even_3", 8), ("norm_g_odd_3", 8), ("hgrn_gamma_fwd_3", 32), ("hgrn_gamma_bwd_3", 32),
    ("hgrn_head_norm_g_3", 16), ("final_norm_g_3", 8), ("attn_sink_3", 8),
]
AT = {}
_n = 0
for _name, _w in VECTORS:
    AT[_name] = (_n, _w)
    _n += _w
NVEC = _n

MASKS = ["ident", "ones", "blk64", "mU16", "mL16", "mUoff", "mU", "mUI", "mLI", "bd", "adm", "iota", "win"]


def mask_arrays():
    i = np.arange(P)
    row, col = i[:, None], i[None, :]
    c64, c16 = row // 64 == col // 64, row // 16 == col // 16
    m = {
        "ident": row == col, "ones": np.ones((P, P), bool), "blk64": c64,
        "mU16": (row < col) & c16, "mL16": (row > col) & c16, "mUoff": (row < col) & c64 & ~c16,
        "mU": (row < col) & c64, "mUI": (row <= col) & c64, "mLI": (row >= col) & c64, "bd": c64,
        "iota": (col % 64 + 1) * np.ones((P, 1)),
        "win": -BIG * ((col < np.clip(row % 64 - 8, 0, 48)) | (col >= np.clip(row % 64 - 8, 0, 48) + 16)),
        "adm": -BIG * ((row < 64) & (col >= 64)),
    }
    return np.concatenate([m[k].astype(np.float32) for k in MASKS], 1)


class Chip:

    def __init__(self, nc, ctx, arrays, plan):
        self.nc, self.ctx, self.A, self.plan = nc, ctx, arrays, plan

        def sb(name, shape, dt=F32):
            return ctx.enter_context(nc.sbuf_tensor(name, shape, dt))

        self.xT = sb("xT", [P, KD, T])
        self.hT = sb("hT", [P, KD, T])
        self.ring = sb("weight_ring", [P, RING, SLOT])
        self.W = sb("work", [P, 12, 2048])
        self.vec = sb("vectors", [P, NVEC])
        self.msk = sb("masks", [P, len(MASKS) * P])
        self.csil = sb("silu_of_conditions", [P, KD, 32])
        self.mstage = sb("modulation_rows", [P, 4, P])
        self.mod1 = sb("mod1", [P, 24])
        self.mod2 = sb("mod2", [P, 48, 2])
        self.sm = sb("small", [P, 192])
        self.eps = sb("eps", [P, 4])
        self.ps = ctx.enter_context(nc.psum_tensor("ps", [P, BANKS, 512], F32))
        self.S = {}
        self.free_at = {}
        for n in ("tensor_step", "vector_step", "scalar_step", "pool_step", "aux_loaded"):
            self.counter(n)
        self.loaded = [self.counter(f"weights_loaded{i}") for i in range(RING)]
        self.arrived = {}
        self.issued = 0
        self.used = 0

    def counter(self, name):
        if name not in self.S:
            self.S[name] = Counter(self.ctx.enter_context(self.nc.semaphore(name)))
        return self.S[name].rebase()

    def counters(self, *names):
        return [self.counter(n) for n in names]

    def v(self, name, i=0, n=None):
        a, w = AT[name]
        return self.vec[:, a + i:a + i + (n or 1)]

    def m(self, name):
        i = MASKS.index(name)
        return self.msk[:, i * P:(i + 1) * P]

    def m4(self, name):
        return self.m(name).unsqueeze(1).to_broadcast([P, 4, P])

    def slot(self, i, n=1, kt=None):
        a = self.W[:, i:i + n, :].rearrange("p s n -> p (s n)")
        return a.rearrange("p (k t) -> p k t", t=T)

    def rslot(self, i):
        a = self.ring[:, i // 2, (i % 2) * 2048:(i % 2 + 1) * 2048]
        return a.rearrange("p (k t) -> p k t", t=T)

    def stream(self, sp, upto):
        upto = min(upto, len(self.plan))
        while self.issued < upto:
            i = self.issued
            sources, kt, c = self.plan[i]
            if i >= RING:
                sp.wait_ge(*self.free_at[i - RING])
            sig = self.loaded[i % RING]
            dst = self.block_view(i)
            for src, c0, n in sources:
                sp.dma_start(dst[:, :, c0:c0 + n], src).then_inc(sig.sem, 16)
                sig.total += 16
            self.arrived[i] = (sig.sem, sig.total)
            self.issued += 1

    def block_view(self, i):
        _, kt, c = self.plan[i]
        return self.ring[:, i % RING, 0:kt * c].rearrange("p (k c) -> p k c", k=kt)

    def block_wait(self, eng, i):
        eng.wait_ge(*self.arrived[i])


def blocks(w, c0, c1):
    kt = w.shape[0] // P
    width = min(SLOT // kt, 512)
    out = []
    for c in range(c0, c1, width):
        n = min(width, c1 - c)
        out.append(([(w[:, c:c + n].rearrange("(k p) c -> p k c", p=P), 0, n)], kt, n))
    return out


def joined(w, parts):
    c, sources = 0, []
    for c0, c1 in parts:
        sources.append((w[:, c0:c1].rearrange("(k p) c -> p k c", p=P), c, c1 - c0))
        c += c1 - c0
    return [(sources, w.shape[0] // P, c)]


def project(ch, nblocks, tiles, ahead=RING, extra_sync=None, vector_after=None, scalar_after=None,
            banks=BANKS, tensor_beside={}, vector_beside={}, scalar_beside={}, norm=None):
    nc = ch.nc
    first = ch.used
    R = banks
    ready, by_act, by_dve = ch.counters("tile_ready", "tile_scalar_done", "tile_vector_done")
    na = np.cumsum([t[5][0] is not None for t in tiles])
    nv = np.cumsum([t[5][1] is not None for t in tiles])

    def shape(t):
        b, kind, where, src, ntok, _ = t
        c = ch.plan[first + b][2] if b is not None else P
        if kind == "T":
            return min(P, c - where), ntok
        if kind == "N":
            return P, c
        if isinstance(kind, tuple):
            return P, kind[2] - kind[1]
        return P, P

    for n, t in enumerate(tiles):
        if t[0] is not None:
            ch.free_at[first + t[0]] = (ready.sem, ready.at(n + 1))

    with nc.Block() as block:
        @block.sync
        def _(sp):
            if extra_sync:
                extra_sync(sp)
            ch.stream(sp, first + nblocks + ahead)

        @block.tensor
        def _(pe):
            last = -1
            for n, t in enumerate(tiles):
                b, kind, where, src, ntok, ev = t
                i = first + b if b is not None else None
                if b is not None and b != last:
                    ch.block_wait(pe, i)
                    last = b
                if n >= R:
                    if tiles[n - R][5][1] is not None:
                        pe.wait_ge(by_dve.sem, by_dve.at(int(nv[n - R])))
                    else:
                        pe.wait_ge(by_act.sem, by_act.at(int(na[n - R])))
                m, f = shape(t)
                bank = ch.ps[:, n % R, :]
                if kind == "X":
                    pe.wait_ge(by_act.sem, by_act.at(int(na[where])))
                    ins = pe.transpose(bank[:, 0:P], src, ch.m("ident"))
                    ins.then_inc(ready.sem, 1)
                    ready.total += 1
                    continue
                w = ch.block_view(i)
                _, kt, c = ch.plan[i]
                if kind == "M":
                    for k in range(kt):
                        for g in range(4):
                            ins = pe.matmul(bank[32 * g:32 * g + 32, 0:P], ch.csil[:, k, :],
                                            w[:, k, g * P:(g + 1) * P], start=k == 0, stop=k == kt - 1)
                else:
                    for k in range(kt):
                        if n == 0 and norm:
                            norm.wait(pe, k)
                        if k == kt // 2 and n - 0.5 in tensor_beside:
                            tensor_beside[n - 0.5](pe)
                        if kind == "T":
                            ins = pe.matmul(bank[0:m, 0:f], w[:, k, where:where + m], src[:, k, 0:ntok],
                                            start=k == 0, stop=k == kt - 1)
                        else:
                            c0 = kind[1] if isinstance(kind, tuple) else 0
                            ins = pe.matmul(bank[0:m, 0:f], src[:, k, where:where + P], w[:, k, c0:c0 + f],
                                            start=k == 0, stop=k == kt - 1)
                ins.then_inc(ready.sem, 1)
                ready.total += 1
                if n in tensor_beside:
                    tensor_beside[n](pe)

        @block.scalar
        def _(act):
            a = Line(act, ch.S["scalar_step"])
            if norm:
                norm.root(a, act)
                norm.add_shift(a, act)
            for n, t in enumerate(tiles):
                if t[5][0] is not None:
                    m, f = shape(t)
                    a.after(ready, n + 1)
                    t[5][0](a, act, ch.ps[0:m, n % R, 0:f], by_act)
                if n in scalar_beside:
                    scalar_beside[n](a, act)
            if scalar_after:
                scalar_after(a, act)

        @block.vector
        def _(dve):
            v = Line(dve, ch.S["vector_step"])
            if norm:
                norm.scale(v, dve)
            for n, t in enumerate(tiles):
                if t[5][1] is not None:
                    m, f = shape(t)
                    v.after(ready, n + 1)
                    if t[5][0] is not None:
                        v.after(by_act, int(na[n]))
                    t[5][1](v, dve, ch.ps[0:m, n % R, 0:f], by_dve)
                if n in vector_beside:
                    vector_beside[n](v, dve)
            if vector_after:
                vector_after(v, dve)
    ch.used = first + nblocks


def weave(main, side):
    out = []
    for i in range(max(len(main), len(side))):
        out += [x[i] for x in (main, side) if i < len(x)]
    return out


def modulated(ch, tiles, nblocks, bands):
    place = {}
    for x in weave([("main", b) for b in range(nblocks)], [("side", i) for i in range(len(bands))]):
        place[x] = len(place)
    out, pending = [], []

    def turn_rows(i, m):
        dst, bias, first = bands[i]
        n = dst.shape[2]

        def part(v, dve, ps, sig):
            v(dve.tensor_tensor(dst, ps.rearrange("p (g r) -> p g r", r=32)[:, :, first:first + n],
                                bias.unsqueeze(2).to_broadcast([P, 4, n]), ADD), sig)
        return (None, "X", m, ch.mstage[:, i % 4, :], T, (None, part))

    for kind, i in sorted(place, key=place.get):
        b = place[kind, i]
        if kind == "main":
            mine = [t for t in tiles if t[0] == i]
            out += [(b,) + mine[0][1:]]
            out += [turn_rows(*x) for x in pending]
            pending = []
            out += [(b,) + t[1:] for t in mine[1:]]
        else:
            if pending and nblocks <= i:
                out += [turn_rows(*x) for x in pending]
                pending = []
            pending.append((i, len(out)))
            out.append((b, "M", 0, None, T, copy_to(ch.mstage[:, i % 4, :])))
    return out + [turn_rows(*x) for x in pending], len(place)


def copy_to(out):
    return (lambda a, act, ps, sig: a(act.copy(out, ps), sig), None)


def act_to(out, func, **kw):
    return (lambda a, act, ps, sig: a(act.activation(out, ps, func, **kw), sig), None)


class Norm:

    def __init__(self, ch, src, dst, ntok, gain, shift, bank, sq, room, tag=""):
        self.ch, self.src, self.dst, self.n, self.gain, self.bias = ch, src, dst, ntok, gain, shift
        self.kt, self.bank = src.shape[1], ch.ps[:, bank, 0:ntok]
        self.sq, self.rstd, self.tmp = sq[:, :, 0:ntok], room[:, 0, 0:ntok], room[:, 1:3, 0:ntok]
        self.squares, self.sums, self.rooted, self.scaled, self.shifted = ch.counters(
            *[tag + n for n in ("norm_squares", "norm_sums", "norm_root", "norm_scaled", "norm_shifted")])

    def square(self, k):
        def part(a, act):
            if k >= 4:
                a.after(self.sums, k - 3)
            a(act.square(self.sq[:, k % 4, :], self.src[:, k, :]), self.squares)
        return part

    def sum(self, k):
        def part(pe):
            pe.wait_ge(self.squares.sem, self.squares.at(k + 1))
            pe.matmul(self.bank, self.ch.m("ones"), self.sq[:, k % 4, :], start=k == 0,
                      stop=k == self.kt - 1).then_inc(self.sums.sem, 1)
            self.sums.total += 1
        return part

    def root(self, a, act):
        a.after(self.sums, self.kt)
        a(act.activation(self.rstd, self.bank, ACT.Sqrt, bias=self.ch.eps[:, 0:1], scale=1.0 / (P * self.kt)),
          self.rooted)

    def add_shift(self, a, act):
        for k in range(self.kt if self.bias is not None else 0):
            a.after(self.scaled, k + 1)
            a(act.activation(self.dst[:, k, :], self.tmp[:, k % 2, :], ACT.Identity, bias=self.bias[k]),
              self.shifted)

    def scale(self, v, dve):
        v.after(self.rooted, 1)
        v(dve.reciprocal(self.rstd, self.rstd))
        for k in range(self.kt):
            if self.bias is not None and k >= 2:
                v.after(self.shifted, k - 1)
            out = self.dst[:, k, :] if self.bias is None else self.tmp[:, k % 2, :]
            v(dve.scalar_tensor_tensor(out, self.src[:, k, :], self.gain[k], self.rstd, MUL, MUL), self.scaled)

    def wait(self, eng, k):
        last = self.scaled if self.bias is None else self.shifted
        eng.wait_ge(last.sem, last.at(k + 1))


def finish_norm(ch, norm, then=None):
    with ch.nc.Block() as block:
        @block.scalar
        def _(act):
            a = Line(act, ch.S["scalar_step"])
            norm.root(a, act)
            norm.add_shift(a, act)
            for k in range(norm.kt if then else 0):
                norm.wait(act, k)
                then.square(k)(a, act)

        @block.vector
        def _(dve):
            norm.scale(Line(dve, ch.S["vector_step"]), dve)

        @block.tensor
        def _(pe):
            for k in range(norm.kt if then else 0):
                then.sum(k)(pe)


def seq(*parts):
    def run(*engine):
        for part in parts:
            part(*engine)
    return run


def beside_stream(norm, n0=0):
    vector_done = norm.ch.S["tile_vector_done"]

    def square(k):
        def part(a, act):
            a.after(vector_done, n0 + k + 1)
            norm.square(k)(a, act)
        return part
    kt = norm.kt
    scalar = {n0 + k: square(k) for k in range(kt)}
    tensor = {n0 + k + 1: norm.sum(k) for k in range(kt - 1)}
    tensor[n0 + kt - 1] = seq(norm.sum(kt - 2), norm.sum(kt - 1))
    return tensor, scalar



def load_constants(ch):
    nc, A = ch.nc, ch.A
    got = ch.counter("aux_loaded")
    with nc.Block() as block:
        @block.sync
        def _(sp):
            for dst, src in ((ch.vec[:, :], A["vectors"]), (ch.msk[:, :], A["masks"]),
                             (ch.xT[:, :, :], A["xT"].rearrange("(k p) t -> p k t", p=P))):
                sp.dma_start(dst, src).then_inc(got.sem, 16)
                got.total += 16
            ch.stream(sp, RING)
            sp.wait_ge(got.sem, got.total)

        @block.vector
        def _(dve):
            v = Line(dve, ch.S["vector_step"])
            for i, e in enumerate((1e-6, 64e-5, 0.0, 1.0)):
                v(dve.memset(ch.eps[:, i:i + 1], e))
            v(dve.memset(ch.csil[:, :, :], 0.0))
    with nc.Block() as block:
        @block.scalar
        def _(act):
            a = Line(act, ch.S["scalar_step"])
            for i, name in enumerate(("c", "c_2", "c_ctx_2")):
                a(act.activation(ch.csil[:, :, i], ch.v(name, 0, 8), ACT.Silu))


def block1_modulation(ch):
    bands = [(ch.mod1[:, 4 * b:4 * b + 4].unsqueeze(2), ch.v("b_ada", 4 * b, 4), 0) for b in range(6)]
    tiles, n = modulated(ch, [], 0, bands)
    norm = Norm(ch, ch.xT, ch.hT, T, [ch.sm[:, 24 + k:25 + k] for k in range(8)],
                [ch.mod1[:, k:k + 1] for k in range(8)], 7, ch.slot(4), ch.slot(5))
    project(ch, n, tiles, banks=7, tensor_beside={0: seq(*[norm.sum(k) for k in range(8)])},
            scalar_beside={0: seq(*[norm.square(k) for k in range(8)])})
    with ch.nc.Block() as block:
        @block.vector
        def _(dve):
            v = Line(dve, ch.S["vector_step"])
            v(dve.scalar_tensor_tensor(ch.sm[:, 24:32], ch.mod1[:, 8:16], 1.0, ch.v("norm_w", 0, 8), ADD, MUL))
            v(dve.tensor_scalar(ch.sm[:, 32:49], ch.v("mu", 0, 17), -1.0, 1.0, MUL, ADD))
    return norm


def bands2(ch, b0, b1):
    return [(ch.mod2[:, 4 * b:4 * b + 4, :], ch.v("b_mod_2", 4 * b, 4), 1) for b in range(b0, b1)]


def block1_rwkv_projection(ch, norm):
    tmp = ch.slot(9, 2)
    outs = [(ch.slot(0), 0), (ch.slot(1), 4), (ch.slot(2), 8), (ch.slot(11), 12), (ch.slot(3), 13)]
    tiles = []
    for b, (dst, first) in enumerate(outs):
        for j in range(1 if first == 12 else 4):
            t8 = tmp[:, len(tiles) % 8, :]
            one_mu, mu = ch.sm[:, 32 + first + j:33 + first + j], ch.v("mu", first + j)

            def part_a(a, act, ps, sig, t8=t8, one_mu=one_mu):
                a(act.activation(t8, ps, ACT.Identity, scale=one_mu, bias=ch.eps[:, 2:3]), sig)

            def part_v(v, dve, ps, sig, t8=t8, mu=mu, o=dst[:, j, :]):
                v(dve.tensor_copy(o[:, 0:1], t8[:, 0:1]))
                v(dve.scalar_tensor_tensor(o[:, 1:T], ps[:, 0:T - 1], mu, t8[:, 1:T], MUL, ADD), sig)
            tiles.append((b, "T", j * P, ch.hT, T, (part_a, part_v)))
    tiles, n = modulated(ch, tiles, 5, bands2(ch, 0, 5))
    project(ch, n, tiles, ahead=0, norm=norm)


def rwkv_prepare(ch):
    nc = ch.nc
    rT, kT, vT, lora = ch.slot(0), ch.slot(1), ch.slot(2), ch.slot(11)[:, 0, :]
    nT, rdT, bT, kdT, bonus = ch.slot(4), ch.slot(5), ch.slot(6), ch.slot(7), ch.slot(8)
    t0, t1, t2, t3, t4, t5, t6, t7 = [ch.rslot(i) for i in range(8)]
    th = ch.slot(11)[:, 1, :]
    keep = ch.slot(11)[:, 2, :]
    wup = ch.slot(9)[:, 0, :]
    aux = ch.counter("aux_loaded")
    (sq_ready, th_ready, products, lora_out, roots, cum_ready, exps, cml_ready, bonus_in) = ch.counters(
        "key_square_ready", "tanh_ready", "prep_products", "lora_read", "roots_ready", "cum_ready",
        "exps_ready", "cml_ready", "bonus_in_ready")
    ps = ch.ps
    with nc.Block() as block:
        @block.sync
        def _(sp):
            for dst, src in ((wup[0:64, :], ch.A["w_up"]), (wup[64:128, :], ch.A["a_up"])):
                sp.dma_start(dst, src).then_inc(aux.sem, 16)
                aux.total += 16

        @block.vector
        def _(dve):
            v = Line(dve, ch.S["vector_step"])
            for j in range(4):
                v(dve.tensor_scalar(t0[:, j, :], kT[:, j, :], ch.v("k_k", j), None, MUL))
                v(dve.tensor_tensor(t1[:, j, :], t0[:, j, :], t0[:, j, :], MUL), sq_ready)
            v(dve.memset(keep, 1.0))
            v(dve.memset(keep.rearrange("p (c t) -> p c t", t=64)[:, :, 0:1], 0.0))
            v.after(lora_out, 8)
            v(dve.tensor_scalar(t2, t2, -DECAY, None, MUL))
            for j in range(4):
                v(dve.tensor_tensor_scan(t4[:, j, :], keep, t2[:, j, :], 0.0, MUL, ADD), cum_ready)
            v(dve.tensor_tensor(t5, t4, t2, SUB), cml_ready)
            v.after(roots, 4)
            v(dve.tensor_scalar(t1, t1, 1e-12, None, MAX))
            v(dve.reciprocal(t1, t1))
            v(dve.tensor_tensor(t0, t0, t1, MUL))
            v(dve.tensor_tensor(t1, t0, t3, MUL))
            for j in range(4):
                v(dve.tensor_scalar(t3[:, j, :], t3[:, j, :], 1.0, ch.v("k_a", j), SUB, MUL))
                v(dve.scalar_tensor_tensor(t3[:, j, :], t3[:, j, :], 1.0, kT[:, j, :], ADD, MUL))
                v(dve.scalar_tensor_tensor(t2[:, j, :], rT[:, j, :], ch.v("r_k", j), t3[:, j, :], MUL, MUL),
                  bonus_in)
            v.after(exps, 3)
            v(dve.scalar_tensor_tensor(nT, t0, -1.0, t5, MUL, MUL))
            v(dve.tensor_tensor(rdT, rT, t6, MUL))
            v(dve.tensor_tensor(bT, t1, t7, MUL))
            v(dve.tensor_tensor(kdT, t3, t7, MUL))
            v(dve.tensor_copy(ch.sm[:, 64:96].rearrange("p (j c) -> p j c", c=8),
                              t6.rearrange("p j (c t) -> p j c t", t=64)[:, :, :, 63]))
            for j in range(4):
                v.after(products, 13 + j)
                v(dve.tensor_tensor(bonus[:, j, :], vT[:, j, :], ps[:, 4 + j, :], MUL))

        @block.scalar
        def _(act):
            a = Line(act, ch.S["scalar_step"])
            a(act.activation(th[0:64, :], lora[0:64, :], ACT.Tanh), th_ready)
            for j in range(4):
                a.after(products, j + 1)
                a(act.activation(t2[:, j, :], ps[:, j, :], ACT.Sigmoid, bias=ch.v("w0", j)), lora_out)
            for j in range(4):
                a.after(products, 5 + j)
                a(act.activation(t3[:, j, :], ps[:, 4 + j, :], ACT.Sigmoid, bias=ch.v("a0", j)), lora_out)
            for j in range(4):
                a.after(products, 9 + j)
                a(act.activation(t1[:, j, :], ps[:, j, :], ACT.Sqrt, bias=ch.eps[:, 2:3]), roots)
            a.after(cum_ready, 4)
            a(act.activation(t6, t4, ACT.Exp), exps)
            a(act.activation(t7, t4, ACT.Exp, scale=-1.0), exps)
            a.after(cml_ready, 1)
            a(act.activation(t5, t5, ACT.Exp), exps)

        @block.tensor
        def _(pe):
            def product(*args):
                pe.matmul(*args, start=True, stop=True).then_inc(products.sem, 1)
                products.total += 1
            pe.wait_ge(aux.sem, aux.total)
            pe.wait_ge(th_ready.sem, th_ready.at(1))
            for j in range(4):
                product(ps[:, j, :], wup[0:64, j * P:(j + 1) * P], th[0:64, :])
            for j in range(4):
                product(ps[:, 4 + j, :], wup[64:128, j * P:(j + 1) * P], lora[64:128, :])
            for j in range(4):
                pe.wait_ge(sq_ready.sem, sq_ready.at(j + 1))
                pe.wait_ge(lora_out.sem, lora_out.at(j + 1))
                product(ps[:, j, :], ch.m("blk64"), t1[:, j, :])
            for j in range(4):
                pe.wait_ge(bonus_in.sem, bonus_in.at(j + 1))
                pe.wait_ge(lora_out.sem, lora_out.at(8))
                product(ps[:, 4 + j, :], ch.m("blk64"), t2[:, j, :])


def rwkv_transpose(ch):
    nc, ps = ch.nc, ch.ps
    pairs = [(ch.slot(6), ch.slot(9)), (ch.slot(7), ch.slot(10)), (ch.slot(2), ch.slot(11)),
             (ch.slot(4), ch.rslot(7))]
    turned, copied = ch.counters("turned", "turned_copied")
    with nc.Block() as block:
        @block.tensor
        def _(pe):
            for n in range(16):
                src = pairs[n // 4][0]
                if n >= 4:
                    pe.wait_ge(copied.sem, copied.at(n - 3))
                for j in range(4):
                    ins = pe.transpose(ps[:, n % 4, j * P:(j + 1) * P], src[:, j, (n % 4) * P:(n % 4 + 1) * P],
                                       ch.m("ident"))
                ins.then_inc(turned.sem, 1)
                turned.total += 1

        @block.scalar
        def _(act):
            a = Line(act, ch.S["scalar_step"])
            for n in range(16):
                a.after(turned, n + 1)
                a(act.copy(pairs[n // 4][1][:, n % 4, :], ps[:, n % 4, :]), copied)


def rwkv_within_chunks(ch):
    nc, ps = ch.nc, ch.ps
    nT, bT, kdT = ch.slot(4), ch.slot(6), ch.slot(7)
    vN, nN = ch.slot(11), ch.rslot(7)
    w1T, w2 = ch.slot(0), ch.slot(1)

    def mats(i):
        return ch.rslot(i).rearrange("p b (s t) -> p b s t", t=P)
    d, xd, xo, lk, d2, xd2, inv = [mats(i) for i in range(7)]
    I4 = ch.m4("ident")
    products, evacuated = ch.counters("chunk_products", "chunk_evacuated")

    def head(half, b):
        h = 4 * half + b
        return h, slice(64 * (h % 2), 64 * (h % 2) + 64), h // 2

    def tok(s):
        return slice(s * P, (s + 1) * P)

    def steps(half):
        def gram(left, right):
            def f(b, s):
                h, rows, j = head(half, b)
                return left[rows, j, tok(s)], right[rows, j, tok(s)]
            return f

        def mm(left, right):
            return lambda b, s: (left[:, b, s, :], right[:, b, s, :])

        def value(left):
            def f(b, s):
                h, _, _ = head(half, b)
                return left[:, b, s, :], vN[:, s, h * HD:(h + 1) * HD]
            return f
        return [
            (gram(nT, bT), "mask", [(d, "mL16")]), (gram(bT, nT), "mask", [(xd, "mU16"), (xo, "mUoff")]),
            (gram(kdT, nT), "mask", [(lk, "mU")]),
            (mm(xd, d), "copy", d2), (mm(d, xd), "copy", xd2),
            (mm(d2, inv), "add", (inv, inv)),
            (mm(xd2, d2), "copy", d), (mm(d2, xd2), "copy", xd),
            (mm(d, inv), "add", (inv, inv)),
            (mm(xd, d), "copy", d2), (mm(d2, inv), "add", (inv, inv)),
            ("turn", "copy", xd2), (mm(xo, xd2), "copy", d2),
            (mm(d2, inv), "add", (d, inv)), (mm(d2, d), "add", (d, inv)), (mm(d2, d), "add", (d, inv)),
            (value(lk), "value", xd), ("w2", "w2", None), ("w1", "w1", None),
        ]

    with nc.Block() as block:
        @block.tensor
        def _(pe):
            n = 0
            for half in range(2):
                for left_right, how, _ in steps(half):
                    for b in range(4):
                        if n >= 4:
                            pe.wait_ge(evacuated.sem, evacuated.at(n - 3))
                        h, rows, j = head(half, b)
                        bank = ps[:, n % BANKS, :]
                        for s in range(4):
                            if left_right == "turn":
                                ins = pe.transpose(bank[:, tok(s)], inv[:, b, s, :], ch.m("ident"))
                            elif left_right == "w2":
                                ins = pe.matmul(bank[:, s * HD:(s + 1) * HD], d[:, b, s, :], xd[:, b, s, 0:HD],
                                                start=True, stop=True)
                            elif left_right == "w1":
                                ins = pe.matmul(bank[rows, tok(s)], nN[:, s, h * HD:(h + 1) * HD],
                                                d[:, b, s, :], start=True, stop=True)
                            else:
                                left, right = left_right(b, s)
                                ins = pe.matmul(bank[:, s * right.shape[-1]:(s + 1) * right.shape[-1]],
                                                left, right, start=True, stop=True)
                        ins.then_inc(products.sem, 1)
                        products.total += 1
                        n += 1

        @block.vector
        def _(dve):
            v = Line(dve, ch.S["vector_step"])
            n = 0
            for half in range(2):
                for left_right, how, out in steps(half):
                    for b in range(4):
                        h, rows, j = head(half, b)
                        v.after(products, n + 1)
                        flat = ps[:, n % BANKS, :]
                        bank = flat.rearrange("p (s t) -> p s t", t=P)
                        if how == "mask":
                            if len(out) == 2:
                                v(dve.tensor_tensor(out[0][0][:, b], bank, ch.m4(out[0][1]), MUL))
                                v(dve.tensor_tensor(inv[:, b], out[0][0][:, b], I4, ADD))
                            v(dve.tensor_tensor(out[-1][0][:, b], bank, ch.m4(out[-1][1]), MUL), evacuated)
                        elif how == "copy":
                            v(dve.tensor_copy(out[:, b], bank), evacuated)
                        elif how == "add":
                            v(dve.tensor_tensor(out[0][:, b], bank, out[1][:, b], ADD), evacuated)
                        elif how == "value":
                            v(dve.tensor_copy(xd[:, b, :, 0:HD], flat[:, 0:4 * HD].rearrange("p (s t) -> p s t", t=HD)),
                              evacuated)
                        elif how == "w2":
                            v(dve.tensor_copy(w2[:, :, h * HD:(h + 1) * HD],
                                              flat[:, 0:4 * HD].rearrange("p (s t) -> p s t", t=HD)), evacuated)
                        elif how == "w1":
                            v(dve.tensor_copy(w1T[rows, j, :], flat[rows, :]), evacuated)
                        n += 1


def rwkv_chain(ch):
    nc, ps = ch.nc, ch.ps
    w1T, u = ch.slot(0), ch.slot(1)
    bN, kN, vN = ch.slot(9), ch.slot(10), ch.slot(11)
    states = [ch.rslot(c).rearrange("p j (h t) -> p (j h t)", t=P)[:, 0:512].rearrange("p (j t) -> p j t", t=P)
              for c in range(8)]
    tmp = ch.rslot(0)[:, 1, :].rearrange("p (j t) -> p j t", t=P)
    bd = ch.m4("bd")
    end = ch.sm[:, 64:96].rearrange("p (j c) -> p j c", c=8)
    u_sum, u_ready, s_sum, s_ready = ch.counters("u_sum", "u_ready", "state_sum", "state_ready")
    with nc.Block() as block:
        @block.tensor
        def _(pe):
            for c in range(7):
                s, rows = c // 2, slice(64 * (c % 2), 64 * (c % 2) + 64)
                if c > 0:
                    pe.wait_ge(s_ready.sem, s_ready.at(c + 1))
                    for j in range(4):
                        ins = pe.matmul(ps[rows, 0, j * P:(j + 1) * P], w1T[:, j, c * 64:(c + 1) * 64],
                                        states[c][:, j, :], start=True, stop=True)
                    ins.then_inc(u_sum.sem, 1)
                    u_sum.total += 1
                    pe.wait_ge(u_ready.sem, u_ready.at(c))
                for j in range(4):
                    cols = slice(j * P, (j + 1) * P)
                    pe.matmul(ps[:, 1, cols], kN[rows, s, cols], vN[rows, s, cols], start=True, stop=False)
                    ins = pe.matmul(ps[:, 1, cols], bN[rows, s, cols], u[rows, s, cols], start=False, stop=True)
                ins.then_inc(s_sum.sem, 1)
                s_sum.total += 1
            pe.wait_ge(s_ready.sem, s_ready.at(8))
            for j in range(4):
                ins = pe.matmul(ps[64:128, 0, j * P:(j + 1) * P], w1T[:, j, 7 * 64:8 * 64],
                                states[7][:, j, :], start=True, stop=True)
            ins.then_inc(u_sum.sem, 1)
            u_sum.total += 1

        @block.vector
        def _(dve):
            v = Line(dve, ch.S["vector_step"])
            v(dve.memset(states[0], 0.0), s_ready)
            for c in range(8):
                s, rows = c // 2, slice(64 * (c % 2), 64 * (c % 2) + 64)
                if c > 0:
                    v.after(u_sum, c)
                    v(dve.tensor_tensor(u[rows, s, :], ps[rows, 0, :], u[rows, s, :], ADD), u_ready)
                if c < 7:
                    v.after(s_sum, c + 1)
                    v(dve.tensor_tensor(tmp, ps[:, 1, :].rearrange("p (j t) -> p j t", t=P), bd, MUL))
                    v(dve.tensor_tensor(tmp, tmp, states[c], ADD))
                    v(dve.tensor_tensor(states[c + 1], tmp, end[:, :, c:c + 1].to_broadcast([P, 4, P]), MUL),
                      s_ready)


def rwkv_output(ch):
    nc, ps = ch.nc, ch.ps
    rdT, bT, kdT, bonus, gate = ch.slot(5), ch.slot(6), ch.slot(7), ch.slot(8), ch.slot(3)
    u, vN, yT = ch.slot(1), ch.slot(11), ch.slot(2)
    states = [ch.rslot(c).rearrange("p j (h t) -> p (j h t)", t=P)[:, 0:512].rearrange("p (j t) -> p j t", t=P)
              for c in range(8)]
    mb = [ch.rslot(i)[:, 2, :].rearrange("p (s t) -> p s t", t=P) for i in range(4)]
    mI = ch.m4("mUI")
    cen, sq = ch.slot(0), ch.slot(4)
    grams, masked, y_sum, y_out, sums, cen_out, sq_out, roots = ch.counters(
        "grams", "grams_masked", "y_sum", "y_out", "y_means", "y_centred", "y_squares", "y_roots")
    with nc.Block() as block:
        @block.tensor
        def _(pe):
            for j in range(4):
                for e in range(2):
                    rows = slice(64 * e, 64 * e + 64)
                    for i, key in enumerate((bT, kdT)):
                        n = 4 * j + 2 * e + i
                        if n >= 4:
                            pe.wait_ge(masked.sem, masked.at(n - 3))
                            if j >= 1:
                                pe.wait_ge(y_sum.sem, y_sum.at(j))
                        for s in range(4):
                            cols = slice(s * P, (s + 1) * P)
                            ins = pe.matmul(ps[:, 2 * e + i, cols], key[rows, j, cols], rdT[rows, j, cols],
                                            start=True, stop=True)
                        ins.then_inc(grams.sem, 1)
                        grams.total += 1
                pe.wait_ge(masked.sem, masked.at(4 * j + 4))
                if j >= 2:
                    pe.wait_ge(y_out.sem, y_out.at(j - 1))
                bank = 4 + j % 2
                for c in range(8):
                    pe.matmul(ps[:, bank, c * 64:(c + 1) * 64], states[c][:, j, :], rdT[:, j, c * 64:(c + 1) * 64],
                              start=c == 0, stop=False, skip_group_check=True)
                for e in range(2):
                    rows, hc = slice(64 * e, 64 * e + 64), slice((2 * j + e) * HD, (2 * j + e + 1) * HD)
                    for s in range(4):
                        cols = slice(s * P, (s + 1) * P)
                        pe.matmul(ps[rows, bank, cols], u[:, s, hc], mb[2 * e][:, s, :], start=False, stop=False,
                                  skip_group_check=True)
                        ins = pe.matmul(ps[rows, bank, cols], vN[:, s, hc], mb[2 * e + 1][:, s, :],
                                        start=False, stop=e == 1 and s == 3, skip_group_check=True)
                ins.then_inc(y_sum.sem, 1)
                y_sum.total += 1
            for j in range(4):
                pe.wait_ge(y_out.sem, y_out.at(j + 1))
                pe.matmul(ps[:, j, :], ch.m("blk64"), yT[:, j, :], start=True, stop=True).then_inc(sums.sem, 1)
                sums.total += 1
            for j in range(4):
                pe.wait_ge(sq_out.sem, sq_out.at(j + 1))
                if j < 2:
                    pe.wait_ge(y_out.sem, y_out.at(4))
                pe.matmul(ps[:, 4 + j, :], ch.m("blk64"), sq[:, j, :], start=True, stop=True).then_inc(sums.sem, 1)
                sums.total += 1

        @block.vector
        def _(dve):
            v = Line(dve, ch.S["vector_step"])
            for j in range(4):
                for n in range(4):
                    v.after(grams, 4 * j + n + 1)
                    if j >= 1 and n == 0:
                        v.after(y_sum, j)
                    v(dve.tensor_tensor(mb[n], ps[:, n, :].rearrange("p (s t) -> p s t", t=P), mI, MUL), masked)
            for j in range(4):
                v.after(sums, j + 1)
                v(dve.scalar_tensor_tensor(cen[:, j, :], ps[:, j, :], -1.0 / HD, yT[:, j, :], MUL, ADD), cen_out)
            v.after(roots, 4)
            v(dve.reciprocal(sq, sq))
            v(dve.tensor_tensor(cen, cen, sq, MUL))
            for j in range(4):
                v(dve.tensor_scalar(cen[:, j, :], cen[:, j, :], ch.v("gn_w", j), ch.v("gn_b", j), MUL, ADD))
            v(dve.tensor_tensor(cen, cen, bonus, ADD))
            v.after(roots, 5)
            v(dve.tensor_tensor(yT, cen, gate, MUL))

        @block.scalar
        def _(act):
            a = Line(act, ch.S["scalar_step"])
            for j in range(4):
                a.after(y_sum, j + 1)
                a(act.copy(yT[:, j, :], ps[:, 4 + j % 2, :]), y_out)
            for j in range(4):
                a.after(cen_out, j + 1)
                a(act.square(sq[:, j, :], cen[:, j, :]), sq_out)
            for j in range(4):
                a.after(sums, 5 + j)
                a(act.activation(sq[:, j, :], ps[:, 4 + j, :], ACT.Sqrt, bias=ch.eps[:, 1:2], scale=1.0 / HD), roots)
            a(act.activation(gate, gate, ACT.Silu), roots)


def head_norm(ch, tiles, mask, width, eps_col=0):
    nc, ps = ch.nc, ch.ps
    squares, sums, roots, normed = ch.counters("hn_squares", "hn_sums", "hn_roots", "hn_normed")
    n = tiles[0][0].shape[-1]
    sq = ch.slot(9)[:, :, 0:n]
    rt = ch.slot(10)[:, :, 0:n]
    with nc.Block() as block:
        @block.scalar
        def _(act):
            a = Line(act, ch.S["scalar_step"])
            for i in range(len(tiles) + 2):
                if i < len(tiles):
                    if i >= 4:
                        a.after(sums, i - 3)
                    a(act.square(sq[:, i % 4, :], tiles[i][0]), squares)
                if i >= 2:
                    k = i - 2
                    a.after(sums, k + 1)
                    if k >= 4:
                        a.after(normed, k - 3)
                    a(act.activation(rt[:, k % 4, :], ps[:, k % 4, 0:n], ACT.Sqrt, bias=ch.eps[:, eps_col:eps_col + 1],
                                     scale=1.0 / width), roots)

        @block.tensor
        def _(pe):
            for i in range(len(tiles)):
                pe.wait_ge(squares.sem, squares.at(i + 1))
                if i >= 4:
                    pe.wait_ge(roots.sem, roots.at(i - 3))
                pe.matmul(ps[:, i % 4, 0:n], ch.m(mask), sq[:, i % 4, :], start=True, stop=True).then_inc(sums.sem, 1)
                sums.total += 1

        @block.vector
        def _(dve):
            v = Line(dve, ch.S["vector_step"])
            for i, (x, gain) in enumerate(tiles):
                v.after(roots, i + 1)
                v(dve.reciprocal(rt[:, i % 4, :], rt[:, i % 4, :]))
                v(dve.scalar_tensor_tensor(x, x, gain, rt[:, i % 4, :], MUL, MUL), normed)


def attention(ch, units, scale, sinks=False, sync_body=None):
    nc, ps = ch.nc, ch.ps
    wide = ch.slot(9, 2).rearrange("p k t -> p (k t)")
    S = [wide[:, i * 768:(i + 1) * 768] for i in range(3)]
    pT = [wide[:, (3 + i) * 768:(4 + i) * 768] for i in range(2)]
    st = ch.sm[:, 96:120].rearrange("p (i c) -> p i c", c=6)
    scores, softened, taken_max, expd, normed, turned, copied, summed, taken = ch.counters(
        "scores", "scores_scaled", "maxima_ready", "exps_done", "probs_normed", "probs_turned", "probs_copied",
        "values_summed", "group_taken")
    N = len(units)
    group, g = [], 0
    for u in units:
        group.append(g)
        g += u["close"] is not None
    with nc.Block() as block:
        if sync_body:
            @block.sync
            def _(sp):
                sync_body(sp, softened)

        @block.tensor
        def _(pe):
            for i in range(N + 3):
                if i < N:
                    u = units[i]
                    if i >= 2:
                        pe.wait_ge(softened.sem, softened.at(i - 1))
                    for k, c0 in u["keys"]:
                        n = k.shape[-1] if len(k.shape) == 2 else k.shape[-1] * k.shape[-2]
                        bank, off = 2 * (i % 2) + c0 // 512, c0 % 512
                        ins = pe.matmul(ps[:, bank, off:off + n], u["q"], k, start=True, stop=True)
                    ins.then_inc(scores.sem, 1)
                    scores.total += 1
                if 2 <= i < N + 2:
                    u = units[i - 2]
                    pe.wait_ge(normed.sem, normed.at(i - 1))
                    if i >= 3:
                        pe.wait_ge(copied.sem, copied.at(i - 2))
                    for t in range(u["cols"] // P):
                        ins = pe.transpose(ps[:, 4 + t // 4, (t % 4) * P:(t % 4 + 1) * P],
                                           S[(i - 2) % 3][:, t * P:(t + 1) * P], ch.m("ident"))
                    ins.then_inc(turned.sem, 1)
                    turned.total += 1
                if i >= 3:
                    u, gi = units[i - 3], group[i - 3]
                    pe.wait_ge(copied.sem, copied.at(i - 2))
                    if gi >= 2:
                        pe.wait_ge(taken.sem, taken.at(gi - 1))
                    vs = u["values"]
                    for t, val in enumerate(vs):
                        ins = pe.matmul(ps[u["rows"], 6 + gi % 2, u["col"]:u["col"] + P], val,
                                        pT[(i - 3) % 2][:, t * P:(t + 1) * P], start=t == 0, stop=t == len(vs) - 1)
                    ins.then_inc(summed.sem, 1)
                    summed.total += 1

        @block.vector
        def _(dve):
            v = Line(dve, ch.S["vector_step"])
            for i in range(N + 5):
                if i < N:
                    u, s = units[i], S[i % 3]
                    stat = st[:, i % 4, :]
                    v.after(scores, i + 1)
                    if i >= 3:
                        v.after(turned, i - 2)
                    if u.get("prepare"):
                        u["prepare"](v, dve)
                    both = ps[:, 2 * (i % 2):2 * (i % 2) + 2, :].rearrange("p b n -> p (b n)")
                    for n, (b, c0, w) in enumerate(u["biases"]):
                        v(dve.scalar_tensor_tensor(s[:, c0:c0 + w], both[:, c0:c0 + w], scale, b, MUL, ADD),
                          softened if n + 1 == len(u["biases"]) and not u["plain"] else None)
                    for n, (c0, w) in enumerate(u["plain"]):
                        v(dve.tensor_scalar(s[:, c0:c0 + w], both[:, c0:c0 + w], scale, None, MUL),
                          softened if n + 1 == len(u["plain"]) else None)
                    v(dve.tensor_reduce(stat[:, 0:1], s[:, 0:u["cols"]], AXX, MAX))
                    if sinks:
                        v(dve.tensor_scalar(stat[:, 1:2], stat[:, 0:1], u["sink"], -1.0, MAX, MUL), taken_max)
                    else:
                        v(dve.tensor_scalar(stat[:, 1:2], stat[:, 0:1], -1.0, None, MUL), taken_max)
                if 1 <= i < N + 1:
                    u, stat = units[i - 1], st[:, (i - 1) % 4, :]
                    v.after(expd, i)
                    if sinks:
                        v(dve.tensor_tensor(stat[:, 2:3], stat[:, 2:3], stat[:, 4:5], ADD))
                    v(dve.reciprocal(stat[:, 3:4], stat[:, 2:3]))
                    s = S[(i - 1) % 3][:, 0:u["cols"]]
                    v(dve.tensor_scalar(s, s, stat[:, 3:4], None, MUL), normed)
                if i >= 5 and units[i - 5]["close"] is not None:
                    v.after(summed, i - 4)
                    units[i - 5]["close"](v, dve, ps[:, 6 + group[i - 5] % 2, :], taken)

        @block.scalar
        def _(act):
            a = Line(act, ch.S["scalar_step"])
            for i in range(N + 2):
                if i < N:
                    u, s, stat = units[i], S[i % 3][:, 0:units[i]["cols"]], st[:, i % 4, :]
                    a.after(taken_max, i + 1)
                    if sinks:
                        a(act.activation(stat[:, 4:5], u["sink"], ACT.Exp, bias=stat[:, 1:2]))
                    a(act.activation(s, s, ACT.Exp, bias=stat[:, 1:2], accum_out=stat[:, 2:3]), expd)
                if i >= 2:
                    u = units[i - 2]
                    a.after(turned, i - 1)
                    if i >= 4:
                        a.after(summed, i - 3)
                    both = ps[:, 4:6, :].rearrange("p b n -> p (b n)")
                    a(act.copy(pT[(i - 2) % 2][:, 0:u["cols"]], both[:, 0:u["cols"]]), copied)


def dsa_projection(ch):
    q, k, gate, iq, ik = ch.slot(0), ch.slot(1), ch.slot(4), ch.slot(5), ch.slot(6)
    v = ch.slot(3)
    iw = ch.sm[:, 120:152]
    tiles = []
    for b, dst in ((0, q), (1, k)):
        tiles += [(b, "T", j * P, ch.hT, T, copy_to(dst[:, j, :])) for j in range(4)]
    tiles += [(2, "N", s * P, ch.hT, T, copy_to(v[:, s, :])) for s in range(4)]
    tiles += [(3, "T", j * P, ch.hT, T, act_to(gate[:, j, :], ACT.Silu)) for j in range(4)]
    tiles += [(4, "T", j * P, ch.hT, T, copy_to(iq[:, j, :])) for j in range(4)]
    tiles += [(5, "T", 0, ch.hT, T, copy_to(ik[:, 0, :]))]
    tiles += [(5, ("N", P, P + 8), s * P, ch.hT, T,
               (lambda a, act, ps, sig, s=s: a(act.mul(iw[:, 8 * s:8 * s + 8], ps, 8 ** -0.5), sig), None))
              for s in range(4)]
    tiles, n = modulated(ch, tiles, 6, bands2(ch, 5, 10))
    project(ch, n, tiles)


def dsa_scores(ch):
    nc, ps = ch.nc, ch.ps
    iq, ik, score = ch.slot(5), ch.slot(6), ch.slot(8)
    iw = ch.sm[:, 120:152]
    rel = ch.slot(9)
    dots, relus, added = ch.counters("index_dots", "index_relus", "index_added")
    units = [(s, h) for s in range(1, 4) for h in range(8)]
    with nc.Block() as block:
        @block.tensor
        def _(pe):
            for i, (s, h) in enumerate(units):
                if i >= 4:
                    pe.wait_ge(relus.sem, relus.at(i - 3))
                rows, n = slice(64 * (h % 2), 64 * (h % 2) + 64), P * (s + 1)
                pe.matmul(ps[:, i % 4, 0:n], iq[rows, h // 2, s * P:(s + 1) * P], ik[rows, 0, 0:n],
                          start=True, stop=True).then_inc(dots.sem, 1)
                dots.total += 1

        @block.scalar
        def _(act):
            a = Line(act, ch.S["scalar_step"])
            for i, (s, h) in enumerate(units):
                a.after(dots, i + 1)
                if i >= 4:
                    a.after(added, i - 3)
                n = P * (s + 1)
                a(act.activation(rel[:, i % 4, 0:n], ps[:, i % 4, 0:n], ACT.Relu, scale=HD ** -0.5), relus)

        @block.vector
        def _(dve):
            v = Line(dve, ch.S["vector_step"])
            for i, (s, h) in enumerate(units):
                v.after(relus, i + 1)
                n = P * (s + 1)
                w = iw[:, 8 * s + h:8 * s + h + 1]
                if h == 0:
                    v(dve.tensor_scalar(score[:, s, 0:n], rel[:, i % 4, 0:n], w, None, MUL), added)
                else:
                    v(dve.scalar_tensor_tensor(score[:, s, 0:n], rel[:, i % 4, 0:n], w, score[:, s, 0:n], MUL, ADD),
                      added)


def dsa_select(ch):
    score, bias = ch.slot(8), ch.slot(7)
    best = ch.sm[:, 152:160]

    def run(v, dve):
        v(dve.tensor_copy(bias[:, 0, 0:P], ch.m("adm")))
        for s in range(1, 4):
            n = P * (s + 1)
            row = score[:, s, 0:n]
            v(dve.tensor_tensor(row[:, n - P:n], row[:, n - P:n], ch.m("adm"), ADD))
            for _ in range(P // 8):
                v(dve.max(best, row))
                v(dve.match_replace(row, best, row, -3e38))
            v(dve.tensor_scalar(bias[:, s, 0:n], row, -2e38, -BIG, ALU.is_gt, MUL))
    return run


def dsa_attention(ch):
    q, k, v, gate, bias, out = (ch.slot(0), ch.slot(1), ch.slot(3), ch.slot(4), ch.slot(7), ch.slot(11))
    units = []
    for h in range(8):
        rows, j = slice(64 * (h % 2), 64 * (h % 2) + 64), h // 2
        for s in range(4):
            n = P * (s + 1)

            def close(line, dve, ps, sig, j=j):
                line(dve.tensor_tensor(out[:, j, :], ps, gate[:, j, :], MUL), sig)
            units.append(dict(
                q=q[rows, j, s * P:(s + 1) * P], keys=[(k[rows, j, 0:n], 0)],
                biases=[(bias[:, s, 0:n], 0, n)], plain=[], cols=n,
                values=[v[:, t, h * HD:(h + 1) * HD] for t in range(s + 1)],
                rows=rows, col=s * P, close=close if h % 2 == 1 and s == 3 else None))
    attention(ch, units, HD ** -0.5)


def block1(ch):
    A = ch.A
    load_constants(ch)
    norm = block1_modulation(ch)
    block1_rwkv_projection(ch, norm)
    rwkv_prepare(ch)
    rwkv_transpose(ch)
    rwkv_within_chunks(ch)
    rwkv_chain(ch)
    rwkv_output(ch)
    dsa_projection(ch)
    head_norm(ch, [(ch.slot(i)[:, j, :], ch.v(g)) for i, g in ((0, "q_gain"), (1, "k_gain")) for j in range(4)],
              "blk64", HD)
    dsa_scores(ch)
    ga = ch.slot(5, 2)
    project(ch, 2, [(b, "T", j * P, ch.hT, T, act_to(ga[:, 4 * b + j, :], ACT.Sigmoid)) for b in range(2)
                    for j in range(4)], vector_after=dsa_select(ch))
    dsa_attention(ch)
    gb, merged, y, yb = ch.slot(0, 2), ch.slot(7, 2), ch.slot(2), ch.slot(11)
    tmp = ch.slot(9)
    tiles = [(b, "T", j * P, ch.hT, T, act_to(gb[:, 4 * b + j, :], ACT.Sigmoid)) for b in range(2) for j in range(4)]
    for b in range(2):
        for j in range(4):
            def part(v, dve, ps, sig, n=4 * b + j):
                v(dve.tensor_tensor(merged[:, n, :], ps, ga[:, n, :], MUL), sig)
            tiles.append((2 + b, "T", j * P, y, T, (None, part)))
    for b in range(2):
        for j in range(4):
            def part(v, dve, ps, sig, n=4 * b + j):
                v(dve.tensor_tensor(tmp[:, n % 4, :], ps, gb[:, n, :], MUL), sig)
                v(dve.tensor_tensor(merged[:, n, :], merged[:, n, :], tmp[:, n % 4, :], ADD))
            tiles.append((4 + b, "T", j * P, yb, T, (None, part)))
    tiles, n = modulated(ch, tiles, 6, bands2(ch, 10, 12))
    project(ch, n, tiles)
    block2_gains(ch)
    tiles = []
    for b in range(2):
        for j in range(4):
            def part(v, dve, ps, sig, n=4 * b + j):
                v(dve.scalar_tensor_tensor(ch.xT[:, n, :], ps, ch.mod1[:, 16 + n:17 + n], ch.xT[:, n, :], MUL, ADD), sig)
            tiles.append((b, "T", j * P, merged, T, (None, part)))
    ctxT, hcT = (ch.W[:, i, :].rearrange("p (k t) -> p k t", t=L) for i in (2, 11))
    norm = Norm(ch, ch.xT, ch.hT, T, [ch.sm[:, 24 + i:25 + i] for i in range(8)],
                [ch.mod2[:, i, 0:1] for i in range(8)], 7, ch.slot(0), ch.slot(10))
    context = Norm(ch, ctxT, hcT, L, [ch.sm[:, 32 + i:33 + i] for i in range(8)],
                   [ch.mod2[:, i, 1:2] for i in range(8)], 6, ch.slot(3), ch.slot(4), "context_")
    aux = ch.counter("aux_loaded")
    tensor, scalar = beside_stream(norm)

    def load(sp):
        sp.dma_start(ctxT, ch.A["ctxT"].rearrange("(k p) t -> p k t", p=P)).then_inc(aux.sem, 16)
        aux.total += 16

    def context_squares(a, act):
        a.after(aux, 16)
        seq(*[context.square(k) for k in range(8)])(a, act)
    tensor[2] = seq(tensor[2], *[context.sum(k) for k in range(8)])
    scalar[1] = seq(scalar[1], context_squares)
    scalar[2] = seq(scalar[2], context.root, context.add_shift)
    project(ch, 2, tiles, banks=6, extra_sync=load, tensor_beside=tensor, scalar_beside=scalar,
            vector_beside={2: context.scale})
    return norm


def block1_plan(A):
    w, m = A["w_in"], blocks(A["w_mod_2"], 0, 6144)
    return (blocks(A["w_ada"], 0, 3072)
            + weave(blocks(w, 0, 1536) + blocks(w, 1536, 1664) + blocks(w, 1664, 2176), m[0:5])
            + weave(blocks(w, 2176, 4736) + joined(w, [(4736, 4800), (4736, 4800), (4800, 4808)]), m[5:10])
            + blocks(w, 4808, 5832)
            + weave(blocks(w, 5832, 6856) + blocks(A["w_a_out"], 0, 1024) + blocks(A["w_b_out"], 0, 1024), m[10:12])
            + blocks(A["w_o"], 0, 1024))



def block2_gains(ch):
    with ch.nc.Block() as block:
        @block.vector
        def _(dve):
            v = Line(dve, ch.S["vector_step"])
            for o, j, c, g in ((24, 8, 0, "norm_mix_g_2"), (32, 8, 1, "norm_mix_g_2"), (40, 32, 0, "norm_ffn_g_2")):
                v(dve.scalar_tensor_tensor(ch.sm[:, o:o + 8], ch.mod2[:, j:j + 8, c], 1.0, ch.v(g, 0, 8), ADD, MUL))


def conv_taps(ch, vpad, y):
    def run(v, dve):
        for j in range(4):
            for w in range(31):
                src, tap = vpad[:, j, w:w + T], ch.v("conv_w_2", 4 * w + j)
                if w == 0:
                    v(dve.tensor_scalar(y[:, j, :], src, tap, ch.v("conv_b_2", j), MUL, ADD))
                else:
                    v(dve.scalar_tensor_tensor(y[:, j, :], src, tap, y[:, j, :], MUL, ADD))
    return run


def conv_norm(ch, y):
    nc, ps = ch.nc, ch.ps
    sq, mean, rstd = ch.slot(5), ch.slot(9)[:, 0, :], ch.slot(9)[:, 1, :]
    sums, centred, squares, root = ch.counters("cn_sums", "cn_centred", "cn_squares", "cn_root")
    with nc.Block() as block:
        @block.tensor
        def _(pe):
            for j in range(4):
                ins = pe.matmul(ps[:, 0, :], ch.m("ones"), y[:, j, :], start=j == 0, stop=j == 3)
            ins.then_inc(sums.sem, 1)
            for j in range(4):
                pe.wait_ge(squares.sem, squares.at(j + 1))
                ins = pe.matmul(ps[:, 1, :], ch.m("ones"), sq[:, j, :], start=j == 0, stop=j == 3)
            ins.then_inc(sums.sem, 1)
            sums.total += 2

        @block.vector
        def _(dve):
            v = Line(dve, ch.S["vector_step"])
            v.after(sums, 1)
            v(dve.tensor_scalar(mean, ps[:, 0, :], 1.0 / 512, None, MUL))
            for j in range(4):
                v(dve.tensor_tensor(y[:, j, :], y[:, j, :], mean, SUB), centred)
            v.after(root, 1)
            v(dve.reciprocal(rstd, rstd))
            for j in range(4):
                v(dve.tensor_tensor(sq[:, j, :], y[:, j, :], rstd, MUL), centred)

        @block.scalar
        def _(act):
            a = Line(act, ch.S["scalar_step"])
            for j in range(4):
                a.after(centred, j + 1)
                a(act.square(sq[:, j, :], y[:, j, :]), squares)
            a.after(sums, 2)
            a(act.activation(rstd, ps[:, 1, :], ACT.Sqrt, bias=ch.eps[:, 0:1], scale=1.0 / 512), root)
            for j in range(4):
                a.after(centred, 5 + j)
                a(act.activation(y[:, j, :], sq[:, j, :], ACT.Silu, bias=ch.v("conv_ln_b_2", j),
                                 scale=ch.v("conv_ln_g_2", j)))


def neighbourhood_attention(ch):
    q, k, v, out = ch.slot(0), ch.slot(1, 2), ch.slot(3, 2), ch.slot(8)
    k = k.rearrange("p a t -> p (a t)")[:, 0:3072].rearrange("p (j t) -> p j t", t=768)
    v = v[:, 0:6, :]
    flat = ch.slot(11).rearrange("p a t -> p (a t)")
    tab = [flat[:, i * 896:(i + 1) * 896] for i in range(2)]
    loaded = ch.counter("bias_loaded")

    def load(sp, softened):
        for h in range(8):
            if h >= 2:
                sp.wait_ge(softened.sem, softened.at(4 * (h - 1)))
            sp.dma_start(tab[h % 2], ch.A["rpb"][:, h * 896:(h + 1) * 896]).then_inc(loaded.sem, 16)
            loaded.total += 16
            sp.wait_ge(loaded.sem, loaded.total)

    units = []
    for h in range(8):
        rows, j = slice(64 * (h % 2), 64 * (h % 2) + 64), h // 2

        def prepare(line, dve, h=h):
            line.after(loaded, 16 * (h + 1))
            t = tab[h % 2].rearrange("p (r c) -> p r c", c=64)
            line(dve.tensor_tensor(t, t, ch.m("win")[:, 0:64].unsqueeze(1).to_broadcast([P, 14, 64]), ADD))
        for s in range(4):
            def close(line, dve, ps, sig, j=j):
                line(dve.tensor_copy(out[:, j, :], ps), sig)
            units.append(dict(
                q=q[rows, j, s * P:(s + 1) * P], keys=[(k[rows, j, 0:512], 0), (k[rows, j, 512:768], 512)],
                biases=[(tab[h % 2][:, (6 - 2 * s) * 64:(6 - 2 * s) * 64 + 512], 0, 512)], plain=[(512, 256)],
                cols=768, values=[v[:, t, h * HD:(h + 1) * HD] for t in range(6)],
                rows=rows, col=s * P, close=close if h % 2 == 1 and s == 3 else None,
                prepare=prepare if s == 0 else None))
    attention(ch, units, HD ** -0.5, sync_body=load)


def block2_mixer(ch, norm):
    nc = ch.nc
    hcT = ch.W[:, 11, :].rearrange("p (k t) -> p k t", t=L)
    q, a_, y = ch.slot(0), ch.slot(8), ch.slot(7)
    k = ch.slot(1, 2).rearrange("p a t -> p (a t)")[:, 0:3072].rearrange("p (j t) -> p j t", t=768)
    v = ch.slot(3, 2)
    vpad = ch.slot(5, 2).rearrange("p a t -> p (a t)")[:, 0:4 * 542].rearrange("p (j t) -> p j t", t=542)
    sig_g = ch.slot(9)
    tiles = [(0, "T", j * P, ch.hT, T, copy_to(a_[:, j, :])) for j in range(4)]
    with nc.Block() as block:
        @block.vector
        def _(dve):
            Line(dve, ch.S["vector_step"])(dve.memset(vpad, 0.0))
    for j in range(4):
        def part_a(a, act, ps, sig, j=j):
            a(act.activation(sig_g[:, j, :], ps, ACT.Sigmoid), sig)

        def part_v(v_, dve, ps, sig, j=j):
            v_(dve.tensor_tensor(vpad[:, j, 15:15 + T], a_[:, j, :], sig_g[:, j, :], MUL), sig)
        tiles.append((1, "T", j * P, ch.hT, T, (part_a, part_v)))
    tiles += [(2, "T", j * P, ch.hT, T, copy_to(q[:, j, :])) for j in range(4)]
    tiles += [(3, "T", j * P, ch.hT, T, copy_to(k[:, j, 0:T])) for j in range(4)]
    tiles += [(3, "T", j * P, hcT, L, copy_to(k[:, j, T:T + L])) for j in range(4)]
    tiles += [(4, "N", s * P, ch.hT, T, copy_to(v[:, s, :])) for s in range(4)]
    tiles += [(4, "N", s * P, hcT, L, copy_to(v[:, 4 + s, :])) for s in range(2)]
    project(ch, 5, tiles, vector_after=conv_taps(ch, vpad, y), norm=norm)
    conv_norm(ch, y)
    neighbourhood_attention(ch)
    tiles = []
    for b in range(2):
        for j in range(4):
            def part(v_, dve, ps, sig, n=4 * b + j):
                v_(dve.scalar_tensor_tensor(ch.xT[:, n, :], ps, ch.mod2[:, 16 + n, 0:1], ch.xT[:, n, :], MUL, ADD), sig)
            tiles.append((b, "T", j * P, ch.slot(7, 2), T, (None, part)))
    norm = Norm(ch, ch.xT, ch.hT, T, [ch.sm[:, 40 + i:41 + i] for i in range(8)],
                [ch.mod2[:, 24 + i, 0:1] for i in range(8)], 7, ch.slot(0), ch.slot(1))
    tensor, scalar = beside_stream(norm)
    project(ch, 2, tiles, banks=7, tensor_beside=tensor, scalar_beside=scalar)
    return norm


def route(ch):
    nc, ps = ch.nc, ch.ps
    wr = ch.slot(2).rearrange("p a t -> p (a t)")[:, 0:128].rearrange("p (k e) -> p k e", e=E_)
    hN = ch.slot(0, 2).rearrange("p a t -> p (a t)").rearrange("p (s d) -> p s d", d=D)
    aff, place = (ch.slot(3)[:, i, 0:64].rearrange("p (s e) -> p s e", e=E_) for i in (0, 1))
    row, sel, pos = (ch.slot(4)[0:E_, i, :] for i in (0, 1, 2))
    best = ch.sm[0:E_, 152:160]
    st = ch.sm[:, 96:104].rearrange("p (i s) -> p i s", s=4)
    aux, turned, copied, steps, expd = ch.counters("aux_loaded", "route_turned", "route_copied", "route_steps",
                                                  "route_exp")
    with nc.Block() as block:
        @block.sync
        def _(sp):
            sp.dma_start(wr, ch.A["w_router_2"].rearrange("(k p) e -> p k e", p=P)).then_inc(aux.sem, 16)
            aux.total += 16

        @block.tensor
        def _(pe):
            pe.wait_ge(aux.sem, aux.at(16))
            for s in range(4):
                for k in range(KD):
                    ins = pe.matmul(ps[:, 0, s * E_:(s + 1) * E_], ch.hT[:, k, s * P:(s + 1) * P], wr[:, k, :],
                                    start=k == 0, stop=k == KD - 1)
            ins.then_inc(turned.sem, 1)
            for n in range(8):
                if n >= 4:
                    pe.wait_ge(copied.sem, copied.at(n - 3))
                for j in range(4):
                    k, s = 4 * (n % 2) + j, n // 2
                    ins = pe.transpose(ps[:, 1 + n % 4, j * P:(j + 1) * P], ch.hT[:, k, s * P:(s + 1) * P], ch.m("ident"))
                ins.then_inc(turned.sem, 1)
            pe.wait_ge(steps.sem, steps.at(1))
            for s in range(4):
                ins = pe.transpose(ps[0:E_, 5, s * P:(s + 1) * P], aff[:, s, :], ch.m("ident"))
            ins.then_inc(turned.sem, 1)
            pe.wait_ge(steps.sem, steps.at(2))
            for s in range(4):
                ins = pe.transpose(ps[:, 6, s * E_:(s + 1) * E_], pos[:, s * P:(s + 1) * P], ch.m("ident")[0:E_, 0:E_])
            ins.then_inc(turned.sem, 1)
            turned.total += 11

        @block.scalar
        def _(act):
            a = Line(act, ch.S["scalar_step"])
            a.after(expd, 1)
            a(act.activation(aff, aff, ACT.Exp), expd)
            for n in range(8):
                a.after(turned, n + 2)
                a(act.copy(hN[:, n // 2, (n % 2) * 512:(n % 2 + 1) * 512], ps[:, 1 + n % 4, :]), copied)

        @block.vector
        def _(dve):
            v = Line(dve, ch.S["vector_step"])
            v.after(turned, 1)
            logits = ps[:, 0, 0:64].rearrange("p (s e) -> p s e", e=E_)
            wide = st[:, 0, :].unsqueeze(2).to_broadcast([P, 4, E_])
            v(dve.tensor_reduce(st[:, 0, :], logits, AXX, MAX))
            v(dve.tensor_tensor(aff, logits, wide, SUB), expd)
            v.after(expd, 2)
            v(dve.tensor_reduce(st[:, 0, :], aff, AXX, ADD))
            v(dve.reciprocal(st[:, 0, :], st[:, 0, :]))
            v(dve.tensor_tensor(aff, aff, wide, MUL), steps)
            v.after(turned, 10)
            v(dve.tensor_copy(row, ps[0:E_, 5, :]))
            for _ in range(CAP // 8):
                v(dve.max(best, row))
                v(dve.match_replace(row, best, row, -1.0))
            v(dve.tensor_scalar(sel, row, 0.0, None, ALU.is_lt))
            v(dve.tensor_tensor_scan(pos, ch.eps[0:E_, 3:4].to_broadcast([E_, T]), sel, 0.0, MUL, ADD))
            v(dve.tensor_tensor(pos, pos, sel, MUL), steps)
            v.after(turned, 11)
            v(dve.tensor_copy(place, ps[:, 6, 0:64].rearrange("p (s e) -> p s e", e=E_)))


def experts(ch):
    nc, ps = ch.nc, ch.ps
    hN = ch.slot(0, 2).rearrange("p a t -> p (a t)").rearrange("p (s d) -> p s d", d=D)
    aff, place = (ch.slot(3)[:, i, 0:64].rearrange("p (s e) -> p s e", e=E_) for i in (0, 1))
    oh = ch.slot(4)[:, 0, 0:256].rearrange("p (s c) -> p s c", c=CAP)
    pw = ch.slot(4)[:, 1, :].rearrange("p (s c) -> p s c", c=P)
    pwT = ch.slot(4)[:, 2, :], ch.slot(4)[:, 3, :]
    xs = ch.slot(5)[:, 0, :].rearrange("p (k c) -> p k c", c=CAP)
    sil = ch.slot(6)[:, 0:2, :]
    hid = ch.slot(6)[:, 2:4, :]
    hidT = ch.slot(7)[:, 0:2, :].rearrange("p a (i q c) -> p a i q c", q=2, c=CAP)
    y = ch.slot(7)[:, 2, :]
    iota = ch.m("iota")
    first = ch.used
    norm = Norm(ch, ch.xT, ch.xT, T, [ch.v("norm_final_g_2", i) for i in range(8)], None, 0, ch.slot(8), ch.slot(9))
    (oh_ready, gathered, xs_ready, gate_up, silus, hid_ready, turned, hidT_ready, down, y_ready,
     pw_ready, pw_turned, pwT_ready, scattered, added) = ch.counters(
        "onehot_ready", "gathered", "xs_ready", "gate_up_done", "silus", "hidden_ready", "hidden_turned",
        "hiddenT_ready", "down_done", "y_ready", "scatter_ready", "scatter_turned", "scatterT_ready", "scattered",
        "residual_added")
    for e in range(E_):
        for i in range(8):
            ch.free_at[first + 12 * e + i] = (gate_up.sem, gate_up.at(4 * e + i // 2 + 1))
        for i in range(4):
            ch.free_at[first + 12 * e + 8 + i] = (down.sem, down.at(4 * e + i + 1))

    with nc.Block() as block:
        @block.sync
        def _(sp):
            ch.stream(sp, first + 12 * E_ + RING)

        @block.tensor
        def _(pe):
            def gather(e):
                pe.wait_ge(oh_ready.sem, oh_ready.at(e + 1))
                if e > 0:
                    pe.wait_ge(xs_ready.sem, xs_ready.at(e))
                for k in range(KD):
                    for s in range(4):
                        ins = pe.matmul(ps[:, 0, k * CAP:(k + 1) * CAP], hN[:, s, k * P:(k + 1) * P], oh[:, s, :],
                                        start=s == 0, stop=s == 3)
                ins.then_inc(gathered.sem, 1)
                gathered.total += 1
                pe.wait_ge(pw_ready.sem, pw_ready.at(e + 1))
                if e > 1:
                    pe.wait_ge(added.sem, added.at(8 * (e - 1)))
                elif e == 1:
                    pe.wait_ge(pwT_ready.sem, pwT_ready.at(1))
                for s in range(4):
                    ins = pe.transpose(ps[:, 5, s * P:(s + 1) * P], pw[:, s, :], ch.m("ident"))
                ins.then_inc(pw_turned.sem, 1)
                pw_turned.total += 1

            def gate_and_up(e, n):
                b0 = first + 12 * e + 2 * n
                w = [ch.block_view(b0 + q) for q in range(2)]
                ch.block_wait(pe, b0)
                ch.block_wait(pe, b0 + 1)
                if e > 0:
                    pe.wait_ge(hid_ready.sem, hid_ready.at(2 * e - 1 + n // 2))
                for k in range(KD):
                    for q in range(2):
                        ins = pe.matmul(ps[64 * q:64 * q + 64, 1 + n, :], xs[:, k, :], w[q][:, k, :],
                                        start=k == 0, stop=k == KD - 1)
                ins.then_inc(gate_up.sem, 1)
                gate_up.total += 1

            def scatter(e):
                pe.wait_ge(y_ready.sem, y_ready.at(e + 1))
                for n in range(8):
                    q, bank = n // 4, 5 + n % 2
                    if n < 2:
                        pe.wait_ge(hidT_ready.sem, hidT_ready.at(2 * e + 2))
                    else:
                        pe.wait_ge(added.sem, added.at(8 * e + n - 1))
                    rows = slice(64 * q, 64 * q + 64)
                    pe.matmul(ps[:, bank, :], y[rows, (n % 4) * P:(n % 4 + 1) * P], pwT[e % 2][rows, :], start=True,
                              stop=True).then_inc(scattered.sem, 1)
                    scattered.total += 1

            gather(0)
            for e in range(E_):
                pe.wait_ge(xs_ready.sem, xs_ready.at(e + 1))
                gate_and_up(e, 0)
                gate_and_up(e, 1)
                if e > 0:
                    scatter(e - 1)
                gate_and_up(e, 2)
                gate_and_up(e, 3)
                if e > 0:
                    pe.wait_ge(added.sem, added.at(8 * e))
                pe.wait_ge(hid_ready.sem, hid_ready.at(2 * e + 1))
                for i in range(4):
                    ins = pe.transpose(ps[:, 6, i * P:(i + 1) * P], hid[:, 0, i * P:(i + 1) * P], ch.m("ident"))
                ins.then_inc(turned.sem, 1)
                if e + 1 < E_:
                    gather(e + 1)
                pe.wait_ge(hid_ready.sem, hid_ready.at(2 * e + 2))
                pe.wait_ge(pwT_ready.sem, pwT_ready.at(min(e + 2, E_)))
                for i in range(4):
                    ins = pe.transpose(ps[:, 5, i * P:(i + 1) * P], hid[:, 1, i * P:(i + 1) * P], ch.m("ident"))
                ins.then_inc(turned.sem, 1)
                turned.total += 2
                if e > 0:
                    pe.wait_ge(y_ready.sem, y_ready.at(e))
                for i in range(4):
                    w = ch.block_view(first + 12 * e + 8 + i)
                    ch.block_wait(pe, first + 12 * e + 8 + i)
                    if i % 2 == 0:
                        pe.wait_ge(hidT_ready.sem, hidT_ready.at(2 * e + 1 + i // 2))
                    for t in range(4):
                        f = 4 * i + t
                        for q in range(2):
                            ins = pe.matmul(ps[64 * q:64 * q + 64, 7, :], hidT[:, f // 8, f % 4, (f // 4) % 2, :],
                                            w[:, t, q * 512:(q + 1) * 512], start=f == 0, stop=f == 15)
                    ins.then_inc(down.sem, 1)
                    down.total += 1
            scatter(E_ - 1)
            for k in range(KD):
                norm.sum(k)(pe)

        @block.scalar
        def _(act):
            a = Line(act, ch.S["scalar_step"])

            def gathered_parts(e):
                a.after(gathered, e + 1)
                a(act.copy(xs, ps[:, 0, :].rearrange("p (k c) -> p k c", c=CAP)), xs_ready)
                a.after(pw_turned, e + 1)
                a(act.copy(pwT[e % 2], ps[:, 5, :]), pwT_ready)

            gathered_parts(0)
            for e in range(E_):
                for p in range(2):
                    a.after(gate_up, 4 * e + 2 * p + 1)
                    if e > 0:
                        a.after(hid_ready, 2 * e - 1 + p)
                    a(act.activation(sil[:, p, :], ps[:, 1 + 2 * p, :], ACT.Silu), silus)
                a.after(turned, 2 * e + 1)
                a(act.copy(hidT[:, 0], ps[:, 6, :].rearrange("p (i q c) -> p i q c", q=2, c=CAP)), hidT_ready)
                if e + 1 < E_:
                    gathered_parts(e + 1)
                a.after(turned, 2 * e + 2)
                a(act.copy(hidT[:, 1], ps[:, 5, :].rearrange("p (i q c) -> p i q c", q=2, c=CAP)), hidT_ready)
            for k in range(KD):
                a.after(added, 8 * (E_ - 1) + k + 1)
                norm.square(k)(a, act)

        @block.vector
        def _(dve):
            v = Line(dve, ch.S["vector_step"])

            def selectors(e):
                if e > 0:
                    v.after(pw_turned, e)
                for s in range(4):
                    v(dve.tensor_scalar(oh[:, s, :], iota[:, 0:CAP], place[:, s, e:e + 1], None, ALU.is_equal),
                      oh_ready if s == 3 else None)
                for s in range(4):
                    v(dve.tensor_scalar(pw[:, s, :], iota, place[:, s, e:e + 1], aff[:, s, e:e + 1], ALU.is_equal, MUL),
                      pw_ready if s == 3 else None)

            def hidden(e, p):
                v.after(gate_up, 4 * e + 2 * p + 2)
                v.after(silus, 2 * e + p + 1)
                if e > 0:
                    v.after(turned, 2 * e - 1 + p)
                v(dve.tensor_tensor(hid[:, p, :], sil[:, p, :], ps[:, 2 + 2 * p, :], MUL), hid_ready)

            def add(e):
                for n in range(8):
                    v.after(scattered, 8 * e + n + 1)
                    v(dve.scalar_tensor_tensor(ch.xT[:, n, :], ps[:, 5 + n % 2, :], ch.mod2[:, 40 + n, 0:1],
                                               ch.xT[:, n, :], MUL, ADD), added)

            selectors(0)
            for e in range(E_):
                hidden(e, 0)
                if e > 0:
                    add(e - 1)
                if e + 1 < E_:
                    selectors(e + 1)
                hidden(e, 1)
                v.after(down, 4 * e + 4)
                v(dve.tensor_copy(y, ps[:, 7, :]), y_ready)
            add(E_ - 1)
    ch.used = first + 12 * E_
    return norm


def block2(ch, norm):
    norm = block2_mixer(ch, norm)
    finish_norm(ch, norm)
    route(ch)
    norm = experts(ch)
    following = Norm(ch, ch.xT, ch.hT, T, [ch.v("norm_g_even_3", i) for i in range(8)], None, 1, ch.slot(8),
                     ch.slot(10), "following_")
    finish_norm(ch, norm, following)
    return following


def block2_plan(A):
    out = blocks(A["w_in_2"], 0, 2560) + blocks(A["w_out_2"], 0, 1024)
    for e in range(E_):
        g, u = blocks(A["w_gate_2"][e], 0, FE), blocks(A["w_up_2"][e], 0, FE)
        out += g[0:2] + u[0:2] + g[2:4] + u[2:4]
        for i in range(4):
            w = A["w_down_2"][e, i * 512:(i + 1) * 512, :].rearrange("(k p) c -> p k c", p=P)
            out.append(([(w, 0, D)], 4, D))
    return out



def even_gating(ch):
    nc, ps = ch.nc, ch.ps
    u, z = ch.slot(0, 2), ch.slot(4, 2)
    v = ch.slot(2, 2).rearrange("p a t -> p (a t)").rearrange("p (s d) -> p s d", d=D)
    c = ch.slot(6, 2).rearrange("p a t -> p (a t)")
    gain, shift, bs, ws = c[:, 0:D], c[:, D:2 * D], c[:, 2 * D:2 * D + 512], c[:, 2 * D + 512:3 * D]
    tmp = ch.slot(8)
    stats = ch.sm[:, 0:48].rearrange("p (s i c) -> p s i c", s=4, c=6)
    mv = ch.sm[:, 48:56].rearrange("p (s c) -> p s c", c=2)
    loaded, var_ready, root, normed, mixed = ch.counters("aux_loaded", "var_ready", "ln_root", "ln_normed", "mixed")
    with nc.Block() as block:
        @block.sync
        def _(sp):
            sp.dma_start(c[:, 0:3 * D], ch.A["gmlp"]).then_inc(loaded.sem, 16)
            loaded.total += 16

        @block.vector
        def _(dve):
            line = Line(dve, ch.S["vector_step"])
            for s in range(4):
                for i in range(2):
                    line(dve.bn_stats(stats[:, s, i, :], v[:, s, i * 512:(i + 1) * 512]))
                line(dve.bn_aggr(mv[:, s, :], stats[:, s].rearrange("p i c -> p (i c)")),
                     var_ready if s == 3 else None)
            line.after(root, 1)
            line(dve.reciprocal(mv[:, :, 1], mv[:, :, 1]))
            line.after(loaded, 16)
            for s in range(4):
                line(dve.tensor_scalar(v[:, s, :], v[:, s, :], mv[:, s, 0:1], mv[:, s, 1:2], SUB, MUL))
                line(dve.tensor_tensor(v[:, s, :], v[:, s, :], gain, MUL))
                line(dve.tensor_tensor(v[:, s, :], v[:, s, :], shift, ADD), normed)
            for k in range(8):
                g = k // 2
                b = bs[:, g * P:(g + 1) * P].unsqueeze(1).to_broadcast([P, 4, P])
                line.after(mixed, k + 1)
                t = tmp[:, k % 4, :]
                line(dve.tensor_tensor(t.rearrange("p (s t) -> p s t", t=P),
                                       ps[:, k, :].rearrange("p (s t) -> p s t", t=P), b, ADD))
                line(dve.tensor_tensor(t, t, u[:, k, :], MUL))
                line(dve.tensor_tensor(u[:, k, :], t, z[:, k, :], MUL))

        @block.scalar
        def _(act):
            a = Line(act, ch.S["scalar_step"])
            a.after(var_ready, 1)
            a(act.activation(mv[:, :, 1], mv[:, :, 1], ACT.Sqrt, bias=ch.eps[:, 0:1]), root)

        @block.tensor
        def _(pe):
            pe.wait_ge(loaded.sem, loaded.at(16))
            pe.wait_ge(normed.sem, normed.at(4))
            for k in range(8):
                g = k // 2
                for s in range(4):
                    ins = pe.matmul(ps[:, k, s * P:(s + 1) * P], v[:, s, k * P:(k + 1) * P], ws[:, g * P:(g + 1) * P],
                                    start=True, stop=True)
                ins.then_inc(mixed.sem, 1)
                mixed.total += 1


def window_attention(ch):
    q, kv, gate = ch.slot(4, 2), ch.slot(6), ch.slot(2, 2)
    k, v = kv[:, 0:2, :], kv[:, 2:4, :].rearrange("p a t -> p (a t)").rearrange("p (s c) -> p s c", c=256)
    band = ch.slot(7).rearrange("p a t -> p (a t)")
    dist, mask = band[:, 0:384], band[:, 384:768]
    bias = [band[:, 768 + i * 384:768 + (i + 1) * 384] for i in range(2)]
    loaded = ch.counter("bias_loaded")

    def load(sp, softened):
        sp.dma_start(band[:, 0:768], ch.A["band"]).then_inc(loaded.sem, 16)
        loaded.total += 16

    units = []
    for h in range(8):
        g = h // 4

        def prepare(line, dve, h=h):
            if h == 0:
                line.after(loaded, 16)
            line(dve.scalar_tensor_tensor(bias[h % 2], dist, -2.0 ** -(h + 1), mask, MUL, ADD))
        for s in range(4):
            t0, t1 = max(s - 1, 0), min(s + 2, 4)
            n, c0 = (t1 - t0) * P, 128 if s == 0 else 0

            def close(line, dve, psum, sig, h=h):
                line(dve.tensor_tensor(gate[:, h, :], psum, gate[:, h, :], MUL), sig)
            units.append(dict(
                q=q[:, h, s * P:(s + 1) * P], keys=[(k[:, g, t0 * P:t1 * P], 0)],
                biases=[(bias[h % 2][:, c0:c0 + n], 0, n)], plain=[], cols=n,
                values=[v[:, t, g * P:(g + 1) * P] for t in range(t0, t1)], rows=slice(0, P), col=s * P,
                close=close if s == 3 else None, prepare=prepare if s == 0 else None, sink=ch.v("attn_sink_3", h)))
    attention(ch, units, P ** -0.5, sinks=True, sync_body=load)


def share_tiles(ch, source, per, nblocks):
    tiles = []
    for b in range(nblocks):
        for j in range(per):
            def part(v, dve, ps, sig, n=per * b + j):
                v(dve.tensor_tensor(ch.xT[:, n, :], ps, ch.xT[:, n, :], ADD), sig)
            tiles.append((b, "T", j * P, source, T, (None, part)))
    return tiles


def add_to_stream(ch, source, per, nblocks, norm):
    tensor, scalar = beside_stream(norm)
    project(ch, nblocks, share_tiles(ch, source, per, nblocks), banks=7, tensor_beside=tensor, scalar_beside=scalar)
    return norm


def even_layer(ch, norm):
    u, z = ch.slot(0, 2), ch.slot(4, 2)
    v = ch.slot(2, 2).rearrange("p a t -> p (a t)").rearrange("p (s d) -> p s d", d=D)
    tiles = []
    for b in range(2):
        tiles += [(b, "T", j * P, ch.hT, T, copy_to(u[:, 4 * b + j, :])) for j in range(4)]
    for b in range(2):
        tiles += [(2 + b, "N", s * P, ch.hT, T, copy_to(v[:, s, b * 512:(b + 1) * 512])) for s in range(4)]
    for b in range(2):
        tiles += [(4 + b, "T", j * P, ch.hT, T, act_to(z[:, 4 * b + j, :], ACT.Silu)) for j in range(4)]
    project(ch, 6, tiles, norm=norm)
    even_gating(ch)
    q, kv, gate = ch.slot(4, 2), ch.slot(6), ch.slot(2, 2)
    vb = kv[:, 2:4, :].rearrange("p a t -> p (a t)").rearrange("p (s c) -> p s c", c=256)
    tiles = []
    for b in range(2):
        tiles += [(b, "T", j * P, ch.hT, T, copy_to(q[:, 4 * b + j, :])) for j in range(4)]
    tiles += [(2, "T", j * P, ch.hT, T, copy_to(kv[:, j, :])) for j in range(2)]
    tiles += [(2, ("N", 256, 512), s * P, ch.hT, T, copy_to(vb[:, s, :])) for s in range(4)]
    for b in range(2):
        tiles += [(3 + b, "T", j * P, ch.hT, T, act_to(gate[:, 4 * b + j, :], ACT.Silu)) for j in range(4)]
    project(ch, 5, tiles)
    window_attention(ch)
    return add_to_stream(ch, ch.slot(0, 4), 2, 4, Norm(
        ch, ch.xT, ch.hT, T, [ch.v("norm_g_odd_3", i) for i in range(8)], None, 7, ch.slot(9), ch.slot(0)))



def odd_bounds(ch):
    with ch.nc.Block() as block:
        @block.vector
        def _(dve):
            v = Line(dve, ch.S["vector_step"])
            for i, n in enumerate(("hgrn_gamma_fwd_3", "hgrn_gamma_bwd_3")):
                v(dve.tensor_tensor(ch.sm[:, 16 * i:16 * i + 16], ch.v(n, 16, 16), ch.v(n, 0, 16), SUB))
    with ch.nc.Block() as block:
        @block.scalar
        def _(act):
            a = Line(act, ch.S["scalar_step"])
            a(act.activation(ch.sm[:, 32:64], ch.sm[:, 0:32], ACT.Sigmoid, scale=-1.0))
            a(act.activation(ch.sm[:, 0:32], ch.sm[:, 0:32], ACT.Sigmoid))


def odd_group(ch, G, norm):
    ps = ch.ps
    F, B, I, Z = [ch.slot(i) for i in (1, 2, 3, 4)]
    qd, kd, ed = (ch.slot(5), ch.slot(8)), (ch.slot(6), ch.slot(9)), (ch.slot(7), ch.slot(10))
    keep = ch.slot(11)[:, 0, :]
    homes = (ch.slot(0), ch.slot(1)), (ch.slot(2), ch.slot(11))
    end = [ch.sm[:, 64 + 32 * d:96 + 32 * d] for d in range(2)]

    def piece(d, i):
        return homes[d][i // 4][:, i % 4, :].rearrange("p (h v) -> p h v", v=P)

    def state(d, c):
        return piece(d, c - 1 if d == 0 else c)
    aT = [piece(0, 7), piece(1, 7)]
    by_dve = ch.S["tile_vector_done"]
    logged, scanned, decayed, ended = ch.counters("f_logged", "decay_scanned", "decay_exponents", "end_keys_ready")
    turned, natural, kv, stepped, grams, masked, summed, squared, sums, rooted, done = ch.counters(
        "end_keys_turned", "end_keys_natural", "kv_products", "states_stepped", "odd_grams", "odd_masked",
        "odd_summed", "odd_squared", "odd_sums", "odd_rooted", "odd_heads_done")

    tiles = share_tiles(ch, Z, 8, 1) if G else []
    n0 = len(tiles)
    b0 = 1 if G else 0
    tF, tB, tI, tQ, tZ = [n0 + 4 * i for i in range(5)]
    for d, dst in ((0, F), (1, B)):
        for j in range(4):
            lb = ch.sm[:, 16 * d + 4 * G + j:16 * d + 4 * G + j + 1]
            om = ch.sm[:, 32 + 16 * d + 4 * G + j:33 + 16 * d + 4 * G + j]

            def part_a(a, act, ps, sig, o=dst[:, j, :]):
                a(act.activation(o, ps, ACT.Sigmoid), sig)

            def part_v(v, dve, ps, sig, o=dst[:, j, :], k=kd[d][:, j, :], lb=lb, om=om):
                v(dve.tensor_scalar(o, o, om, lb, MUL, ADD))
                v(dve.tensor_scalar(k, o, -1.0, 1.0, MUL, ADD), sig)
            tiles.append((b0 + d, "T", j * P, ch.hT, T, (part_a, part_v)))
    tiles += [(b0 + 2, "N", s * P, ch.hT, T, copy_to(I[:, s, :])) for s in range(4)]
    for j in range(4):
        tmp = aT[j % 2].rearrange("p h v -> p (h v)")

        def q_a(a, act, ps, sig, j=j, tmp=tmp):
            if j >= 2:
                a.after(by_dve, n0 + 7 + j)
            a(act.activation(tmp, ps, ACT.Silu), sig)

        def q_v(v, dve, ps, sig, j=j, tmp=tmp):
            for d in range(2):
                v(dve.tensor_tensor(qd[d][:, j, :], qd[d][:, j, :], tmp, MUL), sig if d else None)
        tiles.append((b0 + 3, "T", j * P, ch.hT, T, (q_a, q_v)))
    tiles += [(b0 + 4, "T", j * P, ch.hT, T, act_to(Z[:, j, :], ACT.Silu)) for j in range(4)]

    def turn(d):
        def part(pe):
            pe.wait_ge(ended.sem, ended.at(d + 1))
            if d:
                pe.wait_ge(natural.sem, natural.at(4))
            for s in range(4):
                for h in range(4):
                    ins = pe.transpose(ps[:, 3 + s, h * P:(h + 1) * P], ed[d][:, h, s * P:(s + 1) * P],
                                       ch.m("ident"))
            ins.then_inc(turned.sem, 1)
            turned.total += 1
        return part

    def products(i):
        def part(pe):
            for d in range(2):
                c = i if d == 0 else 7 - i
                s, rows = c // 2, slice(64 * (c % 2), 64 * (c % 2) + 64)
                if i == 0:
                    pe.wait_ge(natural.sem, natural.at(8))
                else:
                    pe.wait_ge(stepped.sem, stepped.at(2 * i - 1 + d))
                for h in range(4):
                    cols = slice(h * P, (h + 1) * P)
                    ins = pe.matmul(ps[:, 3 + d, cols], ed[d][rows, s, cols], I[rows, s, cols], start=True, stop=True)
                ins.then_inc(kv.sem, 1)
                kv.total += 1
        return part

    def gram(h):
        def part(pe):
            pe.wait_ge(by_dve.sem, by_dve.at(n0 + 9 + h))
            if h >= 1:
                pe.wait_ge(masked.sem, masked.at(h))
            for d in range(2):
                for s in range(4):
                    cols = slice(s * P, (s + 1) * P)
                    ins = pe.matmul(ps[:, 5 + d, cols], kd[d][:, h, cols], qd[d][:, h, cols], start=True, stop=True)
            ins.then_inc(grams.sem, 1)
            grams.total += 1
        return part

    def output(h):
        def part(pe):
            pe.wait_ge(stepped.sem, stepped.at(14))
            pe.wait_ge(masked.sem, masked.at(h + 1))
            if h >= 2:
                pe.wait_ge(done.sem, done.at(h - 1))
            bank = 3 + h % 2
            for s in range(4):
                pe.matmul(ps[:, bank, s * P:(s + 1) * P], I[:, s, h * P:(h + 1) * P], aT[h % 2][:, s, :],
                          start=s == 0, stop=False, skip_group_check=True)
            for c in range(8):
                cols = slice(c * 64, (c + 1) * 64)
                for d in range(2):
                    if (c > 0) if d == 0 else (c < 7):
                        ins = pe.matmul(ps[:, bank, cols], state(d, c)[:, h, :], qd[d][:, h, cols], start=False,
                                        stop=c == 7, skip_group_check=True)
            ins.then_inc(summed.sem, 1)
            summed.total += 1
        return part

    def norm_sum(h):
        def part(pe):
            pe.wait_ge(squared.sem, squared.at(h + 1))
            if h >= 1:
                pe.wait_ge(rooted.sem, rooted.at(h))
            pe.matmul(ps[:, 7, :], ch.m("ones"), qd[0][:, h, :], start=True, stop=True).then_inc(sums.sem, 1)
            sums.total += 1
        return part

    def log(d):
        def part(a, act):
            a.after(by_dve, n0 + 4 * d + 4)
            x = (F, B)[d]
            a(act.activation(x, x, ACT.Ln), logged)
        return part

    def exponents(d):
        def part(a, act):
            a.after(scanned, d + 1)
            x = (F, B)[d]
            a(act.activation(qd[d], x, ACT.Exp))
            a(act.activation(ed[d], x, ACT.Exp, scale=-1.0), decayed)
        return part

    def to_natural(d):
        def part(a, act):
            a.after(turned, d + 1)
            for s in range(4):
                a(act.copy(ed[d][:, s, :], ps[:, 3 + s, :]), natural)
        return part

    def square(h):
        def part(a, act):
            a.after(summed, h + 1)
            a(act.square(qd[0][:, h, :], ps[:, 3 + h % 2, :]), squared)
        return part

    def root(h):
        def part(a, act):
            a.after(sums, h + 1)
            a(act.activation(qd[1][:, h, :], ps[:, 7, :], ACT.Sqrt, bias=ch.eps[:, 0:1], scale=1.0 / P), rooted)
        return part

    def scan(d):
        def part(v, dve):
            if d == 0:
                v(dve.memset(keep, 1.0))
                v(dve.memset(keep.rearrange("p (c t) -> p c t", t=64)[:, :, 0:1], 0.0))
            v.after(logged, d + 1)
            for j in range(4):
                x = F[:, j, :] if d == 0 else B[:, j, ::-1]
                v(dve.tensor_tensor_scan(x, keep, x, 0.0, MUL, ADD), scanned if j == 3 else None)
        return part

    def end_keys(d):
        def part(v, dve):
            v.after(decayed, d + 1)
            v(dve.tensor_copy(end[d].rearrange("p (j c) -> p j c", c=8),
                              qd[d].rearrange("p j (c t) -> p j c t", t=64)[:, :, :, 0 if d else 63]))
            v(dve.tensor_tensor(kd[d], kd[d], ed[d], MUL))
            v(dve.tensor_tensor(ed[d].rearrange("p j (c t) -> p (j c) t", t=64),
                                kd[d].rearrange("p j (c t) -> p (j c) t", t=64),
                                end[d].unsqueeze(2).to_broadcast([P, 32, 64]), MUL), ended)
        return part

    def step(i):
        def part(v, dve):
            for d in range(2):
                c = i if d == 0 else 7 - i
                new = state(d, c + 1 if d == 0 else c - 1)
                got = ps[:, 3 + d, :].rearrange("p (h v) -> p h v", v=P)
                e = end[d].rearrange("p (j c) -> p j c", c=8)[:, :, c:c + 1]
                if i == 0:
                    v.after(kv, 2 * i + d + 1)
                    v(dve.tensor_copy(new, got), stepped)
                else:
                    v(dve.tensor_tensor(new, state(d, c), e.to_broadcast([P, 4, P]), MUL))
                    v.after(kv, 2 * i + d + 1)
                    v(dve.tensor_tensor(new, new, got, ADD), stepped)
        return part

    def mask(h):
        def part(v, dve):
            v.after(grams, h + 1)
            if h >= 2:
                v.after(summed, h - 1)
            b = [ps[:, 5 + d, :].rearrange("p (s t) -> p s t", t=P) for d in range(2)]
            v(dve.tensor_tensor(b[1], b[1], ch.m4("mLI"), MUL))
            v(dve.tensor_tensor(aT[h % 2], b[0], ch.m4("mUI"), MUL))
            v(dve.tensor_tensor(aT[h % 2], aT[h % 2], b[1], ADD), masked)
        return part

    def finish(h):
        def part(v, dve):
            t = qd[1][:, h, :]
            v.after(rooted, h + 1)
            v(dve.reciprocal(t, t))
            v(dve.scalar_tensor_tensor(t, t, ch.v("hgrn_head_norm_g_3", 4 * G + h), Z[:, h, :], MUL, MUL))
            v(dve.tensor_tensor(Z[:, h, :], ps[:, 3 + h % 2, :], t, MUL), done)
        return part

    project(
        ch, b0 + 5, tiles, banks=3, norm=norm,
        tensor_beside={
            tI + 1: turn(0), tI + 3: turn(1), tQ: products(0), tQ + 0.5: products(1), tQ + 1: products(2),
            tQ + 1.5: products(3), tQ + 2: products(4), tQ + 2.5: products(5), tQ + 3: seq(products(6), gram(0)),
            tZ: gram(1), tZ + 0.5: output(0), tZ + 1: seq(gram(2), norm_sum(0)),
            tZ + 1.5: output(1), tZ + 2: seq(gram(3), norm_sum(1), output(2)),
            tZ + 2.5: seq(output(3), norm_sum(2)), tZ + 3: norm_sum(3)},
        scalar_beside={
            tB: log(0), tB + 2: exponents(0), tI: log(1), tI + 1: seq(exponents(1), to_natural(0)),
            tI + 3: to_natural(1), tZ: square(0), tZ + 1: seq(root(0), square(1)),
            tZ + 2: seq(root(1), square(2), square(3), root(2)), tZ + 3: root(3)},
        vector_beside={
            tB + 1: scan(0), tB + 3: seq(end_keys(0), scan(1), end_keys(1)),
            tQ: seq(step(0), step(1)), tQ + 1: seq(step(2), step(3)), tQ + 2: seq(step(4), step(5)),
            tQ + 3: seq(step(6), *[mask(0), mask(1), mask(2), finish(0), mask(3), finish(1), finish(2), finish(3)])})


def odd_layer(ch, norm):
    odd_bounds(ch)
    for G in range(4):
        odd_group(ch, G, norm if G == 0 else None)
    return add_to_stream(ch, ch.slot(4), 8, 1, Norm(
        ch, ch.xT, ch.xT, T, [ch.v("final_norm_g_3", i) for i in range(8)], None, 7, ch.slot(0), ch.slot(1)))


def block3(ch, norm):
    norm = even_layer(ch, norm)
    return odd_layer(ch, norm)


def block3_plan(A):
    out = blocks(A["w_in_even_3"], 0, 5632) + blocks(A["w_out_even_3"], 0, D)
    w, o = A["w_in_odd_3"], A["w_out_odd_3"]
    for G in range(4):
        for i in (1, 2, 3, 0, 4):
            out += blocks(w, i * 2048 + G * 512, i * 2048 + (G + 1) * 512)
        out.append(([(o[G * 512:(G + 1) * 512, :].rearrange("(k p) c -> p k c", p=P), 0, D)], 4, D))
    return out


def program(nc, A, out):
    ctx = ExitStack()
    with ctx:
        ch = Chip(nc, ctx, A, plan(A))
        norm = block1(ch)
        norm = block2(ch, norm)
        norm = block3(ch, norm)
        write_out(ch, norm, out)


def plan(A):
    return block1_plan(A) + block2_plan(A) + block3_plan(A)


def write_out(ch, norm, out):
    done = ch.counter("output_written")
    rows = out.rearrange("(k p) t -> p k t", p=P)
    with ch.nc.Block() as block:
        @block.scalar
        def _(act):
            norm.root(Line(act, ch.S["scalar_step"]), act)

        @block.vector
        def _(dve):
            norm.scale(Line(dve, ch.S["vector_step"]), dve)

        @block.sync
        def _(sp):
            for k in range(0, KD, 2):
                norm.wait(sp, k + 1)
                sp.dma_start(rows[:, k:k + 2, :], ch.xT[:, k:k + 2, :]).then_inc(done.sem, 16)
            sp.wait_ge(done.sem, 16 * (KD // 2))


WEIGHTS = ["w_ada", "w_in", "w_up", "a_up", "w_a_out", "w_b_out", "w_o"]
WEIGHTS_2 = ["w_mod", "w_in", "w_out", "w_router", "w_gate", "w_up", "w_down"]
WEIGHTS_3 = ["w_in_even", "w_out_even", "w_in_odd", "w_out_odd"]


def laid_out(inputs):
    cols = []
    for name, w in VECTORS:
        a = np.asarray(inputs[name])
        if name in ("q_gain", "k_gain"):
            a = np.concatenate([a[0], a[0]])
        if name == "attn_sink_3":
            cols.append(np.ascontiguousarray(np.broadcast_to(a.reshape(1, 8), (P, 8))))
            continue
        cols.append(a.reshape(-1, P).T)
    arrays = {"vectors": np.ascontiguousarray(np.concatenate(cols, 1)), "masks": mask_arrays()}
    arrays["xT"] = np.ascontiguousarray(np.asarray(inputs["x"])[0].T)
    arrays["ctxT"] = np.ascontiguousarray(np.asarray(inputs["ctx_2"])[0].T)
    for name in WEIGHTS:
        arrays[name] = np.asarray(inputs[name])[0]
    for name in WEIGHTS_2:
        arrays[name + "_2"] = np.asarray(inputs[name + "_2"])[0]
    rpb = np.asarray(inputs["rpb_2"])[0]
    c, kc = np.arange(64)[:, None], np.arange(64)[None, :]
    dc = np.clip(kc - c + 15, 0, 30)
    lower, upper = rpb[:, 1:15][:, :, dc], rpb[:, 0:14][:, :, dc]
    arrays["rpb"] = np.ascontiguousarray(
        np.concatenate([lower, upper], 2).transpose(2, 0, 1, 3).reshape(P, 8 * 14 * 64))
    for name in WEIGHTS_3:
        arrays[name + "_3"] = np.asarray(inputs[name + "_3"])[0]
    rows = [np.broadcast_to(np.asarray(inputs[n]).reshape(1, -1), (P, np.asarray(inputs[n]).size))
            for n in ("gmlp_ln_g_3", "gmlp_ln_b_3", "gmlp_b_s_3")]
    mixers = np.asarray(inputs["gmlp_w_s_3"])[0].transpose(2, 0, 1).reshape(P, 512)
    arrays["gmlp"] = np.ascontiguousarray(np.concatenate(rows + [mixers], 1))
    dist = np.abs(np.arange(384)[None, :] - 128 - np.arange(P)[:, None]).astype(np.float32)
    arrays["band"] = np.concatenate([dist, np.where(dist > 128, np.float32(-BIG), np.float32(0))], 1)
    return arrays


def kernel(**inputs):
    import concourse.bacc as bacc
    from concourse.bass_utils import run_bass_kernel_spmd

    nc = bacc.Bacc("TRN2", target_bir_lowering=False, num_devices=1)
    arrays = laid_out(inputs)
    A = {n: nc.dram_tensor("in_" + n, a.shape, F32, kind="ExternalInput").ap() for n, a in arrays.items()}
    out = nc.dram_tensor("out", (D, T), F32, kind="ExternalOutput").ap()
    program(nc, A, out)
    r = run_bass_kernel_spmd(nc, [{"in_" + n: a for n, a in arrays.items()}], core_ids=[0])
    return np.ascontiguousarray(r.results[0]["out"].T).reshape(1, T, D)
```

```python
from contextlib import ExitStack

import numpy as np
import concourse.bass as bass
from concourse import mybir

F32 = mybir.dt.float32
ALU = mybir.AluOpType
ACT = mybir.ActivationFunctionType
AXX = mybir.AxisListType.X
MUL, ADD, SUB, MAX, MIN = ALU.mult, ALU.add, ALU.subtract, ALU.max, ALU.min

P = 128
T = 512
D = 1024
KD = D // P
TB = T // P
L = 256
HD = 64
BIG = 1e30
BANKS = 8
RING = 4
SLOT = 4096
DECAY = 0.606531
E_ = 16
CAP = 64
FE = 2048


class Counter:

    def __init__(self, sem):
        self.sem, self.total, self.base = sem, 0, 0

    def rebase(self):
        self.base = self.total
        return self

    def at(self, n):
        return self.base + n


class Line:

    def __init__(self, eng, own):
        self.eng, self.own = eng, own

    def __call__(self, ins, sig=None, step=1):
        sig = sig or self.own
        ins.then_inc(sig.sem, step)
        sig.total += step
        self.eng.wait_ge(sig.sem, sig.total)

    def after(self, sig, n):
        self.eng.wait_ge(sig.sem, sig.at(n))


VECTORS = [
    ("c", 8), ("norm_w", 8), ("b_ada", 24), ("mu", 17), ("w0", 4), ("a0", 4), ("k_k", 4), ("k_a", 4),
    ("r_k", 4), ("gn_w", 4), ("gn_b", 4), ("q_gain", 1), ("k_gain", 1),
    ("c_2", 8), ("c_ctx_2", 8), ("b_mod_2", 48), ("norm_mix_g_2", 8), ("conv_w_2", 31 * 4),
    ("conv_b_2", 4), ("conv_ln_g_2", 4), ("conv_ln_b_2", 4), ("norm_ffn_g_2", 8), ("norm_final_g_2", 8),
    ("norm_g_even_3", 8), ("norm_g_odd_3", 8), ("hgrn_gamma_fwd_3", 32), ("hgrn_gamma_bwd_3", 32),
    ("hgrn_head_norm_g_3", 16), ("final_norm_g_3", 8), ("attn_sink_3", 8),
]
AT = {}
_n = 0
for _name, _w in VECTORS:
    AT[_name] = (_n, _w)
    _n += _w
NVEC = _n

MASKS = ["ident", "ones", "blk64", "mU16", "mL16", "mUoff", "mU", "mUI", "mLI", "bd", "adm", "iota", "win"]


def mask_arrays():
    i = np.arange(P)
    row, col = i[:, None], i[None, :]
    c64, c16 = row // 64 == col // 64, row // 16 == col // 16
    m = {
        "ident": row == col, "ones": np.ones((P, P), bool), "blk64": c64,
        "mU16": (row < col) & c16, "mL16": (row > col) & c16, "mUoff": (row < col) & c64 & ~c16,
        "mU": (row < col) & c64, "mUI": (row <= col) & c64, "mLI": (row >= col) & c64, "bd": c64,
        "iota": (col % 64 + 1) * np.ones((P, 1)),
        "win": -BIG * ((col < np.clip(row % 64 - 8, 0, 48)) | (col >= np.clip(row % 64 - 8, 0, 48) + 16)),
        "adm": -BIG * ((row < 64) & (col >= 64)),
    }
    return np.concatenate([m[k].astype(np.float32) for k in MASKS], 1)


class Chip:

    def __init__(self, nc, ctx, arrays, plan):
        self.nc, self.ctx, self.A, self.plan = nc, ctx, arrays, plan

        def sb(name, shape, dt=F32):
            return ctx.enter_context(nc.sbuf_tensor(name, shape, dt))

        self.xT = sb("xT", [P, KD, T])
        self.hT = sb("hT", [P, KD, T])
        self.ring = sb("weight_ring", [P, RING, SLOT])
        self.W = sb("work", [P, 12, 2048])
        self.vec = sb("vectors", [P, NVEC])
        self.msk = sb("masks", [P, len(MASKS) * P])
        self.csil = sb("silu_of_conditions", [P, KD, 32])
        self.mstage = sb("modulation_rows", [P, 4, P])
        self.mod1 = sb("mod1", [P, 24])
        self.mod2 = sb("mod2", [P, 48, 2])
        self.sm = sb("small", [P, 192])
        self.eps = sb("eps", [P, 4])
        self.ps = ctx.enter_context(nc.psum_tensor("ps", [P, BANKS, 512], F32))
        self.S = {}
        self.free_at = {}
        for n in ("tensor_step", "vector_step", "scalar_step", "pool_step", "aux_loaded"):
            self.counter(n)
        more = [self.slot(10, 2), self.slot(8, 2), self.hT[:, :, :]]
        self.slots = [self.ring[:, i, :] for i in range(RING)] + [a.rearrange("p k t -> p (k t)") for a in more]
        self.loaded = [self.counter(f"weights_loaded{i}") for i in range(len(self.slots))]
        first = len(block1_plan(arrays) + block2_mixer_plan(arrays))
        self.slot_of = [(i - first) % len(self.slots) if first <= i < first + 12 * E_ else i % RING
                        for i in range(len(plan))]
        self.arrived = {}
        self.issued = 0
        self.used = 0

    def counter(self, name):
        if name not in self.S:
            self.S[name] = Counter(self.ctx.enter_context(self.nc.semaphore(name)))
        return self.S[name].rebase()

    def counters(self, *names):
        return [self.counter(n) for n in names]

    def v(self, name, i=0, n=None):
        a, w = AT[name]
        return self.vec[:, a + i:a + i + (n or 1)]

    def m(self, name):
        i = MASKS.index(name)
        return self.msk[:, i * P:(i + 1) * P]

    def m4(self, name):
        return self.m(name).unsqueeze(1).to_broadcast([P, 4, P])

    def slot(self, i, n=1, kt=None):
        a = self.W[:, i:i + n, :].rearrange("p s n -> p (s n)")
        return a.rearrange("p (k t) -> p k t", t=T)

    def rpiece(self, i):
        return self.ring[:, 2 + i // 8, (i % 8) * 512:(i % 8 + 1) * 512]

    def rslot(self, i):
        a = self.ring[:, i // 2, (i % 2) * 2048:(i % 2 + 1) * 2048]
        return a.rearrange("p (k t) -> p k t", t=T)

    def stream(self, sp, upto):
        upto = min(upto, len(self.plan))
        while self.issued < upto:
            i = self.issued
            if self.plan[i] is None:
                self.issued += 1
                continue
            sources, kt, c = self.plan[i]
            before = [j for j in range(i) if self.slot_of[j] == self.slot_of[i] and self.plan[j] is not None]
            if before:
                sp.wait_ge(*self.free_at[before[-1]])
            sig = self.loaded[self.slot_of[i]]
            dst = self.block_view(i)
            for src, c0, n in sources:
                sp.dma_start(dst[:, :, c0:c0 + n], src).then_inc(sig.sem, 16)
                sig.total += 16
            self.arrived[i] = (sig.sem, sig.total)
            self.issued += 1

    def block_view(self, i):
        _, kt, c = self.plan[i]
        return self.slots[self.slot_of[i]][:, 0:kt * c].rearrange("p (k c) -> p k c", k=kt)

    def block_wait(self, eng, i):
        eng.wait_ge(*self.arrived[i])


def blocks(w, c0, c1):
    kt = w.shape[0] // P
    width = min(SLOT // kt, 512)
    out = []
    for c in range(c0, c1, width):
        n = min(width, c1 - c)
        out.append(([(w[:, c:c + n].rearrange("(k p) c -> p k c", p=P), 0, n)], kt, n))
    return out


def joined(w, parts):
    c, sources = 0, []
    for c0, c1 in parts:
        sources.append((w[:, c0:c1].rearrange("(k p) c -> p k c", p=P), c, c1 - c0))
        c += c1 - c0
    return [(sources, w.shape[0] // P, c)]


def nothing(*engine):
    pass


def project(ch, nblocks, tiles, ahead=RING, extra_sync=None, vector_after=None, scalar_after=None,
            banks=BANKS, tensor_beside={}, vector_beside={}, scalar_beside={}, norm=None):
    nc = ch.nc
    first = ch.used
    R = banks
    ready, by_act, by_dve = ch.counters("tile_ready", "tile_scalar_done", "tile_vector_done")
    na = np.cumsum([t[5][0] is not None for t in tiles])
    nv = np.cumsum([t[5][1] is not None for t in tiles])

    def shape(t):
        b, kind, where, src, ntok, _ = t
        c = ch.plan[first + b][2] if b is not None else P
        if kind == "T":
            return min(P, c - where), ntok
        if kind == "N":
            return P, c
        if isinstance(kind, tuple):
            return P, kind[2] - kind[1]
        return P, P

    for n, t in enumerate(tiles):
        if t[0] is not None:
            ch.free_at[first + t[0]] = (ready.sem, ready.at(n + 1))

    with nc.Block() as block:
        @block.sync
        def _(sp):
            if extra_sync:
                extra_sync(sp)
            ch.stream(sp, first + nblocks + ahead)

        @block.tensor
        def _(pe):
            last = -1
            tensor_beside.get(-1, nothing)(pe)
            for n, t in enumerate(tiles):
                b, kind, where, src, ntok, ev = t
                i = first + b if b is not None else None
                if b is not None and b != last:
                    ch.block_wait(pe, i)
                    last = b
                if n >= R:
                    if tiles[n - R][5][1] is not None:
                        pe.wait_ge(by_dve.sem, by_dve.at(int(nv[n - R])))
                    else:
                        pe.wait_ge(by_act.sem, by_act.at(int(na[n - R])))
                m, f = shape(t)
                bank = ch.ps[:, n % R, :]
                if kind == "X":
                    pe.wait_ge(by_act.sem, by_act.at(int(na[where])))
                    ins = pe.transpose(bank[:, 0:P], src, ch.m("ident"))
                    ins.then_inc(ready.sem, 1)
                    ready.total += 1
                    tensor_beside.get(n, nothing)(pe)
                    continue
                w = ch.block_view(i)
                _, kt, c = ch.plan[i]
                if kind == "M":
                    for k in range(kt):
                        for g in range(4):
                            ins = pe.matmul(bank[32 * g:32 * g + 32, 0:P], ch.csil[:, k, :],
                                            w[:, k, g * P:(g + 1) * P], start=k == 0, stop=k == kt - 1)
                else:
                    for k in range(kt):
                        if n == 0 and norm:
                            norm.wait(pe, k)
                        if k == kt // 2 and n - 0.5 in tensor_beside:
                            tensor_beside[n - 0.5](pe)
                        if kind == "T":
                            ins = pe.matmul(bank[0:m, 0:f], w[:, k, where:where + m], src[:, k, 0:ntok],
                                            start=k == 0, stop=k == kt - 1)
                        else:
                            c0 = kind[1] if isinstance(kind, tuple) else 0
                            ins = pe.matmul(bank[0:m, 0:f], src[:, k, where:where + P], w[:, k, c0:c0 + f],
                                            start=k == 0, stop=k == kt - 1)
                ins.then_inc(ready.sem, 1)
                ready.total += 1
                tensor_beside.get(n, nothing)(pe)

        @block.scalar
        def _(act):
            a = Line(act, ch.S["scalar_step"])
            if norm:
                norm.root(a, act)
                norm.add_shift(a, act)
            scalar_beside.get(-1, nothing)(a, act)
            for n, t in enumerate(tiles):
                if t[5][0] is not None:
                    m, f = shape(t)
                    a.after(ready, n + 1)
                    t[5][0](a, act, ch.ps[0:m, n % R, 0:f], by_act)
                scalar_beside.get(n, nothing)(a, act)
            if scalar_after:
                scalar_after(a, act)

        @block.vector
        def _(dve):
            v = Line(dve, ch.S["vector_step"])
            if norm:
                norm.scale(v, dve)
            vector_beside.get(-1, nothing)(v, dve)
            for n, t in enumerate(tiles):
                if t[5][1] is not None:
                    m, f = shape(t)
                    v.after(ready, n + 1)
                    if t[5][0] is not None:
                        v.after(by_act, int(na[n]))
                    t[5][1](v, dve, ch.ps[0:m, n % R, 0:f], by_dve)
                vector_beside.get(n, nothing)(v, dve)
            if vector_after:
                vector_after(v, dve)
    ch.used = first + nblocks


def weave(main, side):
    out = []
    for i in range(max(len(main), len(side))):
        out += [x[i] for x in (main, side) if i < len(x)]
    return out


def modulated(ch, tiles, nblocks, bands):
    place = {}
    for x in weave([("main", b) for b in range(nblocks)], [("side", i) for i in range(len(bands))]):
        place[x] = len(place)
    out, pending = [], []

    def turn_rows(i, m):
        dst, bias, first = bands[i]
        n = dst.shape[2]

        def part(v, dve, ps, sig):
            v(dve.tensor_tensor(dst, ps.rearrange("p (g r) -> p g r", r=32)[:, :, first:first + n],
                                bias.unsqueeze(2).to_broadcast([P, 4, n]), ADD), sig)
        return (None, "X", m, ch.mstage[:, i % 4, :], T, (None, part))

    for kind, i in sorted(place, key=place.get):
        b = place[kind, i]
        if kind == "main":
            mine = [t for t in tiles if t[0] == i]
            out += [(b,) + mine[0][1:]]
            out += [turn_rows(*x) for x in pending]
            pending = []
            out += [(b,) + t[1:] for t in mine[1:]]
        else:
            if pending and nblocks <= i:
                out += [turn_rows(*x) for x in pending]
                pending = []
            pending.append((i, len(out)))
            out.append((b, "M", 0, None, T, copy_to(ch.mstage[:, i % 4, :])))
    return out + [turn_rows(*x) for x in pending], len(place)


def copy_to(out):
    return (lambda a, act, ps, sig: a(act.copy(out, ps), sig), None)


def act_to(out, func, **kw):
    return (lambda a, act, ps, sig: a(act.activation(out, ps, func, **kw), sig), None)


def inverse_root(a, act, out, src, scale, eps, done):
    a(act.activation(out, src, ACT.Ln, bias=eps, scale=scale))
    a(act.activation(out, out, ACT.Exp, scale=-0.5), done)


class Norm:

    def __init__(self, ch, src, dst, ntok, gain, shift, bank, sq, room, tag=""):
        self.ch, self.src, self.dst, self.n, self.gain, self.bias = ch, src, dst, ntok, gain, shift
        self.kt, self.bank = src.shape[1], ch.ps[:, bank, 0:ntok]
        self.sq, self.rstd, self.tmp = sq[:, :, 0:ntok], room[:, 0, 0:ntok], room[:, 1:3, 0:ntok]
        self.squares, self.sums, self.rooted, self.scaled, self.shifted = ch.counters(
            *[tag + n for n in ("norm_squares", "norm_sums", "norm_root", "norm_scaled", "norm_shifted")])

    def square(self, k):
        def part(a, act):
            if k >= 4:
                a.after(self.sums, k - 3)
            a(act.square(self.sq[:, k % 4, :], self.src[:, k, :]), self.squares)
        return part

    def sum(self, k):
        def part(pe):
            pe.wait_ge(self.squares.sem, self.squares.at(k + 1))
            pe.matmul(self.bank, self.ch.m("ones"), self.sq[:, k % 4, :], start=k == 0,
                      stop=k == self.kt - 1).then_inc(self.sums.sem, 1)
            self.sums.total += 1
        return part

    def root(self, a, act):
        a.after(self.sums, self.kt)
        inverse_root(a, act, self.rstd, self.bank, 1.0 / (P * self.kt), self.ch.eps[:, 0:1], self.rooted)

    def add_shift(self, a, act):
        for k in range(self.kt if self.bias is not None else 0):
            a.after(self.scaled, k + 1)
            a(act.activation(self.dst[:, k, :], self.tmp[:, k % 2, :], ACT.Identity, bias=self.bias[k]),
              self.shifted)

    def scale(self, v, dve):
        v.after(self.rooted, 1)
        for k in range(self.kt):
            if self.bias is not None and k >= 2:
                v.after(self.shifted, k - 1)
            out = self.dst[:, k, :] if self.bias is None else self.tmp[:, k % 2, :]
            v(dve.scalar_tensor_tensor(out, self.src[:, k, :], self.gain[k], self.rstd, MUL, MUL), self.scaled)

    def wait(self, eng, k):
        last = self.scaled if self.bias is None else self.shifted
        eng.wait_ge(last.sem, last.at(k + 1))


def finish_norm(ch, norm, then=None):
    with ch.nc.Block() as block:
        @block.scalar
        def _(act):
            a = Line(act, ch.S["scalar_step"])
            norm.root(a, act)
            norm.add_shift(a, act)
            for k in range(norm.kt if then else 0):
                norm.wait(act, k)
                then.square(k)(a, act)

        @block.vector
        def _(dve):
            norm.scale(Line(dve, ch.S["vector_step"]), dve)

        @block.tensor
        def _(pe):
            for k in range(norm.kt if then else 0):
                then.sum(k)(pe)


def seq(*parts):
    def run(*engine):
        for part in parts:
            part(*engine)
    return run


class Beside:

    def __init__(self):
        self.tensor, self.scalar, self.vector = {}, {}, {}

    def add(self, where, tensor=None, scalar=None, vector=None):
        place = int(np.floor(where))
        for parts, key, part in ((self.tensor, where, tensor), (self.scalar, place, scalar),
                                 (self.vector, place, vector)):
            if part:
                parts[key] = seq(parts[key], part) if key in parts else part

    def project(self, ch, nblocks, tiles, **options):
        project(ch, nblocks, tiles, tensor_beside=self.tensor, scalar_beside=self.scalar,
                vector_beside=self.vector, **options)


def beside_stream(norm, n0=0):
    vector_done = norm.ch.S["tile_vector_done"]

    def square(k):
        def part(a, act):
            a.after(vector_done, n0 + k + 1)
            norm.square(k)(a, act)
        return part
    kt = norm.kt
    scalar = {n0 + k: square(k) for k in range(kt)}
    tensor = {n0 + k + 1: norm.sum(k) for k in range(kt - 1)}
    tensor[n0 + kt - 1] = seq(norm.sum(kt - 2), norm.sum(kt - 1))
    return tensor, scalar



def load_constants(ch):
    nc, A = ch.nc, ch.A
    got = ch.counter("aux_loaded")
    with nc.Block() as block:
        @block.sync
        def _(sp):
            for dst, src in ((ch.vec[:, :], A["vectors"]), (ch.msk[:, :], A["masks"]),
                             (ch.xT[:, :, :], A["xT"].rearrange("(k p) t -> p k t", p=P))):
                sp.dma_start(dst, src).then_inc(got.sem, 16)
                got.total += 16
            ch.stream(sp, RING)
            sp.wait_ge(got.sem, got.total)

        @block.vector
        def _(dve):
            v = Line(dve, ch.S["vector_step"])
            for i, e in enumerate((1e-6, 64e-5, 0.0, 1.0)):
                v(dve.memset(ch.eps[:, i:i + 1], e))
            v(dve.memset(ch.csil[:, :, :], 0.0))
    with nc.Block() as block:
        @block.scalar
        def _(act):
            a = Line(act, ch.S["scalar_step"])
            for i, name in enumerate(("c", "c_2", "c_ctx_2")):
                a(act.activation(ch.csil[:, :, i], ch.v(name, 0, 8), ACT.Silu))


def block1_modulation(ch):
    bands = [(ch.mod1[:, 4 * b:4 * b + 4].unsqueeze(2), ch.v("b_ada", 4 * b, 4), 0) for b in range(6)]
    tiles, n = modulated(ch, [], 0, bands)
    norm = Norm(ch, ch.xT, ch.hT, T, [ch.sm[:, 24 + k:25 + k] for k in range(8)],
                [ch.mod1[:, k:k + 1] for k in range(8)], 7, ch.slot(4), ch.slot(5))
    project(ch, n, tiles, banks=7, tensor_beside={0: seq(*[norm.sum(k) for k in range(8)])},
            scalar_beside={0: seq(*[norm.square(k) for k in range(8)])})
    with ch.nc.Block() as block:
        @block.vector
        def _(dve):
            v = Line(dve, ch.S["vector_step"])
            v(dve.scalar_tensor_tensor(ch.sm[:, 24:32], ch.mod1[:, 8:16], 1.0, ch.v("norm_w", 0, 8), ADD, MUL))
            v(dve.tensor_scalar(ch.sm[:, 32:49], ch.v("mu", 0, 17), -1.0, 1.0, MUL, ADD))
    return norm


def bands2(ch, b0, b1):
    return [(ch.mod2[:, 4 * b:4 * b + 4, :], ch.v("b_mod_2", 4 * b, 4), 1) for b in range(b0, b1)]


def block1_rwkv_projection(ch, norm):
    tmp = ch.slot(9)
    outs = [(ch.slot(11), 12), (ch.slot(1), 4), (ch.slot(0), 0), (ch.slot(2), 8), (ch.slot(3), 13)]
    tiles = []
    for b, (dst, first) in enumerate(outs):
        for j in range(1 if first == 12 else 4):
            t4 = tmp[:, len(tiles) % 4, :]
            one_mu, mu = ch.sm[:, 32 + first + j:33 + first + j], ch.v("mu", first + j)

            def part_a(a, act, ps, sig, t4=t4, one_mu=one_mu):
                a(act.activation(t4, ps, ACT.Identity, scale=one_mu, bias=ch.eps[:, 2:3]), sig)

            def part_v(v, dve, ps, sig, t4=t4, mu=mu, o=dst[:, j, :]):
                v(dve.tensor_copy(o[:, 0:1], t4[:, 0:1]))
                v(dve.scalar_tensor_tensor(o[:, 1:T], ps[:, 0:T - 1], mu, t4[:, 1:T], MUL, ADD), sig)
            tiles.append((b, "T", j * P, ch.hT, T, (part_a, part_v)))
    woven, n = modulated(ch, tiles, 5, bands2(ch, 0, 5))
    at = [next(i for i, w in enumerate(woven) if w[5] is t[5]) for t in tiles]
    beside = Beside()
    load = rwkv_prepare(ch, beside, at[1:5], at[5:9], at[13:17])
    beside.project(ch, n, woven, banks=4, ahead=0, norm=norm, extra_sync=load)


def rwkv_prepare(ch, beside, k_at, r_at, g_at):
    ps = ch.ps
    rT, kT, vT, lora = ch.slot(0), ch.slot(1), ch.slot(2), ch.slot(11)[:, 0, :]
    th, keep, wup = (ch.slot(11)[:, i, :] for i in (1, 2, 3))
    kk, kka, key = ch.slot(4), ch.slot(6), ch.slot(7)
    before, cum, inverse = ch.slot(8), ch.slot(5), ch.slot(10)
    aux = ch.counter("aux_loaded")
    (sq_ready, th_ready, products, lora_out, roots, cum_ready, exps, cml_ready, bonus_in) = ch.counters(
        "key_square_ready", "tanh_ready", "prep_products", "lora_read", "roots_ready", "cum_ready",
        "exps_ready", "cml_ready", "bonus_in_ready")
    by_dve = ch.S["tile_vector_done"]

    def load(sp):
        for dst, src in ((wup[0:64, :], ch.A["w_up"]), (wup[64:128, :], ch.A["a_up"])):
            sp.dma_start(dst, src).then_inc(aux.sem, 16)
            aux.total += 16

    def product(pe, *args):
        pe.matmul(*args, start=True, stop=True).then_inc(products.sem, 1)
        products.total += 1

    def decay_products(pe):
        pe.wait_ge(aux.sem, aux.at(32))
        pe.wait_ge(th_ready.sem, th_ready.at(1))
        for j in range(4):
            product(pe, ps[:, 4 + j, :], wup[0:64, j * P:(j + 1) * P], th[0:64, :])

    def rate_products(pe):
        for j in range(4):
            pe.wait_ge(lora_out.sem, lora_out.at(j + 1))
            product(pe, ps[:, 4 + j, :], wup[64:128, j * P:(j + 1) * P], lora[64:128, :])

    def key_sums(pe):
        for j in range(4):
            pe.wait_ge(sq_ready.sem, sq_ready.at(j + 1))
            pe.wait_ge(lora_out.sem, lora_out.at(5 + j))
            product(pe, ps[:, 4 + j, :], ch.m("blk64"), kka[:, j, :])

    def bonus_sums(pe):
        for j in range(4):
            pe.wait_ge(roots.sem, roots.at(j + 1))
            pe.wait_ge(bonus_in.sem, bonus_in.at(j + 1))
            product(pe, ps[:, 4 + j, :], ch.m("blk64"), before[:, j, :])

    def tanh(a, act):
        a.after(by_dve, 1)
        a(act.activation(th[0:64, :], lora[0:64, :], ACT.Tanh), th_ready)

    def sigmoids(a, act, first, out, bias):
        for j in range(4):
            a.after(products, first + j + 1)
            a(act.activation(out[:, j, :], ps[:, 4 + j, :], ACT.Sigmoid, bias=ch.v(bias, j)), lora_out)

    def key_roots(a, act):
        for j in range(4):
            a.after(products, 9 + j)
            a(act.activation(kka[:, j, :], ps[:, 4 + j, :], ACT.Sqrt, bias=ch.eps[:, 2:3]), roots)

    def exponents(a, act):
        a.after(cml_ready, 1)
        a(act.activation(inverse, cum, ACT.Exp, scale=-1.0), exps)
        a(act.activation(cum, cum, ACT.Exp), exps)
        a(act.activation(before, before, ACT.Exp), exps)

    def log_decays(v, dve):
        v(dve.memset(keep, 1.0))
        v(dve.memset(keep.rearrange("p (c t) -> p c t", t=64)[:, :, 0:1], 0.0))
        v.after(lora_out, 4)
        v(dve.tensor_scalar(before, before, -DECAY, None, MUL))
        for j in range(4):
            v(dve.tensor_tensor_scan(cum[:, j, :], keep, before[:, j, :], 0.0, MUL, ADD), cum_ready)
        v(dve.tensor_tensor(before, cum, before, SUB), cml_ready)

    def key_squares(v, dve):
        for j in range(4):
            v(dve.tensor_scalar(kk[:, j, :], kT[:, j, :], ch.v("k_k", j), None, MUL))
            v(dve.tensor_tensor(kka[:, j, :], kk[:, j, :], kk[:, j, :], MUL), sq_ready)

    def keys(v, dve):
        v.after(roots, 4)
        v(dve.tensor_scalar(kka, kka, 1e-12, None, MAX))
        v(dve.reciprocal(kka, kka))
        v(dve.tensor_tensor(kk, kk, kka, MUL))
        v.after(lora_out, 8)
        v(dve.tensor_tensor(kka, kk, key, MUL))
        for j in range(4):
            v(dve.tensor_scalar(key[:, j, :], key[:, j, :], 1.0, ch.v("k_a", j), SUB, MUL))
            v(dve.scalar_tensor_tensor(key[:, j, :], key[:, j, :], 1.0, kT[:, j, :], ADD, MUL))

    def operands(v, dve):
        v.after(exps, 3)
        v(dve.scalar_tensor_tensor(kk, kk, -1.0, before, MUL, MUL))
        for j in range(4):
            v(dve.scalar_tensor_tensor(before[:, j, :], rT[:, j, :], ch.v("r_k", j), key[:, j, :], MUL, MUL),
              bonus_in)
        v(dve.tensor_copy(ch.sm[:, 64:96].rearrange("p (j c) -> p j c", c=8),
                          cum.rearrange("p j (c t) -> p j c t", t=64)[:, :, :, 63]))
        v(dve.tensor_tensor(cum, rT, cum, MUL))
        v(dve.tensor_tensor(kka, kka, inverse, MUL))
        v(dve.tensor_tensor(key, key, inverse, MUL))

    def bonus(v, dve):
        for j in range(4):
            v.after(products, 13 + j)
            v(dve.tensor_tensor(before[:, j, :], vT[:, j, :], ps[:, 4 + j, :], MUL))

    beside.add(k_at[0], None, tanh)
    beside.add(k_at[1], decay_products, lambda a, act: sigmoids(a, act, 0, before, "w0"))
    beside.add(k_at[2], rate_products, lambda a, act: sigmoids(a, act, 4, key, "a0"), log_decays)
    beside.add(k_at[3], None, exponents, key_squares)
    beside.add(r_at[0], key_sums, key_roots)
    beside.add(r_at[1], None, None, keys)
    beside.add(r_at[3], None, None, operands)
    beside.add(g_at[0], bonus_sums)
    beside.add(g_at[1], None, None, bonus)
    return load


def rwkv_transpose(ch):
    nc, ps = ch.nc, ch.ps
    pairs = [(ch.slot(6), ch.slot(9)), (ch.slot(7), ch.slot(10)), (ch.slot(2), ch.slot(11)),
             (ch.slot(4), ch.rslot(7))]
    turned, copied = ch.counters("turned", "turned_copied")
    with nc.Block() as block:
        @block.tensor
        def _(pe):
            for n in range(16):
                src = pairs[n // 4][0]
                if n >= 4:
                    pe.wait_ge(copied.sem, copied.at(n - 3))
                for j in range(4):
                    ins = pe.transpose(ps[:, n % 4, j * P:(j + 1) * P], src[:, j, (n % 4) * P:(n % 4 + 1) * P],
                                       ch.m("ident"))
                ins.then_inc(turned.sem, 1)
                turned.total += 1

        @block.scalar
        def _(act):
            a = Line(act, ch.S["scalar_step"])
            for n in range(16):
                a.after(turned, n + 1)
                a(act.copy(pairs[n // 4][1][:, n % 4, :], ps[:, n % 4, :]), copied)


def rwkv_within_chunks(ch):
    nc, ps = ch.nc, ch.ps
    nT, bT, kdT = ch.slot(4), ch.slot(6), ch.slot(7)
    vN, nN = ch.slot(11), ch.rslot(7)
    w1T, w2 = ch.slot(0), ch.slot(1)

    def mats(i):
        return ch.rslot(i).rearrange("p b (s t) -> p b s t", t=P)
    d, xd, xo, lk, d2, xd2, inv = [mats(i) for i in range(7)]
    I4 = ch.m4("ident")
    products, evacuated = ch.counters("chunk_products", "chunk_evacuated")

    def head(half, b):
        h = 4 * half + b
        return h, slice(64 * (h % 2), 64 * (h % 2) + 64), h // 2

    def tok(s):
        return slice(s * P, (s + 1) * P)

    def steps(half):
        def gram(left, right):
            def f(b, s):
                h, rows, j = head(half, b)
                return left[rows, j, tok(s)], right[rows, j, tok(s)]
            return f

        def mm(left, right):
            return lambda b, s: (left[:, b, s, :], right[:, b, s, :])

        def value(left):
            def f(b, s):
                h, _, _ = head(half, b)
                return left[:, b, s, :], vN[:, s, h * HD:(h + 1) * HD]
            return f
        return [
            (gram(nT, bT), "mask", [(d, "mL16")]), (gram(bT, nT), "mask", [(xd, "mU16"), (xo, "mUoff")]),
            (gram(kdT, nT), "mask", [(lk, "mU")]),
            (mm(xd, d), "copy", d2), (mm(d, xd), "copy", xd2),
            (mm(d2, inv), "add", (inv, inv)),
            (mm(xd2, d2), "copy", d), (mm(d2, xd2), "copy", xd),
            (mm(d, inv), "add", (inv, inv)),
            (mm(xd, d), "copy", d2), (mm(d2, inv), "add", (inv, inv)),
            ("turn", "copy", xd2), (mm(xo, xd2), "copy", d2),
            (mm(d2, inv), "add", (d, inv)), (mm(d2, d), "add", (d, inv)), (mm(d2, d), "add", (d, inv)),
            (value(lk), "value", xd), ("w2", "w2", None), ("w1", "w1", None),
        ]

    with nc.Block() as block:
        @block.tensor
        def _(pe):
            n = 0
            for half in range(2):
                for left_right, how, _ in steps(half):
                    for b in range(4):
                        if n >= 4:
                            pe.wait_ge(evacuated.sem, evacuated.at(n - 3))
                        h, rows, j = head(half, b)
                        bank = ps[:, n % BANKS, :]
                        for s in range(4):
                            if left_right == "turn":
                                ins = pe.transpose(bank[:, tok(s)], inv[:, b, s, :], ch.m("ident"))
                            elif left_right == "w2":
                                ins = pe.matmul(bank[:, s * HD:(s + 1) * HD], d[:, b, s, :], xd[:, b, s, 0:HD],
                                                start=True, stop=True)
                            elif left_right == "w1":
                                ins = pe.matmul(bank[rows, tok(s)], nN[:, s, h * HD:(h + 1) * HD],
                                                d[:, b, s, :], start=True, stop=True)
                            else:
                                left, right = left_right(b, s)
                                ins = pe.matmul(bank[:, s * right.shape[-1]:(s + 1) * right.shape[-1]],
                                                left, right, start=True, stop=True)
                        ins.then_inc(products.sem, 1)
                        products.total += 1
                        n += 1

        @block.vector
        def _(dve):
            v = Line(dve, ch.S["vector_step"])
            n = 0
            for half in range(2):
                for left_right, how, out in steps(half):
                    for b in range(4):
                        h, rows, j = head(half, b)
                        v.after(products, n + 1)
                        flat = ps[:, n % BANKS, :]
                        bank = flat.rearrange("p (s t) -> p s t", t=P)
                        if how == "mask":
                            if len(out) == 2:
                                v(dve.tensor_tensor(out[0][0][:, b], bank, ch.m4(out[0][1]), MUL))
                                v(dve.tensor_tensor(inv[:, b], out[0][0][:, b], I4, ADD))
                            v(dve.tensor_tensor(out[-1][0][:, b], bank, ch.m4(out[-1][1]), MUL), evacuated)
                        elif how == "copy":
                            v(dve.tensor_copy(out[:, b], bank), evacuated)
                        elif how == "add":
                            v(dve.tensor_tensor(out[0][:, b], bank, out[1][:, b], ADD), evacuated)
                        elif how == "value":
                            v(dve.tensor_copy(xd[:, b, :, 0:HD], flat[:, 0:4 * HD].rearrange("p (s t) -> p s t", t=HD)),
                              evacuated)
                        elif how == "w2":
                            v(dve.tensor_copy(w2[:, :, h * HD:(h + 1) * HD],
                                              flat[:, 0:4 * HD].rearrange("p (s t) -> p s t", t=HD)), evacuated)
                        elif how == "w1":
                            v(dve.tensor_copy(w1T[rows, j, :], flat[rows, :]), evacuated)
                        n += 1


def rwkv_chain(ch):
    nc, ps = ch.nc, ch.ps
    w1T, u = ch.slot(0), ch.slot(1)
    bN, kN, vN = ch.slot(9), ch.slot(10), ch.slot(11)
    states = [ch.rpiece(c).rearrange("p (j t) -> p j t", t=P) for c in range(8)]
    tmp = ch.rpiece(8).rearrange("p (j t) -> p j t", t=P)
    bd = ch.m4("bd")
    end = ch.sm[:, 64:96].rearrange("p (j c) -> p j c", c=8)
    u_sum, u_ready, s_sum, s_ready = ch.counters("u_sum", "u_ready", "state_sum", "state_ready")
    v_keys = ch.slot(4)

    def read_state(c):
        def part(pe):
            s, rows = c // 2, slice(64 * (c % 2), 64 * (c % 2) + 64)
            pe.wait_ge(s_ready.sem, s_ready.at(c + 1))
            for j in range(4):
                ins = pe.matmul(ps[rows, BANKS - 2, j * P:(j + 1) * P], w1T[:, j, c * 64:(c + 1) * 64],
                                states[c][:, j, :], start=True, stop=True)
            ins.then_inc(u_sum.sem, 1)
            u_sum.total += 1
        return part

    def write_state(c):
        def part(pe):
            s, rows = c // 2, slice(64 * (c % 2), 64 * (c % 2) + 64)
            if c > 0:
                pe.wait_ge(u_ready.sem, u_ready.at(c))
                pe.wait_ge(s_ready.sem, s_ready.at(c + 1))
            for j in range(4):
                cols = slice(j * P, (j + 1) * P)
                pe.matmul(ps[:, BANKS - 1, cols], kN[rows, s, cols], vN[rows, s, cols], start=True, stop=False)
                ins = pe.matmul(ps[:, BANKS - 1, cols], bN[rows, s, cols], u[rows, s, cols], start=False, stop=True)
            ins.then_inc(s_sum.sem, 1)
            s_sum.total += 1
        return part

    def update(v, dve):
        v(dve.memset(states[0], 0.0), s_ready)
        for c in range(8):
            s, rows = c // 2, slice(64 * (c % 2), 64 * (c % 2) + 64)
            if c > 0:
                v.after(u_sum, c)
                v(dve.tensor_tensor(u[rows, s, :], ps[rows, BANKS - 2, :], u[rows, s, :], ADD), u_ready)
            if c < 7:
                v.after(s_sum, c + 1)
                v(dve.tensor_tensor(tmp, ps[:, BANKS - 1, :].rearrange("p (j t) -> p j t", t=P), bd, MUL))
                v(dve.tensor_tensor(tmp, tmp, states[c], ADD))
                v(dve.tensor_tensor(states[c + 1], tmp, end[:, :, c:c + 1].to_broadcast([P, 4, P]), MUL),
                  s_ready)

    beside = Beside()
    beside.add(-1, write_state(0), None, update)
    places = [-1, -1, -1, -1, -0.5, 0, 0.5, 1, 1.5, 2, 2.5, 3, 3, 3]
    for c in range(1, 8):
        beside.add(places[2 * c - 2], read_state(c))
        if c < 7:
            beside.add(places[2 * c - 1], write_state(c))
    tiles = [(0, "N", s * P, ch.hT, T, copy_to(v_keys[:, s, :])) for s in range(4)]
    beside.project(ch, 1, tiles, banks=2, ahead=1)


def rwkv_output(ch):
    nc, ps = ch.nc, ch.ps
    rdT, bT, kdT, bonus, gate = ch.slot(5), ch.slot(6), ch.slot(7), ch.slot(8), ch.slot(3)
    u, vN, yT = ch.slot(1), ch.slot(11), ch.slot(2)
    states = [ch.rpiece(c).rearrange("p (j t) -> p j t", t=P) for c in range(8)]
    mb = [ch.rpiece(9 + i).rearrange("p (s t) -> p s t", t=P) for i in range(4)]
    mI = ch.m4("mUI")
    cen, sq = ch.slot(0), [ch.rpiece(9 + i) for i in range(4)]
    q, k = ch.slot(9), ch.slot(10)
    grams, masked, y_sum, y_out, sums, cen_out, sq_out, roots = ch.counters(
        "grams", "grams_masked", "y_sum", "y_out", "y_means", "y_centred", "y_squares", "y_roots")
    B0 = 2

    def pair_grams(j):
        def part(pe):
            for e in range(2):
                rows = slice(64 * e, 64 * e + 64)
                for i, key in enumerate((bT, kdT)):
                    n = 4 * j + 2 * e + i
                    if n >= 4:
                        pe.wait_ge(masked.sem, masked.at(n - 3))
                        if j >= 1:
                            pe.wait_ge(y_sum.sem, y_sum.at(j))
                    for s in range(4):
                        cols = slice(s * P, (s + 1) * P)
                        ins = pe.matmul(ps[:, B0 + 2 * e + i, cols], key[rows, j, cols], rdT[rows, j, cols],
                                        start=True, stop=True)
                    ins.then_inc(grams.sem, 1)
                    grams.total += 1
        return part

    def pair_output(j):
        def part(pe):
            pe.wait_ge(masked.sem, masked.at(4 * j + 4))
            if j >= 2:
                pe.wait_ge(y_out.sem, y_out.at(j - 1))
            bank = B0 + 4 + j % 2
            for c in range(8):
                pe.matmul(ps[:, bank, c * 64:(c + 1) * 64], states[c][:, j, :], rdT[:, j, c * 64:(c + 1) * 64],
                          start=c == 0, stop=False, skip_group_check=True)
            for e in range(2):
                rows, hc = slice(64 * e, 64 * e + 64), slice((2 * j + e) * HD, (2 * j + e + 1) * HD)
                for s in range(4):
                    cols = slice(s * P, (s + 1) * P)
                    pe.matmul(ps[rows, bank, cols], u[:, s, hc], mb[2 * e][:, s, :], start=False, stop=False,
                              skip_group_check=True)
                    ins = pe.matmul(ps[rows, bank, cols], vN[:, s, hc], mb[2 * e + 1][:, s, :],
                                    start=False, stop=e == 1 and s == 3, skip_group_check=True)
            ins.then_inc(y_sum.sem, 1)
            y_sum.total += 1
        return part

    def mean(j):
        def part(pe):
            pe.wait_ge(y_out.sem, y_out.at(j + 1))
            pe.wait_ge(masked.sem, masked.at(16))
            pe.matmul(ps[:, B0 + j, :], ch.m("blk64"), yT[:, j, :], start=True, stop=True).then_inc(sums.sem, 1)
            sums.total += 1
        return part

    def square_mean(j):
        def part(pe):
            pe.wait_ge(sq_out.sem, sq_out.at(j + 1))
            pe.matmul(ps[:, B0 + j, :], ch.m("blk64"), sq[j], start=True, stop=True).then_inc(sums.sem, 1)
            sums.total += 1
        return part

    def mask_pair(j):
        def part(v, dve):
            for n in range(4):
                v.after(grams, 4 * j + n + 1)
                if j >= 1 and n == 0:
                    v.after(y_sum, j)
                v(dve.tensor_tensor(mb[n], ps[:, B0 + n, :].rearrange("p (s t) -> p s t", t=P), mI, MUL), masked)
        return part

    def centre(v, dve):
        for j in range(4):
            v.after(sums, j + 1)
            v(dve.scalar_tensor_tensor(cen[:, j, :], ps[:, B0 + j, :], -1.0 / HD, yT[:, j, :], MUL, ADD), cen_out)

    def finish(v, dve):
        for j in range(4):
            v.after(roots, j + 1)
            v(dve.tensor_tensor(cen[:, j, :], cen[:, j, :], sq[j], MUL))
            v(dve.tensor_scalar(cen[:, j, :], cen[:, j, :], ch.v("gn_w", j), ch.v("gn_b", j), MUL, ADD))
        v(dve.tensor_tensor(cen, cen, bonus, ADD))
        v.after(roots, 5)
        v(dve.tensor_tensor(yT, cen, gate, MUL))

    def take_output(j):
        def part(a, act):
            a.after(y_sum, j + 1)
            a(act.copy(yT[:, j, :], ps[:, B0 + 4 + j % 2, :]), y_out)
        return part

    def square(a, act):
        for j in range(4):
            a.after(cen_out, j + 1)
            a(act.square(sq[j], cen[:, j, :]), sq_out)

    def take_roots(a, act):
        for j in range(4):
            a.after(sums, 5 + j)
            inverse_root(a, act, sq[j], ps[:, B0 + j, :], 1.0 / HD, ch.eps[:, 1:2], roots)
        a(act.activation(gate, gate, ACT.Silu), roots)

    beside = Beside()
    beside.add(-1, pair_grams(0), None, mask_pair(0))
    for j in range(4):
        beside.add(j + 0.5, pair_output(j), take_output(j))
        if j < 3:
            beside.add(j + 0.5, pair_grams(j + 1), None, mask_pair(j + 1))
    beside.add(4, seq(*[mean(j) for j in range(4)]), None, centre)
    beside.add(4.5, None, square)
    beside.add(4.5, seq(*[square_mean(j) for j in range(4)]), take_roots, finish)
    tiles = [(3 * b, "T", j * P, ch.hT, T, copy_to(dst[:, j, :])) for b, dst in ((0, q), (1, k)) for j in range(4)]
    beside.project(ch, 4, tiles, banks=2, ahead=1)


def head_norm(ch, beside, places, tiles, mask, width, bank, sq, rt, eps_col=0):
    ps = ch.ps
    squares, sums, roots, normed = ch.counters("hn_squares", "hn_sums", "hn_roots", "hn_normed")

    def square(i):
        def part(a, act):
            if i >= 4:
                a.after(sums, i - 3)
            a(act.square(sq[:, i % 4, :], tiles[i][0]), squares)
        return part

    def total(i):
        def part(pe):
            pe.wait_ge(squares.sem, squares.at(i + 1))
            if i >= 2:
                pe.wait_ge(roots.sem, roots.at(i - 1))
            pe.matmul(ps[:, bank + i % 2, :], ch.m(mask), sq[:, i % 4, :], start=True, stop=True).then_inc(sums.sem, 1)
            sums.total += 1
        return part

    def root(i):
        def part(a, act):
            a.after(sums, i + 1)
            if i >= 4:
                a.after(normed, i - 3)
            a(act.activation(rt[:, i % 4, :], ps[:, bank + i % 2, :], ACT.Sqrt, bias=ch.eps[:, eps_col:eps_col + 1],
                             scale=1.0 / width), roots)
        return part

    def scale(i):
        def part(v, dve):
            x, gain = tiles[i]
            v.after(roots, i + 1)
            v(dve.reciprocal(rt[:, i % 4, :], rt[:, i % 4, :]))
            v(dve.scalar_tensor_tensor(x, x, gain, rt[:, i % 4, :], MUL, MUL), normed)
        return part
    beside.add(-1, None, square(0))
    for i, n in enumerate(places[:len(tiles)]):
        beside.add(n, total(i), root(i), scale(i))
        if i + 1 < len(tiles):
            beside.add(n, None, square(i + 1))


class Attention:

    def __init__(self, ch, units, scale, bank, width, room, sinks=False):
        self.ch, self.units, self.scale, self.sinks = ch, units, scale, sinks
        self.width, self.sign = width, 1.0 if sinks else -1.0
        self.turn_bank = bank + 2 * width
        self.value_bank = self.turn_bank + width
        self.bank = bank
        wide = room.rearrange("p k t -> p (k t)")
        self.S = [wide[:, i * 768:(i + 1) * 768] for i in range(3)]
        self.pT = [wide[:, (3 + i) * 768:(4 + i) * 768] for i in range(2)]
        self.st = ch.sm[:, 96:120].rearrange("p (i c) -> p i c", c=6)
        (self.scores, self.softened, self.taken_max, self.expd, self.normed, self.turned, self.copied,
         self.summed, self.taken, self.plain_scaled) = ch.counters(
            "scores", "scores_scaled", "maxima_ready", "exps_done", "probs_normed", "probs_turned",
            "probs_copied", "values_summed", "group_taken", "plain_scaled")
        self.N = len(units)
        self.turns = self.N + 5
        self.group, g = [], 0
        for u in units:
            self.group.append(g)
            g += u["close"] is not None

    def score_banks(self, i):
        b = self.bank + self.width * (i % 2)
        return self.ch.ps[:, b:b + self.width, :].rearrange("p b n -> p (b n)")

    def turn_banks(self):
        return self.ch.ps[:, self.turn_bank:self.turn_bank + self.width, :].rearrange("p b n -> p (b n)")

    def score(self, pe, i):
        if i < self.N:
            u = self.units[i]
            if i >= 2:
                pe.wait_ge(self.softened.sem, self.softened.at(i - 1))
                if self.units[i - 2]["plain"]:
                    pe.wait_ge(self.plain_scaled.sem, self.plain_scaled.at(i - 1))
            for k, c0 in u["keys"]:
                n = k.shape[-1] if len(k.shape) == 2 else k.shape[-1] * k.shape[-2]
                ins = pe.matmul(self.score_banks(i)[:, c0:c0 + n], u["q"], k, start=True, stop=True)
            ins.then_inc(self.scores.sem, 1)
            self.scores.total += 1

    def tensor(self, i):
        def part(pe):
            if i == 0:
                self.score(pe, 0)
            self.score(pe, i + 1)
            if 2 <= i < self.N + 2:
                u = self.units[i - 2]
                pe.wait_ge(self.normed.sem, self.normed.at(i - 1))
                if i >= 3:
                    pe.wait_ge(self.copied.sem, self.copied.at(i - 2))
                for t in range(u["cols"] // P):
                    ins = pe.transpose(self.turn_banks()[:, t * P:(t + 1) * P],
                                       self.S[(i - 2) % 3][:, t * P:(t + 1) * P], self.ch.m("ident"))
                ins.then_inc(self.turned.sem, 1)
                self.turned.total += 1
            if 3 <= i < self.N + 3:
                u, gi = self.units[i - 3], self.group[i - 3]
                pe.wait_ge(self.copied.sem, self.copied.at(i - 2))
                if gi >= 2:
                    pe.wait_ge(self.taken.sem, self.taken.at(gi - 1))
                vs = u["values"]
                for t, val in enumerate(vs):
                    ins = pe.matmul(self.ch.ps[u["rows"], self.value_bank + gi % 2, u["col"]:u["col"] + P], val,
                                    self.pT[(i - 3) % 2][:, t * P:(t + 1) * P], start=t == 0, stop=t == len(vs) - 1)
                ins.then_inc(self.summed.sem, 1)
                self.summed.total += 1
        return part

    def vector(self, i):
        def part(v, dve):
            if i < self.N:
                u, s, stat = self.units[i], self.S[i % 3], self.st[:, i % 4, :]
                v.after(self.scores, i + 1)
                if i >= 3:
                    v.after(self.turned, i - 2)
                if u.get("prepare"):
                    u["prepare"](v, dve)
                both = self.score_banks(i)
                for n, (b, c0, w) in enumerate(u["biases"]):
                    v(dve.scalar_tensor_tensor(s[:, c0:c0 + w], both[:, c0:c0 + w], self.sign * self.scale, b, MUL,
                                               ADD if self.sinks else SUB),
                      self.softened if n + 1 == len(u["biases"]) else None)
                if u["plain"]:
                    v.after(self.plain_scaled, i + 1)
                if self.sinks:
                    v(dve.tensor_reduce(stat[:, 0:1], s[:, 0:u["cols"]], AXX, MAX))
                    v(dve.tensor_scalar(stat[:, 1:2], stat[:, 0:1], u["sink"], -1.0, MAX, MUL), self.taken_max)
                else:
                    v(dve.tensor_reduce(stat[:, 1:2], s[:, 0:u["cols"]], AXX, MIN), self.taken_max)
            if 1 <= i < self.N + 1:
                u, stat = self.units[i - 1], self.st[:, (i - 1) % 4, :]
                v.after(self.expd, i)
                if self.sinks:
                    v(dve.tensor_tensor(stat[:, 2:3], stat[:, 2:3], stat[:, 4:5], ADD))
                v(dve.reciprocal(stat[:, 3:4], stat[:, 2:3]))
                s = self.S[(i - 1) % 3][:, 0:u["cols"]]
                v(dve.tensor_scalar(s, s, stat[:, 3:4], None, MUL), self.normed)
            if i >= 5 and self.units[i - 5]["close"] is not None:
                v.after(self.summed, i - 4)
                self.units[i - 5]["close"](v, dve, self.ch.ps[:, self.value_bank + self.group[i - 5] % 2, :], self.taken)
        return part

    def scale_plain(self, a, act, i):
        if i < self.N and self.units[i]["plain"]:
            a.after(self.scores, i + 1)
            if i >= 3:
                a.after(self.turned, i - 2)
            for c0, w in self.units[i]["plain"]:
                a(act.mul(self.S[i % 3][:, c0:c0 + w], self.score_banks(i)[:, c0:c0 + w],
                          self.sign * self.scale), self.plain_scaled)

    def scalar(self, i):
        def part(a, act):
            if i == 0:
                self.scale_plain(a, act, 0)
            if 2 <= i < self.N + 2:
                u = self.units[i - 2]
                a.after(self.turned, i - 1)
                if i >= 4:
                    a.after(self.summed, i - 3)
                a(act.copy(self.pT[(i - 2) % 2][:, 0:u["cols"]], self.turn_banks()[:, 0:u["cols"]]), self.copied)
            if i < self.N:
                u, s, stat = self.units[i], self.S[i % 3][:, 0:self.units[i]["cols"]], self.st[:, i % 4, :]
                a.after(self.taken_max, i + 1)
                if self.sinks:
                    a(act.activation(stat[:, 4:5], u["sink"], ACT.Exp, bias=stat[:, 1:2]))
                a(act.activation(s, s, ACT.Exp, bias=stat[:, 1:2], scale=self.sign, accum_out=stat[:, 2:3]), self.expd)
            self.scale_plain(a, act, i + 1)
        return part

    def spread(self, beside, places, first=0):
        for n, i in enumerate(range(first, self.turns)):
            beside.add(places[min(n, len(places) - 1)], self.tensor(i), self.scalar(i), self.vector(i))


def halves(n0, n1):
    return [n + h for n in range(n0, n1) for h in (-0.5, 0)]


def dsa_projection(ch):
    gate, iq, ik = ch.slot(3), ch.slot(5), ch.slot(6)
    iw = ch.sm[:, 120:152]
    tiles = [(0, "T", j * P, ch.hT, T, act_to(gate[:, j, :], ACT.Silu)) for j in range(4)]
    tiles += [(1, "T", j * P, ch.hT, T, copy_to(iq[:, j, :])) for j in range(4)]
    tiles += [(2, "T", 0, ch.hT, T, copy_to(ik[:, 0, :]))]
    tiles += [(2, ("N", P, P + 8), s * P, ch.hT, T,
               (lambda a, act, ps, sig, s=s: a(act.mul(iw[:, 8 * s:8 * s + 8], ps, 8 ** -0.5), sig), None))
              for s in range(4)]
    tiles, n = modulated(ch, tiles, 3, bands2(ch, 5, 10))
    beside = Beside()
    head_norm(ch, beside, list(range(8)),
              [(ch.slot(i)[:, j, :], ch.v(g)) for i, g in ((9, "q_gain"), (10, "k_gain")) for j in range(4)],
              "blk64", HD, 6, ch.slot(0), ch.slot(1))
    beside.project(ch, n, tiles, banks=6)


def dsa_scores(ch):
    nc, ps = ch.nc, ch.ps
    iq, ik, score = ch.slot(5), ch.slot(6), ch.slot(8)
    iw = ch.sm[:, 120:152]
    rel = ch.slot(0)
    dots, relus, added = ch.counters("index_dots", "index_relus", "index_added")
    units = [(s, h) for s in range(1, 4) for h in range(8)]
    with nc.Block() as block:
        @block.tensor
        def _(pe):
            for i, (s, h) in enumerate(units):
                if i >= 4:
                    pe.wait_ge(relus.sem, relus.at(i - 3))
                rows, n = slice(64 * (h % 2), 64 * (h % 2) + 64), P * (s + 1)
                pe.matmul(ps[:, i % 4, 0:n], iq[rows, h // 2, s * P:(s + 1) * P], ik[rows, 0, 0:n],
                          start=True, stop=True).then_inc(dots.sem, 1)
                dots.total += 1

        @block.scalar
        def _(act):
            a = Line(act, ch.S["scalar_step"])
            for i, (s, h) in enumerate(units):
                a.after(dots, i + 1)
                if i >= 4:
                    a.after(added, i - 3)
                n = P * (s + 1)
                a(act.activation(rel[:, i % 4, 0:n], ps[:, i % 4, 0:n], ACT.Relu, scale=HD ** -0.5), relus)

        @block.vector
        def _(dve):
            v = Line(dve, ch.S["vector_step"])
            for i, (s, h) in enumerate(units):
                v.after(relus, i + 1)
                n = P * (s + 1)
                w = iw[:, 8 * s + h:8 * s + h + 1]
                if h == 0:
                    v(dve.tensor_scalar(score[:, s, 0:n], rel[:, i % 4, 0:n], w, None, MUL), added)
                else:
                    v(dve.scalar_tensor_tensor(score[:, s, 0:n], rel[:, i % 4, 0:n], w, score[:, s, 0:n], MUL, ADD),
                      added)


def dsa_select(ch):
    score, bias = ch.slot(8), ch.slot(7)
    best = ch.sm[:, 152:160]

    def run(v, dve):
        v(dve.tensor_copy(bias[:, 0, 0:P], ch.m("adm")))
        for s in range(1, 4):
            n = P * (s + 1)
            row = score[:, s, 0:n]
            v(dve.tensor_tensor(row[:, n - P:n], row[:, n - P:n], ch.m("adm"), ADD))
            for _ in range(P // 8):
                v(dve.max(best, row))
                v(dve.match_replace(row, best, row, -3e38))
            v(dve.tensor_scalar(bias[:, s, 0:n], row, -2e38, -BIG, ALU.is_gt, MUL))
    return run


def dsa_attention(ch, tiles):
    q, k, v, gate, bias, out = (ch.slot(9), ch.slot(10), ch.slot(4), ch.slot(3), ch.slot(7), ch.slot(11))
    units = []
    for h in range(8):
        rows, j = slice(64 * (h % 2), 64 * (h % 2) + 64), h // 2
        for s in range(4):
            n = P * (s + 1)

            def close(line, dve, ps, sig, j=j):
                line(dve.tensor_tensor(out[:, j, :], ps, gate[:, j, :], MUL), sig)
            units.append(dict(
                q=q[rows, j, s * P:(s + 1) * P], keys=[(k[rows, j, 0:n], 0)],
                biases=[(bias[:, s, 0:n], 0, n)], plain=[], cols=n,
                values=[v[:, t, h * HD:(h + 1) * HD] for t in range(s + 1)],
                rows=rows, col=s * P, close=close if h % 2 == 1 and s == 3 else None))
    beside = Beside()
    att = Attention(ch, units, HD ** -0.5, bank=3, width=1, room=ch.slot(0, 2))
    att.spread(beside, [-1] * 3 + sorted(halves(0, 8) * 2))
    beside.project(ch, 2, tiles, banks=3)


def block1(ch):
    A = ch.A
    load_constants(ch)
    norm = block1_modulation(ch)
    block1_rwkv_projection(ch, norm)
    rwkv_transpose(ch)
    rwkv_within_chunks(ch)
    rwkv_chain(ch)
    rwkv_output(ch)
    dsa_projection(ch)
    dsa_scores(ch)
    ga = ch.slot(5, 2)
    project(ch, 2, [(b, "T", j * P, ch.hT, T, act_to(ga[:, 4 * b + j, :], ACT.Sigmoid)) for b in range(2)
                    for j in range(4)], vector_after=dsa_select(ch))
    merged, gb, y, yb, tmp = ga, ch.slot(0, 2), ch.slot(2), ch.slot(11), ch.slot(9)
    tiles = []
    for b in range(2):
        for j in range(4):
            def part(v, dve, ps, sig, n=4 * b + j):
                v(dve.tensor_tensor(merged[:, n, :], ps, ga[:, n, :], MUL), sig)
            tiles.append((b, "T", j * P, y, T, (None, part)))
    dsa_attention(ch, tiles)
    tiles = [(b, "T", j * P, ch.hT, T, act_to(gb[:, 4 * b + j, :], ACT.Sigmoid)) for b in range(2) for j in range(4)]
    for b in range(2):
        for j in range(4):
            def part(v, dve, ps, sig, n=4 * b + j):
                v(dve.tensor_tensor(tmp[:, n % 4, :], ps, gb[:, n, :], MUL), sig)
                v(dve.tensor_tensor(merged[:, n, :], merged[:, n, :], tmp[:, n % 4, :], ADD))
            tiles.append((2 + b, "T", j * P, yb, T, (None, part)))
    tiles, n = modulated(ch, tiles, 4, bands2(ch, 10, 12))
    project(ch, n, tiles)
    block2_gains(ch)
    tiles = []
    for b in range(2):
        for j in range(4):
            def part(v, dve, ps, sig, n=4 * b + j):
                v(dve.scalar_tensor_tensor(ch.xT[:, n, :], ps, ch.mod1[:, 16 + n:17 + n], ch.xT[:, n, :], MUL, ADD), sig)
            tiles.append((b, "T", j * P, merged, T, (None, part)))
    ctxT, hcT = (ch.W[:, i, :].rearrange("p (k t) -> p k t", t=L) for i in (2, 11))
    norm = Norm(ch, ch.xT, ch.hT, T, [ch.sm[:, 24 + i:25 + i] for i in range(8)],
                [ch.mod2[:, i, 0:1] for i in range(8)], 7, ch.slot(0), ch.slot(10))
    context = Norm(ch, ctxT, hcT, L, [ch.sm[:, 32 + i:33 + i] for i in range(8)],
                   [ch.mod2[:, i, 1:2] for i in range(8)], 6, ch.slot(3), ch.slot(4), "context_")
    aux = ch.counter("aux_loaded")
    tensor, scalar = beside_stream(norm)

    def load(sp):
        sp.dma_start(ctxT, ch.A["ctxT"].rearrange("(k p) t -> p k t", p=P)).then_inc(aux.sem, 16)
        aux.total += 16

    def context_squares(a, act):
        a.after(aux, 16)
        seq(*[context.square(k) for k in range(8)])(a, act)
    tensor[2] = seq(tensor[2], *[context.sum(k) for k in range(8)])
    scalar[1] = seq(scalar[1], context_squares)
    scalar[2] = seq(scalar[2], context.root, context.add_shift)
    project(ch, 2, tiles, banks=6, extra_sync=load, tensor_beside=tensor, scalar_beside=scalar,
            vector_beside={2: context.scale})
    return norm


def block1_plan(A):
    w, m = A["w_in"], blocks(A["w_mod_2"], 0, 6144)
    return (blocks(A["w_ada"], 0, 3072)
            + weave(blocks(w, 1536, 1664) + blocks(w, 512, 1024) + blocks(w, 0, 512) + blocks(w, 1024, 1536)
                    + blocks(w, 1664, 2176), m[0:5])
            + blocks(w, 3200, 3712) + blocks(w, 2176, 2688) + [None, None] + blocks(w, 2688, 3200)
            + weave(blocks(w, 3712, 4736) + joined(w, [(4736, 4800), (4736, 4800), (4800, 4808)]), m[5:10])
            + blocks(w, 4808, 5832) + blocks(A["w_a_out"], 0, 1024)
            + weave(blocks(w, 5832, 6856) + blocks(A["w_b_out"], 0, 1024), m[10:12])
            + blocks(A["w_o"], 0, 1024))



def block2_gains(ch):
    with ch.nc.Block() as block:
        @block.vector
        def _(dve):
            v = Line(dve, ch.S["vector_step"])
            for o, j, c, g in ((24, 8, 0, "norm_mix_g_2"), (32, 8, 1, "norm_mix_g_2"), (40, 32, 0, "norm_ffn_g_2")):
                v(dve.scalar_tensor_tensor(ch.sm[:, o:o + 8], ch.mod2[:, j:j + 8, c], 1.0, ch.v(g, 0, 8), ADD, MUL))


def conv_taps(ch, vpad, y):
    def run(v, dve):
        for j in range(4):
            for w in range(31):
                src, tap = vpad[:, j, w:w + T], ch.v("conv_w_2", 4 * w + j)
                if w == 0:
                    v(dve.tensor_scalar(y[:, j, :], src, tap, ch.v("conv_b_2", j), MUL, ADD))
                else:
                    v(dve.scalar_tensor_tensor(y[:, j, :], src, tap, y[:, j, :], MUL, ADD))
    return run


def conv_norm(ch, y, sq, room, bank):
    ps = ch.ps
    mean, rstd = room[:, 0, :], room[:, 1, :]
    sums, centred, squares, root, made = ch.counters("cn_sums", "cn_centred", "cn_squares", "cn_root", "cn_made")

    def total(pe):
        for j in range(4):
            ins = pe.matmul(ps[:, bank, :], ch.m("ones"), y[:, j, :], start=j == 0, stop=j == 3)
        ins.then_inc(sums.sem, 1)
        sums.total += 1

    def square_total(pe):
        for j in range(4):
            pe.wait_ge(squares.sem, squares.at(j + 1))
            ins = pe.matmul(ps[:, bank, :], ch.m("ones"), sq[:, j, :], start=j == 0, stop=j == 3)
        ins.then_inc(sums.sem, 1)
        sums.total += 1

    def centre(v, dve):
        v.after(sums, 1)
        v(dve.tensor_scalar(mean, ps[:, bank, :], 1.0 / 512, None, MUL))
        for j in range(4):
            v(dve.tensor_tensor(y[:, j, :], y[:, j, :], mean, SUB), centred)

    def scale(v, dve):
        v.after(root, 1)
        for j in range(4):
            v(dve.tensor_tensor(sq[:, j, :], y[:, j, :], rstd, MUL), centred)

    def square(a, act):
        for j in range(4):
            a.after(centred, j + 1)
            a(act.square(sq[:, j, :], y[:, j, :]), squares)

    def take_root(a, act):
        a.after(sums, 2)
        inverse_root(a, act, rstd, ps[:, bank, :], 1.0 / 512, ch.eps[:, 0:1], root)

    def finish(a, act):
        for j in range(4):
            a.after(centred, 5 + j)
            a(act.activation(y[:, j, :], sq[:, j, :], ACT.Silu, bias=ch.v("conv_ln_b_2", j),
                             scale=ch.v("conv_ln_g_2", j)), made)
    return (total, square_total), (square, take_root, finish), (centre, scale), made


def neighbourhood_attention(ch, y):
    q, k, v, out = ch.slot(0), ch.slot(1, 2), ch.slot(3, 2), ch.slot(8)
    k = k.rearrange("p a t -> p (a t)")[:, 0:3072].rearrange("p (j t) -> p j t", t=768)
    v = v[:, 0:6, :]
    flat = ch.slot(11).rearrange("p a t -> p (a t)")
    tab = [flat[:, i * 896:(i + 1) * 896] for i in range(2)]
    loaded = ch.counter("bias_loaded")

    def load(sp):
        softened = att.softened
        for h in range(8):
            if h >= 2:
                sp.wait_ge(softened.sem, softened.at(4 * (h - 1)))
            sp.dma_start(tab[h % 2], ch.A["rpb"][:, h * 896:(h + 1) * 896]).then_inc(loaded.sem, 16)
            loaded.total += 16
            sp.wait_ge(loaded.sem, loaded.total)

    units = []
    for h in range(8):
        rows, j = slice(64 * (h % 2), 64 * (h % 2) + 64), h // 2

        def prepare(line, dve, h=h):
            line.after(loaded, 16 * (h + 1))
            t = tab[h % 2].rearrange("p (r c) -> p r c", c=64)
            line(dve.tensor_tensor(t, t, ch.m("win")[:, 0:64].unsqueeze(1).to_broadcast([P, 14, 64]), ADD))
        for s in range(4):
            def close(line, dve, ps, sig, j=j):
                line(dve.tensor_copy(out[:, j, :], ps), sig)
            units.append(dict(
                q=q[rows, j, s * P:(s + 1) * P], keys=[(k[rows, j, 0:512], 0), (k[rows, j, 512:768], 512)],
                biases=[(tab[h % 2][:, (6 - 2 * s) * 64:(6 - 2 * s) * 64 + 512], 0, 512)], plain=[(512, 256)],
                cols=768, values=[v[:, t, h * HD:(h + 1) * HD] for t in range(6)],
                rows=rows, col=s * P, close=close if h % 2 == 1 and s == 3 else None,
                prepare=prepare if s == 0 else None))
    att = Attention(ch, units, HD ** -0.5, bank=0, width=2, room=ch.slot(9, 2))
    (total, square_total), (square, take_root, finish), (centre, scale), made = conv_norm(
        ch, y, ch.slot(5), ch.slot(6), 7)

    def conv_made(pe):
        pe.wait_ge(made.sem, made.at(4))
    convolution = {0: (total, None, centre), 1: (None, square, None), 3: (square_total, take_root, scale),
                   5: (None, finish, None), 8: (conv_made, None, None)}
    beside = Beside()
    for i in range(att.turns):
        beside.add(-1, att.tensor(i), att.scalar(i), att.vector(i))
        beside.add(-1, *convolution.get(i, ()))
    beside.project(ch, 0, [], extra_sync=load)


def block2_mixer(ch, norm):
    nc = ch.nc
    hcT = ch.W[:, 11, :].rearrange("p (k t) -> p k t", t=L)
    q, a_, y = ch.slot(0), ch.slot(8), ch.slot(7)
    k = ch.slot(1, 2).rearrange("p a t -> p (a t)")[:, 0:3072].rearrange("p (j t) -> p j t", t=768)
    v = ch.slot(3, 2)
    vpad = ch.slot(5, 2).rearrange("p a t -> p (a t)")[:, 0:4 * 542].rearrange("p (j t) -> p j t", t=542)
    sig_g = ch.slot(9)
    tiles = [(0, "T", j * P, ch.hT, T, copy_to(a_[:, j, :])) for j in range(4)]
    with nc.Block() as block:
        @block.vector
        def _(dve):
            Line(dve, ch.S["vector_step"])(dve.memset(vpad, 0.0))
    for j in range(4):
        def part_a(a, act, ps, sig, j=j):
            a(act.activation(sig_g[:, j, :], ps, ACT.Sigmoid), sig)

        def part_v(v_, dve, ps, sig, j=j):
            v_(dve.tensor_tensor(vpad[:, j, 15:15 + T], a_[:, j, :], sig_g[:, j, :], MUL), sig)
        tiles.append((1, "T", j * P, ch.hT, T, (part_a, part_v)))
    tiles += [(2, "T", j * P, ch.hT, T, copy_to(q[:, j, :])) for j in range(4)]
    tiles += [(3, "T", j * P, ch.hT, T, copy_to(k[:, j, 0:T])) for j in range(4)]
    tiles += [(3, "T", j * P, hcT, L, copy_to(k[:, j, T:T + L])) for j in range(4)]
    tiles += [(4, "N", s * P, ch.hT, T, copy_to(v[:, s, :])) for s in range(4)]
    tiles += [(4, "N", s * P, hcT, L, copy_to(v[:, 4 + s, :])) for s in range(2)]
    project(ch, 5, tiles, vector_after=conv_taps(ch, vpad, y), norm=norm)
    neighbourhood_attention(ch, y)
    tiles = []
    for b in range(2):
        for j in range(4):
            def part(v_, dve, ps, sig, n=4 * b + j):
                v_(dve.scalar_tensor_tensor(ch.xT[:, n, :], ps, ch.mod2[:, 16 + n, 0:1], ch.xT[:, n, :], MUL, ADD), sig)
            tiles.append((b, "T", j * P, ch.slot(7, 2), T, (None, part)))
    norm = Norm(ch, ch.xT, ch.hT, T, [ch.sm[:, 40 + i:41 + i] for i in range(8)],
                [ch.mod2[:, 24 + i, 0:1] for i in range(8)], 7, ch.slot(0), ch.slot(1))
    tensor, scalar = beside_stream(norm)
    project(ch, 2, tiles, banks=7, tensor_beside=tensor, scalar_beside=scalar)
    return norm


def route(ch):
    nc, ps = ch.nc, ch.ps
    wr = ch.slot(2).rearrange("p a t -> p (a t)")[:, 0:128].rearrange("p (k e) -> p k e", e=E_)
    hN = ch.slot(0, 2).rearrange("p a t -> p (a t)").rearrange("p (s d) -> p s d", d=D)
    aff, place = (ch.slot(3)[:, i, 0:64].rearrange("p (s e) -> p s e", e=E_) for i in (0, 1))
    row, sel, pos = (ch.slot(4)[0:E_, i, :] for i in (0, 1, 2))
    best = ch.sm[0:E_, 152:160]
    st = ch.sm[:, 96:104].rearrange("p (i s) -> p i s", s=4)
    aux, turned, copied, steps, expd, aff_turned = ch.counters(
        "aux_loaded", "route_turned", "route_copied", "route_steps", "route_exp", "affinities_turned")
    with nc.Block() as block:
        @block.sync
        def _(sp):
            sp.dma_start(wr, ch.A["w_router_2"].rearrange("(k p) e -> p k e", p=P)).then_inc(aux.sem, 16)
            aux.total += 16
            ch.stream(sp, ch.used + RING + 2)
            sp.wait_ge(turned.sem, turned.at(9))
            ch.stream(sp, ch.used + RING + 3)

        @block.tensor
        def _(pe):
            pe.wait_ge(aux.sem, aux.at(16))
            for s in range(4):
                for k in range(KD):
                    ins = pe.matmul(ps[:, 0, s * E_:(s + 1) * E_], ch.hT[:, k, s * P:(s + 1) * P], wr[:, k, :],
                                    start=k == 0, stop=k == KD - 1)
            ins.then_inc(turned.sem, 1)
            for n in range(8):
                if n == 4:
                    pe.wait_ge(steps.sem, steps.at(1))
                    for s in range(4):
                        ins = pe.transpose(ps[0:E_, 5, s * P:(s + 1) * P], aff[:, s, :], ch.m("ident"))
                    ins.then_inc(aff_turned.sem, 1)
                if n >= 4:
                    pe.wait_ge(copied.sem, copied.at(n - 3))
                for j in range(4):
                    k, s = 4 * (n % 2) + j, n // 2
                    ins = pe.transpose(ps[:, 1 + n % 4, j * P:(j + 1) * P], ch.hT[:, k, s * P:(s + 1) * P], ch.m("ident"))
                ins.then_inc(turned.sem, 1)
            pe.wait_ge(steps.sem, steps.at(2))
            for s in range(4):
                ins = pe.transpose(ps[:, 6, s * E_:(s + 1) * E_], pos[:, s * P:(s + 1) * P], ch.m("ident")[0:E_, 0:E_])
            ins.then_inc(turned.sem, 1)
            turned.total += 10
            aff_turned.total += 1

        @block.scalar
        def _(act):
            a = Line(act, ch.S["scalar_step"])
            a.after(expd, 1)
            a(act.activation(aff, aff, ACT.Exp), expd)
            for n in range(8):
                a.after(turned, n + 2)
                a(act.copy(hN[:, n // 2, (n % 2) * 512:(n % 2 + 1) * 512], ps[:, 1 + n % 4, :]), copied)

        @block.vector
        def _(dve):
            v = Line(dve, ch.S["vector_step"])
            v.after(turned, 1)
            logits = ps[:, 0, 0:64].rearrange("p (s e) -> p s e", e=E_)
            wide = st[:, 0, :].unsqueeze(2).to_broadcast([P, 4, E_])
            v(dve.tensor_reduce(st[:, 0, :], logits, AXX, MAX))
            v(dve.tensor_tensor(aff, logits, wide, SUB), expd)
            v.after(expd, 2)
            v(dve.tensor_reduce(st[:, 0, :], aff, AXX, ADD))
            v(dve.reciprocal(st[:, 0, :], st[:, 0, :]))
            v(dve.tensor_tensor(aff, aff, wide, MUL), steps)
            v.after(aff_turned, 1)
            v(dve.tensor_copy(row, ps[0:E_, 5, :]))
            for _ in range(CAP // 8):
                v(dve.max(best, row))
                v(dve.match_replace(row, best, row, -1.0))
            v(dve.tensor_scalar(sel, row, 0.0, None, ALU.is_lt))
            v(dve.tensor_tensor_scan(pos, ch.eps[0:E_, 3:4].to_broadcast([E_, T]), sel, 0.0, MUL, ADD))
            v(dve.tensor_tensor(pos, pos, sel, MUL), steps)
            v.after(turned, 10)
            v(dve.tensor_copy(place, ps[:, 6, 0:64].rearrange("p (s e) -> p s e", e=E_)))


def experts(ch):
    nc, ps = ch.nc, ch.ps
    hN = ch.slot(0, 2).rearrange("p a t -> p (a t)").rearrange("p (s d) -> p s d", d=D)
    aff, place = (ch.slot(3)[:, i, 0:64].rearrange("p (s e) -> p s e", e=E_) for i in (0, 1))
    oh = ch.slot(4)[:, 0, 0:256].rearrange("p (s c) -> p s c", c=CAP)
    pw = ch.slot(4)[:, 1, :].rearrange("p (s c) -> p s c", c=P)
    pwT = ch.slot(4)[:, 2, :], ch.slot(4)[:, 3, :]
    xs = ch.slot(5)[:, 0, :].rearrange("p (k c) -> p k c", c=CAP)
    sil = ch.slot(6)[:, 0:2, :]
    hid = ch.slot(6)[:, 2:4, :]
    hidT = ch.slot(7)[:, 0:2, :].rearrange("p a (i q c) -> p a i q c", q=2, c=CAP)
    y = ch.slot(7)[:, 2, :]
    iota = ch.m("iota")
    first = ch.used
    norm = Norm(ch, ch.xT, ch.xT, T, [ch.v("norm_final_g_2", i) for i in range(8)], None, 0, ch.slot(0), ch.slot(9))
    (oh_ready, gathered, xs_ready, gate_up, silus, hid_ready, turned, hidT_ready, down, y_ready,
     pw_ready, pw_turned, pwT_ready, scattered, added) = ch.counters(
        "onehot_ready", "gathered", "xs_ready", "gate_up_done", "silus", "hidden_ready", "hidden_turned",
        "hiddenT_ready", "down_done", "y_ready", "scatter_ready", "scatter_turned", "scatterT_ready", "scattered",
        "residual_added")
    for e in range(E_):
        for i in range(8):
            ch.free_at[first + 12 * e + i] = (gate_up.sem, gate_up.at(4 * e + i // 2 + 1))
        for i in range(4):
            ch.free_at[first + 12 * e + 8 + i] = (down.sem, down.at(4 * e + i + 1))

    with nc.Block() as block:
        @block.sync
        def _(sp):
            ch.stream(sp, first + 12 * E_ + RING)

        @block.tensor
        def _(pe):
            def gather(e):
                pe.wait_ge(oh_ready.sem, oh_ready.at(e + 1))
                if e > 0:
                    pe.wait_ge(xs_ready.sem, xs_ready.at(e))
                for k in range(KD):
                    for s in range(4):
                        ins = pe.matmul(ps[:, 0, k * CAP:(k + 1) * CAP], hN[:, s, k * P:(k + 1) * P], oh[:, s, :],
                                        start=s == 0, stop=s == 3)
                ins.then_inc(gathered.sem, 1)
                gathered.total += 1
                pe.wait_ge(pw_ready.sem, pw_ready.at(e + 1))
                if e > 1:
                    pe.wait_ge(added.sem, added.at(8 * (e - 1)))
                elif e == 1:
                    pe.wait_ge(pwT_ready.sem, pwT_ready.at(1))
                for s in range(4):
                    ins = pe.transpose(ps[:, 5, s * P:(s + 1) * P], pw[:, s, :], ch.m("ident"))
                ins.then_inc(pw_turned.sem, 1)
                pw_turned.total += 1

            def gate_and_up(e, n):
                b0 = first + 12 * e + 2 * n
                w = [ch.block_view(b0 + q) for q in range(2)]
                ch.block_wait(pe, b0)
                ch.block_wait(pe, b0 + 1)
                if e > 0:
                    pe.wait_ge(hid_ready.sem, hid_ready.at(2 * e - 1 + n // 2))
                for k in range(KD):
                    for q in range(2):
                        ins = pe.matmul(ps[64 * q:64 * q + 64, 1 + n, :], xs[:, k, :], w[q][:, k, :],
                                        start=k == 0, stop=k == KD - 1)
                ins.then_inc(gate_up.sem, 1)
                gate_up.total += 1

            def scatter(e):
                pe.wait_ge(y_ready.sem, y_ready.at(e + 1))
                for n in range(8):
                    q, bank = n // 4, 5 + n % 2
                    if n < 2:
                        pe.wait_ge(hidT_ready.sem, hidT_ready.at(2 * e + 2))
                    else:
                        pe.wait_ge(added.sem, added.at(8 * e + n - 1))
                    rows = slice(64 * q, 64 * q + 64)
                    pe.matmul(ps[:, bank, :], y[rows, (n % 4) * P:(n % 4 + 1) * P], pwT[e % 2][rows, :], start=True,
                              stop=True).then_inc(scattered.sem, 1)
                    scattered.total += 1

            gather(0)
            for e in range(E_):
                pe.wait_ge(xs_ready.sem, xs_ready.at(e + 1))
                gate_and_up(e, 0)
                gate_and_up(e, 1)
                if e > 0:
                    scatter(e - 1)
                gate_and_up(e, 2)
                gate_and_up(e, 3)
                if e > 0:
                    pe.wait_ge(added.sem, added.at(8 * e))
                pe.wait_ge(hid_ready.sem, hid_ready.at(2 * e + 1))
                for i in range(4):
                    ins = pe.transpose(ps[:, 6, i * P:(i + 1) * P], hid[:, 0, i * P:(i + 1) * P], ch.m("ident"))
                ins.then_inc(turned.sem, 1)
                if e + 1 < E_:
                    gather(e + 1)
                pe.wait_ge(hid_ready.sem, hid_ready.at(2 * e + 2))
                pe.wait_ge(pwT_ready.sem, pwT_ready.at(min(e + 2, E_)))
                for i in range(4):
                    ins = pe.transpose(ps[:, 5, i * P:(i + 1) * P], hid[:, 1, i * P:(i + 1) * P], ch.m("ident"))
                ins.then_inc(turned.sem, 1)
                turned.total += 2
                if e > 0:
                    pe.wait_ge(y_ready.sem, y_ready.at(e))
                for i in range(4):
                    w = ch.block_view(first + 12 * e + 8 + i)
                    ch.block_wait(pe, first + 12 * e + 8 + i)
                    if i % 2 == 0:
                        pe.wait_ge(hidT_ready.sem, hidT_ready.at(2 * e + 1 + i // 2))
                    for t in range(4):
                        f = 4 * i + t
                        for q in range(2):
                            ins = pe.matmul(ps[64 * q:64 * q + 64, 7, :], hidT[:, f // 8, f % 4, (f // 4) % 2, :],
                                            w[:, t, q * 512:(q + 1) * 512], start=f == 0, stop=f == 15)
                    ins.then_inc(down.sem, 1)
                    down.total += 1
            scatter(E_ - 1)
            for k in range(KD):
                norm.sum(k)(pe)

        @block.scalar
        def _(act):
            a = Line(act, ch.S["scalar_step"])

            def gathered_parts(e):
                a.after(gathered, e + 1)
                a(act.copy(xs, ps[:, 0, :].rearrange("p (k c) -> p k c", c=CAP)), xs_ready)
                a.after(pw_turned, e + 1)
                a(act.copy(pwT[e % 2], ps[:, 5, :]), pwT_ready)

            gathered_parts(0)
            for e in range(E_):
                for p in range(2):
                    a.after(gate_up, 4 * e + 2 * p + 1)
                    if e > 0:
                        a.after(hid_ready, 2 * e - 1 + p)
                    a(act.activation(sil[:, p, :], ps[:, 1 + 2 * p, :], ACT.Silu), silus)
                a.after(turned, 2 * e + 1)
                a(act.copy(hidT[:, 0], ps[:, 6, :].rearrange("p (i q c) -> p i q c", q=2, c=CAP)), hidT_ready)
                if e + 1 < E_:
                    gathered_parts(e + 1)
                a.after(turned, 2 * e + 2)
                a(act.copy(hidT[:, 1], ps[:, 5, :].rearrange("p (i q c) -> p i q c", q=2, c=CAP)), hidT_ready)
            for k in range(KD):
                a.after(added, 8 * (E_ - 1) + k + 1)
                norm.square(k)(a, act)

        @block.vector
        def _(dve):
            v = Line(dve, ch.S["vector_step"])

            def selectors(e):
                if e > 0:
                    v.after(pw_turned, e)
                for s in range(4):
                    v(dve.tensor_scalar(oh[:, s, :], iota[:, 0:CAP], place[:, s, e:e + 1], None, ALU.is_equal),
                      oh_ready if s == 3 else None)
                for s in range(4):
                    v(dve.tensor_scalar(pw[:, s, :], iota, place[:, s, e:e + 1], aff[:, s, e:e + 1], ALU.is_equal, MUL),
                      pw_ready if s == 3 else None)

            def hidden(e, p):
                v.after(gate_up, 4 * e + 2 * p + 2)
                v.after(silus, 2 * e + p + 1)
                if e > 0:
                    v.after(turned, 2 * e - 1 + p)
                v(dve.tensor_tensor(hid[:, p, :], sil[:, p, :], ps[:, 2 + 2 * p, :], MUL), hid_ready)

            def add(e):
                for n in range(8):
                    v.after(scattered, 8 * e + n + 1)
                    v(dve.scalar_tensor_tensor(ch.xT[:, n, :], ps[:, 5 + n % 2, :], ch.mod2[:, 40 + n, 0:1],
                                               ch.xT[:, n, :], MUL, ADD), added)

            selectors(0)
            for e in range(E_):
                hidden(e, 0)
                if e > 0:
                    add(e - 1)
                if e + 1 < E_:
                    selectors(e + 1)
                hidden(e, 1)
                v.after(down, 4 * e + 4)
                v(dve.tensor_copy(y, ps[:, 7, :]), y_ready)
            add(E_ - 1)
    ch.used = first + 12 * E_
    return norm


def block2(ch, norm):
    norm = block2_mixer(ch, norm)
    finish_norm(ch, norm)
    route(ch)
    norm = experts(ch)
    following = Norm(ch, ch.xT, ch.hT, T, [ch.v("norm_g_even_3", i) for i in range(8)], None, 1, ch.slot(8),
                     ch.slot(10), "following_")
    finish_norm(ch, norm, following)
    return following


def block2_mixer_plan(A):
    return blocks(A["w_in_2"], 0, 2560) + blocks(A["w_out_2"], 0, D)


def block2_plan(A):
    out = block2_mixer_plan(A)
    for e in range(E_):
        g, u = blocks(A["w_gate_2"][e], 0, FE), blocks(A["w_up_2"][e], 0, FE)
        out += g[0:2] + u[0:2] + g[2:4] + u[2:4]
        for i in range(4):
            w = A["w_down_2"][e, i * 512:(i + 1) * 512, :].rearrange("(k p) c -> p k c", p=P)
            out.append(([(w, 0, D)], 4, D))
    return out



def even_gating(ch, beside, n0):
    ps = ch.ps
    u, z = ch.slot(0, 2), ch.slot(4, 2)
    v = ch.slot(2, 2).rearrange("p a t -> p (a t)").rearrange("p (s d) -> p s d", d=D)
    c = ch.slot(6, 2).rearrange("p a t -> p (a t)")
    gain, shift, bs, ws = c[:, 0:D], c[:, D:2 * D], c[:, 2 * D:2 * D + 512], c[:, 2 * D + 512:3 * D]
    tmp = ch.slot(8)
    stats = ch.sm[:, 0:48].rearrange("p (s i c) -> p s i c", s=4, c=6)
    mv = ch.sm[:, 48:56].rearrange("p (s c) -> p s c", c=2)
    loaded, var_ready, root, normed, mixed, gated = ch.counters(
        "aux_loaded", "var_ready", "ln_root", "ln_normed", "mixed", "gated")

    def load(sp):
        sp.dma_start(c[:, 0:3 * D], ch.A["gmlp"]).then_inc(loaded.sem, 16)
        loaded.total += 16

    def layer_norm(line, dve):
        for s in range(4):
            for i in range(2):
                line(dve.bn_stats(stats[:, s, i, :], v[:, s, i * 512:(i + 1) * 512]))
            line(dve.bn_aggr(mv[:, s, :], stats[:, s].rearrange("p i c -> p (i c)")),
                 var_ready if s == 3 else None)
        line.after(root, 1)
        line(dve.reciprocal(mv[:, :, 1], mv[:, :, 1]))
        line.after(loaded, 16)
        for s in range(4):
            line(dve.tensor_scalar(v[:, s, :], v[:, s, :], mv[:, s, 0:1], mv[:, s, 1:2], SUB, MUL))
            line(dve.tensor_tensor(v[:, s, :], v[:, s, :], gain, MUL))
            line(dve.tensor_tensor(v[:, s, :], v[:, s, :], shift, ADD), normed)

    def deviation(a, act):
        a.after(var_ready, 1)
        a(act.activation(mv[:, :, 1], mv[:, :, 1], ACT.Sqrt, bias=ch.eps[:, 0:1]), root)

    def mix(k):
        def part(pe):
            g = k // 2
            pe.wait_ge(loaded.sem, loaded.at(16))
            pe.wait_ge(normed.sem, normed.at(4))
            if k >= 4:
                pe.wait_ge(gated.sem, gated.at(k - 3))
            for s in range(4):
                ins = pe.matmul(ps[:, 4 + k % 4, s * P:(s + 1) * P], v[:, s, k * P:(k + 1) * P],
                                ws[:, g * P:(g + 1) * P], start=True, stop=True)
            ins.then_inc(mixed.sem, 1)
            mixed.total += 1
        return part

    def gate(k):
        def part(line, dve):
            g = k // 2
            b = bs[:, g * P:(g + 1) * P].unsqueeze(1).to_broadcast([P, 4, P])
            line.after(mixed, k + 1)
            t = tmp[:, k % 4, :]
            line(dve.tensor_tensor(t.rearrange("p (s t) -> p s t", t=P),
                                   ps[:, 4 + k % 4, :].rearrange("p (s t) -> p s t", t=P), b, ADD), gated)
            line(dve.tensor_tensor(t, t, u[:, k, :], MUL))
            line(dve.tensor_tensor(u[:, k, :], t, z[:, k, :], MUL))
        return part

    beside.add(0, None, deviation, layer_norm)
    for k in range(8):
        beside.add(n0 + k, mix(k), None, gate(k))
    return load


def window_attention(ch):
    q, kv, gate = ch.slot(9, 2), ch.slot(11), ch.slot(2, 2)
    k, v = kv[:, 0:2, :], kv[:, 2:4, :].rearrange("p a t -> p (a t)").rearrange("p (s c) -> p s c", c=256)
    band = ch.slot(7).rearrange("p a t -> p (a t)")
    dist, mask = band[:, 0:384], band[:, 384:768]
    bias = [band[:, 768 + i * 384:768 + (i + 1) * 384] for i in range(2)]
    loaded = ch.counter("bias_loaded")

    def load(sp):
        sp.dma_start(band[:, 0:768], ch.A["band"]).then_inc(loaded.sem, 16)
        loaded.total += 16

    units = []
    for h in range(8):
        g = h // 4

        def prepare(line, dve, h=h):
            if h == 0:
                line.after(loaded, 16)
            line(dve.scalar_tensor_tensor(bias[h % 2], dist, -2.0 ** -(h + 1), mask, MUL, ADD))
        for s in range(4):
            t0, t1 = max(s - 1, 0), min(s + 2, 4)
            n, c0 = (t1 - t0) * P, 128 if s == 0 else 0

            def close(line, dve, psum, sig, h=h):
                line.after(by_act, h + 1)
                line(dve.tensor_tensor(gate[:, h, :], psum, gate[:, h, :], MUL), sig)
            units.append(dict(
                q=q[:, h, s * P:(s + 1) * P], keys=[(k[:, g, t0 * P:t1 * P], 0)],
                biases=[(bias[h % 2][:, c0:c0 + n], 0, n)], plain=[], cols=n,
                values=[v[:, t, g * P:(g + 1) * P] for t in range(t0, t1)], rows=slice(0, P), col=s * P,
                close=close if s == 3 else None, prepare=prepare if s == 0 else None, sink=ch.v("attn_sink_3", h)))
    by_act = ch.S["tile_scalar_done"]
    tiles = [(b, "T", j * P, ch.hT, T, act_to(gate[:, 4 * b + j, :], ACT.Silu)) for b in range(2) for j in range(4)]
    tiles += [(2 + t[0],) + t[1:] for t in share_tiles(ch, ch.slot(0, 2), 4, 2)]
    beside = Beside()
    att = Attention(ch, units, P ** -0.5, bank=3, width=1, room=ch.slot(4, 2), sinks=True)
    att.spread(beside, halves(0, 2) + [2, 2.5, 3] + sorted(halves(4, 16) + [4, 6, 8, 10, 12]))
    beside.project(ch, 4, tiles, banks=3, extra_sync=load)


def share_tiles(ch, source, per, nblocks):
    tiles = []
    for b in range(nblocks):
        for j in range(per):
            def part(v, dve, ps, sig, n=per * b + j):
                v(dve.tensor_tensor(ch.xT[:, n, :], ps, ch.xT[:, n, :], ADD), sig)
            tiles.append((b, "T", j * P, source, T, (None, part)))
    return tiles


def add_to_stream(ch, source, per, nblocks, norm):
    tensor, scalar = beside_stream(norm)
    project(ch, nblocks, share_tiles(ch, source, per, nblocks), banks=7, tensor_beside=tensor, scalar_beside=scalar)
    return norm


def even_layer(ch, norm):
    u, z = ch.slot(0, 2), ch.slot(4, 2)
    v = ch.slot(2, 2).rearrange("p a t -> p (a t)").rearrange("p (s d) -> p s d", d=D)
    tiles = []
    for b in range(2):
        tiles += [(b, "T", j * P, ch.hT, T, copy_to(u[:, 4 * b + j, :])) for j in range(4)]
    for b in range(2):
        tiles += [(2 + b, "N", s * P, ch.hT, T, copy_to(v[:, s, b * 512:(b + 1) * 512])) for s in range(4)]
    for b in range(2):
        tiles += [(4 + b, "T", j * P, ch.hT, T, act_to(z[:, 4 * b + j, :], ACT.Silu)) for j in range(4)]
    project(ch, 6, tiles, norm=norm)
    q, kv = ch.slot(9, 2), ch.slot(11)
    vb = kv[:, 2:4, :].rearrange("p a t -> p (a t)").rearrange("p (s c) -> p s c", c=256)
    tiles = []
    for b in range(2):
        tiles += [(b, "T", j * P, ch.hT, T, copy_to(q[:, 4 * b + j, :])) for j in range(4)]
    tiles += [(2, "T", j * P, ch.hT, T, copy_to(kv[:, j, :])) for j in range(2)]
    tiles += [(2, ("N", 256, 512), s * P, ch.hT, T, copy_to(vb[:, s, :])) for s in range(4)]
    beside = Beside()
    load = even_gating(ch, beside, 4)
    beside.project(ch, 3, tiles, banks=4, extra_sync=load)
    window_attention(ch)
    return add_to_stream(ch, ch.slot(2, 2), 4, 2, Norm(
        ch, ch.xT, ch.hT, T, [ch.v("norm_g_odd_3", i) for i in range(8)], None, 7, ch.slot(9), ch.slot(0)))



def odd_bounds(ch):
    with ch.nc.Block() as block:
        @block.vector
        def _(dve):
            v = Line(dve, ch.S["vector_step"])
            for i, n in enumerate(("hgrn_gamma_fwd_3", "hgrn_gamma_bwd_3")):
                v(dve.tensor_tensor(ch.sm[:, 16 * i:16 * i + 16], ch.v(n, 16, 16), ch.v(n, 0, 16), SUB))
    with ch.nc.Block() as block:
        @block.scalar
        def _(act):
            a = Line(act, ch.S["scalar_step"])
            a(act.activation(ch.sm[:, 32:64], ch.sm[:, 0:32], ACT.Sigmoid, scale=-1.0))
            a(act.activation(ch.sm[:, 0:32], ch.sm[:, 0:32], ACT.Sigmoid))


def odd_group(ch, G, norm):
    ps = ch.ps
    F, B, I, Z = [ch.slot(i) for i in (1, 2, 3, 4)]
    qd, kd, ed = (ch.slot(5), ch.slot(8)), (ch.slot(6), ch.slot(9)), (ch.slot(7), ch.slot(10))
    keep = ch.slot(11)[:, 0, :]
    homes = (ch.slot(0), ch.slot(1)), (ch.slot(2), ch.slot(11))
    end = [ch.sm[:, 64 + 32 * d:96 + 32 * d] for d in range(2)]

    def piece(d, i):
        return homes[d][i // 4][:, i % 4, :].rearrange("p (h v) -> p h v", v=P)

    def state(d, c):
        return piece(d, c - 1 if d == 0 else c)
    aT = [piece(0, 7), piece(1, 7)]
    by_dve, by_act = ch.S["tile_vector_done"], ch.S["tile_scalar_done"]
    logged, scanned, decayed, ended = ch.counters("f_logged", "decay_scanned", "decay_exponents", "end_keys_ready")
    turned, natural, kv, stepped, grams, masked, summed, squared, sums, rooted, done = ch.counters(
        "end_keys_turned", "end_keys_natural", "kv_products", "states_stepped", "odd_grams", "odd_masked",
        "odd_summed", "odd_squared", "odd_sums", "odd_rooted", "odd_heads_done")

    tiles = share_tiles(ch, Z, 8, 1) if G else []
    n0 = len(tiles)
    b0 = 1 if G else 0
    tF, tB, tI, tQ, tZ = [n0 + 4 * i for i in range(5)]
    for d, dst in ((0, F), (1, B)):
        for j in range(4):
            lb = ch.sm[:, 16 * d + 4 * G + j:16 * d + 4 * G + j + 1]
            om = ch.sm[:, 32 + 16 * d + 4 * G + j:33 + 16 * d + 4 * G + j]

            def part_a(a, act, ps, sig, o=dst[:, j, :]):
                a(act.activation(o, ps, ACT.Sigmoid), sig)

            def part_v(v, dve, ps, sig, o=dst[:, j, :], k=kd[d][:, j, :], lb=lb, om=om):
                v(dve.tensor_scalar(o, o, om, lb, MUL, ADD))
                v(dve.tensor_scalar(k, o, -1.0, 1.0, MUL, ADD), sig)
            tiles.append((b0 + d, "T", j * P, ch.hT, T, (part_a, part_v)))
    tiles += [(b0 + 2, "N", s * P, ch.hT, T, copy_to(I[:, s, :])) for s in range(4)]
    for j in range(4):
        tmp = aT[j % 2].rearrange("p h v -> p (h v)")

        def q_a(a, act, ps, sig, j=j, tmp=tmp):
            if j >= 2:
                a.after(by_dve, n0 + 7 + j)
            a(act.activation(tmp, ps, ACT.Silu), sig)

        def q_v(v, dve, ps, sig, j=j, tmp=tmp):
            for d in range(2):
                v(dve.tensor_tensor(qd[d][:, j, :], qd[d][:, j, :], tmp, MUL), sig if d else None)
        tiles.append((b0 + 3, "T", j * P, ch.hT, T, (q_a, q_v)))
    tiles += [(b0 + 4, "T", j * P, ch.hT, T, act_to(Z[:, j, :], ACT.Silu)) for j in range(4)]

    def turn(d):
        def part(pe):
            pe.wait_ge(ended.sem, ended.at(d + 1))
            if d:
                pe.wait_ge(natural.sem, natural.at(4))
            for s in range(4):
                for h in range(4):
                    ins = pe.transpose(ps[:, 3 + s, h * P:(h + 1) * P], ed[d][:, h, s * P:(s + 1) * P],
                                       ch.m("ident"))
            ins.then_inc(turned.sem, 1)
            turned.total += 1
        return part

    def products(i):
        def part(pe):
            for d in range(2):
                c = i if d == 0 else 7 - i
                s, rows = c // 2, slice(64 * (c % 2), 64 * (c % 2) + 64)
                if i == 0:
                    pe.wait_ge(natural.sem, natural.at(8))
                else:
                    pe.wait_ge(stepped.sem, stepped.at(2 * i - 1 + d))
                for h in range(4):
                    cols = slice(h * P, (h + 1) * P)
                    ins = pe.matmul(ps[:, 3 + d, cols], ed[d][rows, s, cols], I[rows, s, cols], start=True, stop=True)
                ins.then_inc(kv.sem, 1)
                kv.total += 1
        return part

    def gram(h):
        def part(pe):
            pe.wait_ge(by_dve.sem, by_dve.at(n0 + 9 + h))
            if h >= 1:
                pe.wait_ge(masked.sem, masked.at(h))
            for d in range(2):
                for s in range(4):
                    cols = slice(s * P, (s + 1) * P)
                    ins = pe.matmul(ps[:, 5 + d, cols], kd[d][:, h, cols], qd[d][:, h, cols], start=True, stop=True)
            ins.then_inc(grams.sem, 1)
            grams.total += 1
        return part

    def output(h):
        def part(pe):
            pe.wait_ge(stepped.sem, stepped.at(14))
            pe.wait_ge(masked.sem, masked.at(h + 1))
            if h >= 2:
                pe.wait_ge(done.sem, done.at(h - 1))
            bank = 3 + h % 2
            for s in range(4):
                pe.matmul(ps[:, bank, s * P:(s + 1) * P], I[:, s, h * P:(h + 1) * P], aT[h % 2][:, s, :],
                          start=s == 0, stop=False, skip_group_check=True)
            for c in range(8):
                cols = slice(c * 64, (c + 1) * 64)
                for d in range(2):
                    if (c > 0) if d == 0 else (c < 7):
                        ins = pe.matmul(ps[:, bank, cols], state(d, c)[:, h, :], qd[d][:, h, cols], start=False,
                                        stop=c == 7, skip_group_check=True)
            ins.then_inc(summed.sem, 1)
            summed.total += 1
        return part

    def sum_bank(h):
        return 5 if h == 3 else 7

    def norm_sum(h):
        def part(pe):
            pe.wait_ge(squared.sem, squared.at(h + 1))
            if 1 <= h < 3:
                pe.wait_ge(rooted.sem, rooted.at(h))
            pe.matmul(ps[:, sum_bank(h), :], ch.m("ones"), qd[0][:, h, :], start=True, stop=True).then_inc(sums.sem, 1)
            sums.total += 1
        return part

    def log(d):
        def part(a, act):
            a.after(by_dve, n0 + 4 * d + 4)
            x = (F, B)[d]
            a(act.activation(x, x, ACT.Ln), logged)
        return part

    def exponents(d):
        def part(a, act):
            a.after(scanned, d + 1)
            x = (F, B)[d]
            a(act.activation(qd[d], x, ACT.Exp))
            a(act.activation(ed[d], x, ACT.Exp, scale=-1.0), decayed)
        return part

    def to_natural(d):
        def part(a, act):
            a.after(turned, d + 1)
            for s in range(4):
                a(act.copy(ed[d][:, s, :], ps[:, 3 + s, :]), natural)
        return part

    def square(h):
        def part(a, act):
            a.after(summed, h + 1)
            a(act.square(qd[0][:, h, :], ps[:, 3 + h % 2, :]), squared)
        return part

    def root(h):
        def part(a, act):
            a.after(sums, h + 1)
            inverse_root(a, act, qd[1][:, h, :], ps[:, sum_bank(h), :], 1.0 / P, ch.eps[:, 0:1], rooted)
        return part

    def last_roots(a, act):
        a.after(sums, 4)
        for h in (2, 3):
            a(act.activation(qd[1][:, h, :], ps[:, sum_bank(h), :], ACT.Ln, bias=ch.eps[:, 0:1], scale=1.0 / P))
        for h in (2, 3):
            a(act.activation(qd[1][:, h, :], qd[1][:, h, :], ACT.Exp, scale=-0.5), rooted)

    def scan(d):
        def part(v, dve):
            if d == 0:
                v(dve.memset(keep, 1.0))
                v(dve.memset(keep.rearrange("p (c t) -> p c t", t=64)[:, :, 0:1], 0.0))
            v.after(logged, d + 1)
            for j in range(4):
                x = F[:, j, :] if d == 0 else B[:, j, ::-1]
                v(dve.tensor_tensor_scan(x, keep, x, 0.0, MUL, ADD), scanned if j == 3 else None)
        return part

    def end_keys(d):
        def part(v, dve):
            v.after(decayed, d + 1)
            v(dve.tensor_copy(end[d].rearrange("p (j c) -> p j c", c=8),
                              qd[d].rearrange("p j (c t) -> p j c t", t=64)[:, :, :, 0 if d else 63]))
            v(dve.tensor_tensor(kd[d], kd[d], ed[d], MUL))
            v(dve.tensor_tensor(ed[d].rearrange("p j (c t) -> p (j c) t", t=64),
                                kd[d].rearrange("p j (c t) -> p (j c) t", t=64),
                                end[d].unsqueeze(2).to_broadcast([P, 32, 64]), MUL), ended)
        return part

    def step(i):
        def part(v, dve):
            for d in range(2):
                c = i if d == 0 else 7 - i
                new = state(d, c + 1 if d == 0 else c - 1)
                got = ps[:, 3 + d, :].rearrange("p (h v) -> p h v", v=P)
                e = end[d].rearrange("p (j c) -> p j c", c=8)[:, :, c:c + 1]
                if i == 0:
                    v.after(kv, 2 * i + d + 1)
                    v(dve.tensor_copy(new, got), stepped)
                else:
                    v(dve.tensor_tensor(new, state(d, c), e.to_broadcast([P, 4, P]), MUL))
                    v.after(kv, 2 * i + d + 1)
                    v(dve.tensor_tensor(new, new, got, ADD), stepped)
        return part

    def mask(h):
        def part(v, dve):
            v.after(grams, h + 1)
            if h >= 2:
                v.after(summed, h - 1)
            b = [ps[:, 5 + d, :].rearrange("p (s t) -> p s t", t=P) for d in range(2)]
            v(dve.tensor_tensor(b[1], b[1], ch.m4("mLI"), MUL))
            v(dve.tensor_tensor(aT[h % 2], b[0], ch.m4("mUI"), MUL))
            v(dve.tensor_tensor(aT[h % 2], aT[h % 2], b[1], ADD), masked)
        return part

    def finish(h):
        def part(v, dve):
            t = qd[1][:, h, :]
            v.after(rooted, h + 1)
            v(dve.tensor_tensor(t, ps[:, 3 + h % 2, :], t, MUL), done)
            v.after(by_act, 17 + h)
            v(dve.scalar_tensor_tensor(Z[:, h, :], t, ch.v("hgrn_head_norm_g_3", 4 * G + h), Z[:, h, :], MUL, MUL))
        return part

    project(
        ch, b0 + 5, tiles, banks=3, norm=norm,
        tensor_beside={
            tI + 1: turn(0), tI + 3: turn(1), tQ: products(0), tQ + 0.5: products(1), tQ + 1: products(2),
            tQ + 1.5: products(3), tQ + 2: products(4), tQ + 2.5: products(5), tQ + 3: seq(products(6), gram(0)),
            tZ - 0.5: gram(1), tZ: output(0), tZ + 0.5: seq(gram(2), output(1)), tZ + 1: seq(norm_sum(0), gram(3)),
            tZ + 1.5: seq(norm_sum(1), output(2)), tZ + 2: output(3), tZ + 2.5: seq(norm_sum(2), norm_sum(3))},
        scalar_beside={
            tB: log(0), tB + 2: exponents(0), tI: log(1), tI + 1: seq(exponents(1), to_natural(0)),
            tI + 3: to_natural(1), tZ: seq(square(0), square(1)), tZ + 1: seq(root(0), root(1), square(2)),
            tZ + 2: seq(square(3), last_roots)},
        vector_beside={
            tB + 1: scan(0), tB + 3: seq(end_keys(0), scan(1), end_keys(1)),
            tQ: seq(step(0), step(1)), tQ + 1: seq(step(2), step(3)), tQ + 2: seq(step(4), step(5)),
            tQ + 3: seq(step(6), *[mask(0), mask(1), mask(2), finish(0), mask(3), finish(1), finish(2), finish(3)])})


def odd_layer(ch, norm):
    odd_bounds(ch)
    for G in range(4):
        odd_group(ch, G, norm if G == 0 else None)
    return add_to_stream(ch, ch.slot(4), 8, 1, Norm(
        ch, ch.xT, ch.xT, T, [ch.v("final_norm_g_3", i) for i in range(8)], None, 7, ch.slot(0), ch.slot(1)))


def block3(ch, norm):
    norm = even_layer(ch, norm)
    return odd_layer(ch, norm)


def block3_plan(A):
    out = (blocks(A["w_in_even_3"], 0, 5632) + blocks(A["w_out_even_3"][0:D, :], 0, D)
           + blocks(A["w_out_even_3"][D:2 * D, :], 0, D))
    w, o = A["w_in_odd_3"], A["w_out_odd_3"]
    for G in range(4):
        for i in (1, 2, 3, 0, 4):
            out += blocks(w, i * 2048 + G * 512, i * 2048 + (G + 1) * 512)
        out.append(([(o[G * 512:(G + 1) * 512, :].rearrange("(k p) c -> p k c", p=P), 0, D)], 4, D))
    return out


def program(nc, A, out):
    ctx = ExitStack()
    with ctx:
        ch = Chip(nc, ctx, A, plan(A))
        norm = block1(ch)
        norm = block2(ch, norm)
        norm = block3(ch, norm)
        write_out(ch, norm, out)


def plan(A):
    return block1_plan(A) + block2_plan(A) + block3_plan(A)


def write_out(ch, norm, out):
    done = ch.counter("output_written")
    rows = out.rearrange("(k p) t -> p k t", p=P)
    with ch.nc.Block() as block:
        @block.scalar
        def _(act):
            norm.root(Line(act, ch.S["scalar_step"]), act)

        @block.vector
        def _(dve):
            norm.scale(Line(dve, ch.S["vector_step"]), dve)

        @block.sync
        def _(sp):
            for k in range(0, KD, 2):
                norm.wait(sp, k + 1)
                sp.dma_start(rows[:, k:k + 2, :], ch.xT[:, k:k + 2, :]).then_inc(done.sem, 16)
            sp.wait_ge(done.sem, 16 * (KD // 2))


WEIGHTS = ["w_ada", "w_in", "w_up", "a_up", "w_a_out", "w_b_out", "w_o"]
WEIGHTS_2 = ["w_mod", "w_in", "w_out", "w_router", "w_gate", "w_up", "w_down"]
WEIGHTS_3 = ["w_in_even", "w_out_even", "w_in_odd", "w_out_odd"]


def laid_out(inputs):
    cols = []
    for name, w in VECTORS:
        a = np.asarray(inputs[name])
        if name in ("q_gain", "k_gain"):
            a = np.concatenate([a[0], a[0]])
        if name == "attn_sink_3":
            cols.append(np.ascontiguousarray(np.broadcast_to(a.reshape(1, 8), (P, 8))))
            continue
        cols.append(a.reshape(-1, P).T)
    arrays = {"vectors": np.ascontiguousarray(np.concatenate(cols, 1)), "masks": mask_arrays()}
    arrays["xT"] = np.ascontiguousarray(np.asarray(inputs["x"])[0].T)
    arrays["ctxT"] = np.ascontiguousarray(np.asarray(inputs["ctx_2"])[0].T)
    for name in WEIGHTS:
        arrays[name] = np.asarray(inputs[name])[0]
    for name in WEIGHTS_2:
        arrays[name + "_2"] = np.asarray(inputs[name + "_2"])[0]
    rpb = np.asarray(inputs["rpb_2"])[0]
    c, kc = np.arange(64)[:, None], np.arange(64)[None, :]
    dc = np.clip(kc - c + 15, 0, 30)
    lower, upper = rpb[:, 1:15][:, :, dc], rpb[:, 0:14][:, :, dc]
    arrays["rpb"] = np.ascontiguousarray(
        np.concatenate([lower, upper], 2).transpose(2, 0, 1, 3).reshape(P, 8 * 14 * 64))
    for name in WEIGHTS_3:
        arrays[name + "_3"] = np.asarray(inputs[name + "_3"])[0]
    rows = [np.broadcast_to(np.asarray(inputs[n]).reshape(1, -1), (P, np.asarray(inputs[n]).size))
            for n in ("gmlp_ln_g_3", "gmlp_ln_b_3", "gmlp_b_s_3")]
    mixers = np.asarray(inputs["gmlp_w_s_3"])[0].transpose(2, 0, 1).reshape(P, 512)
    arrays["gmlp"] = np.ascontiguousarray(np.concatenate(rows + [mixers], 1))
    dist = np.abs(np.arange(384)[None, :] - 128 - np.arange(P)[:, None]).astype(np.float32)
    arrays["band"] = np.concatenate([dist, np.where(dist > 128, np.float32(-BIG), np.float32(0))], 1)
    return arrays


def kernel(**inputs):
    import concourse.bacc as bacc
    from concourse.bass_utils import run_bass_kernel_spmd

    nc = bacc.Bacc("TRN2", target_bir_lowering=False, num_devices=1)
    arrays = laid_out(inputs)
    A = {n: nc.dram_tensor("in_" + n, a.shape, F32, kind="ExternalInput").ap() for n, a in arrays.items()}
    out = nc.dram_tensor("out", (D, T), F32, kind="ExternalOutput").ap()
    program(nc, A, out)
    r = run_bass_kernel_spmd(nc, [{"in_" + n: a for n, a in arrays.items()}], core_ids=[0])
    return np.ascontiguousarray(r.results[0]["out"].T).reshape(1, T, D)
```
